# Optimizing a Trainium2 kernel written in Bass

```python
import math
import jax
import jax.numpy as jnp
from jax import lax
import numpy as np

D_MODEL = 2048
BATCH = 1
SEQ = 256
DEPTH = 2
DEC_BATCH = 8
DEC_SEQ = 8
PAST_LEN = 2048
PAGE_SIZE = 128

HEAD_DIM = 128
QBLK = 128
A_GROUPS = ((128, 1), (512, 4), (2048, 16))
A_NG = 3
A_HPG = 8
A_QKV = A_NG * A_HPG * HEAD_DIM
A_WIDTH = A_HPG * HEAD_DIM
B_WIDTH = 1024
CONV_W = 31
EVEN_MIX = A_WIDTH + B_WIDTH
EVEN_IN = 3 * A_QKV + A_WIDTH + 3 * B_WIDTH
C_HEADS = 16
C_KV_HEADS = 2
C_HPG = C_HEADS // C_KV_HEADS
C_WIDTH = C_HEADS * HEAD_DIM
C_KV = C_KV_HEADS * HEAD_DIM
CMP_BLK = 32
CMP_STRIDE = 16
CMP_HID = 128
SEL_BLK = 64
SEL_N = 16
WIN = 512
ODD_IN = 2 * C_WIDTH + 6 * C_KV + 3 * C_HEADS
NUM_BUCKETS = 32
MAX_DIST = 2048
BIAS_HEADS = A_NG * A_HPG
EPS = 1e-6
N_EVEN = (DEPTH + 1) // 2
N_ODD = DEPTH // 2

kernel_name = "hybrid_dilated_conv_nsa_decoder_step"

def rms_norm(x, g):
    x32 = x.astype(jnp.float32)
    y = x32 * lax.rsqrt(jnp.mean(x32 * x32, axis=-1, keepdims=True) + EPS)
    return (y * g.astype(jnp.float32)).astype(x.dtype)

def t5_bucket(dist):
    max_exact = NUM_BUCKETS // 2
    d = jnp.maximum(dist, 0)
    ratio = jnp.log(jnp.maximum(d, 1).astype(jnp.float32) / max_exact) / math.log(MAX_DIST / max_exact)
    large = jnp.minimum(max_exact + (ratio * (NUM_BUCKETS - max_exact)).astype(jnp.int32), NUM_BUCKETS - 1)
    return jnp.where(d < max_exact, d, large)

def masked_softmax(s, valid, axes):
    s = jnp.where(valid, s, -jnp.inf)
    m = jnp.max(s, axis=axes, keepdims=True)
    m = jnp.where(jnp.isfinite(m), m, 0.0)
    e = jnp.where(valid, jnp.exp(s - m), 0.0)
    den = jnp.sum(e, axis=axes, keepdims=True)
    return e / jnp.where(den > 0.0, den, 1.0)

def split_cols(z, widths):
    out, off = [], 0
    for w in widths:
        out.append(z[..., off:off + w])
        off += w
    return out

def over_query_blocks(fn, q):
    b, t = q.shape[:2]
    qb = QBLK if t % QBLK == 0 else t
    nb = t // qb
    q_blocks = jnp.swapaxes(q.reshape((b, nb, qb) + q.shape[2:]), 0, 1)
    starts = jnp.arange(nb, dtype=jnp.int32) * qb
    out = lax.map(lambda args: fn(args[0], args[1]), (q_blocks, starts))
    out = jnp.swapaxes(out, 0, 1)
    return out.reshape((b, t) + out.shape[3:])

def dilated_attention(q, kv_full, hist_lens, rel_bias):
    scale = HEAD_DIM ** -0.5
    dt = q.dtype

    def block(qb, start):
        tq = qb.shape[1]
        lses, outs = [], []
        for g, (win, dil) in enumerate(A_GROUPS):
            steps = jnp.arange(win // dil + 1, dtype=jnp.int32) * dil
            qidx = hist_lens[g] + start + jnp.arange(tq, dtype=jnp.int32)
            kidx = qidx[:, None] - steps[None, :]
            valid = (kidx >= 0)[None, :, None, :]
            kv = kv_full[g][:, jnp.maximum(kidx, 0)]
            bias = rel_bias[t5_bucket(steps), g * A_HPG:(g + 1) * A_HPG]
            s = jnp.einsum('bqhd,bqjhd->bqhj', qb[:, :, g], kv[:, :, :, 0]).astype(jnp.float32) * scale
            s = jnp.where(valid, s + bias.T.astype(jnp.float32), -jnp.inf)
            m = jnp.max(s, axis=-1, keepdims=True)
            e = jnp.exp(s - m)
            den = jnp.sum(e, axis=-1, keepdims=True)
            outs.append(jnp.einsum('bqhj,bqjhd->bqhd', (e / den).astype(dt), kv[:, :, :, 1]))
            lses.append((m + jnp.log(den))[..., 0])
        w = jax.nn.softmax(jnp.stack(lses, axis=-1), axis=-1)
        return jnp.einsum('bqhg,gbqhd->bqhd', w.astype(dt), jnp.stack(outs))

    return over_query_blocks(block, q)

def conv_module(glu_in, hist, conv_w, conv_b, ln_g, ln_b, pw_w, pw_b):
    a, gt = glu_in[..., :B_WIDTH], glu_in[..., B_WIDTH:]
    u = a * jax.nn.sigmoid(gt)
    full = jnp.concatenate([hist.astype(u.dtype), u], axis=1)
    y = lax.conv_general_dilated(full, conv_w[:, None, :].astype(u.dtype), (1,), 'VALID',
                                 dimension_numbers=('NWC', 'WIO', 'NWC'),
                                 feature_group_count=B_WIDTH) + conv_b
    y32 = y.astype(jnp.float32)
    mu = jnp.mean(y32, axis=-1, keepdims=True)
    var = jnp.mean(jnp.square(y32 - mu), axis=-1, keepdims=True)
    y = (y32 - mu) * lax.rsqrt(var + EPS) * ln_g.astype(jnp.float32) + ln_b.astype(jnp.float32)
    y = jax.nn.silu(y).astype(u.dtype)
    return y @ pw_w + pw_b, full[:, full.shape[1] - (CONV_W - 1):]

def compress(x, pos, w1, b1, w2):
    b, l = x.shape[:2]
    n_ch = l // CMP_STRIDE
    ch = x[:, :n_ch * CMP_STRIDE].reshape(b, n_ch, CMP_STRIDE, C_KV_HEADS, HEAD_DIM)
    blocks = jnp.concatenate([ch[:, :-1], ch[:, 1:]], axis=2) + pos[None, None, :, None, :]
    h = jax.nn.silu(jnp.einsum('bnlgd,lde->bnge', blocks, w1) + b1)
    return jnp.einsum('bnge,ed->bngd', h, w2)

def nsa_attention(q, cs_full, win_full, win_hist_len, rel_bias, cmp_pos, cmp_w1, cmp_b1, cmp_w2):
    b, t = q.shape[:2]
    l = cs_full.shape[1]
    q_pos0 = l - t
    dt = q.dtype
    scale = HEAD_DIM ** -0.5
    k_cmp = compress(cs_full[:, :, 0], cmp_pos[0], cmp_w1[0], cmp_b1[0], cmp_w2[0])
    v_cmp = compress(cs_full[:, :, 1], cmp_pos[1], cmp_w1[1], cmp_b1[1], cmp_w2[1])
    n_cmp = k_cmp.shape[1]
    cmp_end = jnp.arange(n_cmp, dtype=jnp.int32) * CMP_STRIDE + (CMP_BLK - 1)
    n_sel = -(-l // SEL_BLK)
    sel = jnp.pad(cs_full[:, :, 2:4], ((0, 0), (0, n_sel * SEL_BLK - l), (0, 0), (0, 0), (0, 0)))
    sel = sel.reshape(b, n_sel, SEL_BLK, 2, C_KV_HEADS, HEAD_DIM).transpose(0, 4, 1, 2, 3, 5)
    ci = np.arange(n_cmp)[:, None]
    si = np.arange(n_sel)[None, :]
    overlap = jnp.asarray(((ci * CMP_STRIDE < (si + 1) * SEL_BLK) &
                           (ci * CMP_STRIDE + CMP_BLK > si * SEL_BLK)).astype(np.float32))
    n_top = min(SEL_N, n_sel)
    tab = rel_bias[:, :C_HEADS].reshape(NUM_BUCKETS, C_KV_HEADS, C_HPG).astype(jnp.float32)
    tab_g = tab.transpose(1, 0, 2)
    win_keys = jnp.pad(win_full, ((0, 0), (WIN, 0), (0, 0), (0, 0), (0, 0)))
    bidx = jnp.arange(b)[:, None, None, None]
    gidx = jnp.arange(C_KV_HEADS)[None, :, None, None]

    def block(qb, start):
        tq = qb.shape[1]
        qpos = q_pos0 + start + jnp.arange(tq, dtype=jnp.int32)
        s_c = jnp.einsum('bqghd,bngd->bqghn', qb, k_cmp).astype(jnp.float32) * scale
        ok_c = (cmp_end[None, :] <= qpos[:, None])[None, :, None, None, :]
        p_c = masked_softmax(s_c, ok_c, (-1,))
        o_c = jnp.einsum('bqghn,bngd->bqghd', p_c.astype(dt), v_cmp)
        imp = jnp.einsum('bqghn,ns->bqgs', p_c, overlap)
        blk = jnp.arange(n_sel, dtype=jnp.int32)[None, :]
        qblk = (qpos // SEL_BLK)[:, None]
        forced = (blk == 0) | (blk == qblk) | (blk == qblk - 1)
        score = jnp.where(forced[None, :, None, :], jnp.inf, imp)
        score = jnp.where((blk <= qblk)[None, :, None, :], score, -jnp.inf)
        top_v, top_i = lax.top_k(score, n_top)
        top_i = top_i.transpose(0, 2, 1, 3)
        top_ok = (top_v > -jnp.inf).transpose(0, 2, 1, 3)
        kv_s = sel[bidx, gidx, top_i]
        kpos = top_i[..., None] * SEL_BLK + jnp.arange(SEL_BLK, dtype=jnp.int32)
        dist = qpos[None, None, :, None, None] - kpos
        ok_s = (top_ok[..., None] & (dist >= 0))[:, :, :, None]
        bias_s = jnp.moveaxis(tab_g[gidx[..., None], t5_bucket(dist)], -1, 3)
        s_s = jnp.einsum('bqghd,bgqkld->bgqhkl', qb, kv_s[..., 0, :]).astype(jnp.float32) * scale + bias_s
        p_s = masked_softmax(s_s, ok_s, (-2, -1))
        o_s = jnp.einsum('bgqhkl,bgqkld->bqghd', p_s.astype(dt), kv_s[..., 1, :])
        kv_w = lax.dynamic_slice_in_dim(win_keys, win_hist_len + start, WIN + tq, axis=1)
        kwpos = q_pos0 + start - WIN + jnp.arange(WIN + tq, dtype=jnp.int32)
        dist_w = qpos[:, None] - kwpos[None, :]
        ok_w = ((dist_w >= 0) & (dist_w <= WIN) & (kwpos[None, :] >= 0))[None, :, None, None, :]
        bias_w = tab[t5_bucket(dist_w)].transpose(0, 2, 3, 1)
        s_w = jnp.einsum('bqghd,bkgd->bqghk', qb, kv_w[:, :, 0]).astype(jnp.float32) * scale + bias_w[None]
        p_w = masked_softmax(s_w, ok_w, (-1,))
        o_w = jnp.einsum('bqghk,bkgd->bqghd', p_w.astype(dt), kv_w[:, :, 1])
        return jnp.stack([o_c, o_s, o_w], axis=2)

    return over_query_blocks(block, q)

def even_layer(x, a_hists, conv_hist, p_len, rel_bias, norm_g, w_in, conv_w, conv_b, ln_g, ln_b, pw_w, pw_b, w_out):
    b, t = x.shape[:2]
    z = rms_norm(x, norm_g) @ w_in
    q, k, v, ga, glu, gb = split_cols(z, (A_QKV, A_QKV, A_QKV, A_WIDTH, 2 * B_WIDTH, B_WIDTH))
    shp = (b, t, A_NG, A_HPG, HEAD_DIM)
    q, k, v = q.reshape(shp), k.reshape(shp), v.reshape(shp)
    kv_full, new_hists = [], []
    for g, (win, _) in enumerate(A_GROUPS):
        full = jnp.concatenate([a_hists[g].astype(k.dtype), jnp.stack([k[:, :, g], v[:, :, g]], axis=2)], axis=1)
        kv_full.append(full)
        keep = min(win, p_len + t)
        new_hists.append(full[:, full.shape[1] - keep:])
    o_a = dilated_attention(q, kv_full, [h.shape[1] for h in a_hists], rel_bias).reshape(b, t, A_WIDTH)
    o_b, new_conv = conv_module(glu, conv_hist, conv_w, conv_b, ln_g, ln_b, pw_w, pw_b)
    mix = jnp.concatenate([o_a * jax.nn.silu(ga), o_b * jax.nn.silu(gb)], axis=-1)
    return x + mix @ w_out, new_hists, new_conv

def odd_layer(x, c_past, win_hist, rel_bias, norm_g, w_in, cmp_pos, cmp_w1, cmp_b1, cmp_w2, w_out):
    b, t = x.shape[:2]
    p_len = c_past.shape[1]
    z = rms_norm(x, norm_g) @ w_in
    q, kc, vc, ks, vs, kw, vw, gl, gp = split_cols(z, (C_WIDTH, C_KV, C_KV, C_KV, C_KV, C_KV, C_KV, 3 * C_HEADS, C_WIDTH))
    kvh = lambda a: a.reshape(b, t, C_KV_HEADS, HEAD_DIM)
    rows = jnp.stack([kvh(kc), kvh(vc), kvh(ks), kvh(vs)], axis=2)
    cs_full = jnp.concatenate([c_past.astype(rows.dtype), rows], axis=1)
    win_full = jnp.concatenate([win_hist.astype(rows.dtype), jnp.stack([kvh(kw), kvh(vw)], axis=2)], axis=1)
    o = nsa_attention(q.reshape(b, t, C_KV_HEADS, C_HPG, HEAD_DIM), cs_full, win_full, win_hist.shape[1],
                      rel_bias, cmp_pos, cmp_w1, cmp_b1, cmp_w2)
    gates = jax.nn.sigmoid(gl.astype(jnp.float32)).reshape(b, t, 3, C_KV_HEADS, C_HPG, 1).astype(o.dtype)
    o = jnp.sum(gates * o, axis=2).reshape(b, t, C_WIDTH)
    keep = min(WIN, p_len + t)
    return x + (o * jax.nn.silu(gp)) @ w_out, rows, win_full[:, win_full.shape[1] - keep:]

def run_trunk(x, p_len, a_hists, conv_hist, get_c_past, c_win, rel_bias, norm_even, w_in_even, conv_w, conv_b,
              conv_ln_g, conv_ln_b, conv_pw_w, conv_pw_b, w_out_even, norm_odd, w_in_odd, cmp_pos, cmp_w1,
              cmp_b1, cmp_w2, w_out_odd, final_norm):
    new_a = [[] for _ in A_GROUPS]
    new_conv, new_rows, new_win = [], [], []
    for layer in range(DEPTH):
        i = layer // 2
        if layer % 2 == 0:
            x, hists, conv = even_layer(x, [h[i] for h in a_hists], conv_hist[i], p_len, rel_bias, norm_even[i],
                                        w_in_even[i], conv_w[i], conv_b[i], conv_ln_g[i], conv_ln_b[i],
                                        conv_pw_w[i], conv_pw_b[i], w_out_even[i])
            for g in range(A_NG):
                new_a[g].append(hists[g])
            new_conv.append(conv)
        else:
            x, rows, win = odd_layer(x, get_c_past(i), c_win[i], rel_bias, norm_odd[i], w_in_odd[i],
                                     cmp_pos[i], cmp_w1[i], cmp_b1[i], cmp_w2[i], w_out_odd[i])
            new_rows.append(rows)
            new_win.append(win)
    y = rms_norm(x, final_norm)
    return y, [jnp.stack(a) for a in new_a], jnp.stack(new_conv), jnp.stack(new_rows), jnp.stack(new_win)

def setup_inputs(seed: int = 0) -> dict:
    key = jax.random.key(seed)
    k = jax.random.split(key, 27)
    nrm = lambda kk, shape, scale: jax.random.normal(kk, shape, jnp.float32) * scale
    n_pages = PAST_LEN // PAGE_SIZE
    n_pool = (5 * DEC_BATCH * n_pages + 3) // 4
    a_caches = [nrm(k[2 + g], (N_EVEN, DEC_BATCH, min(w, PAST_LEN), 2, A_HPG, HEAD_DIM), 1.0)
                for g, (w, _) in enumerate(A_GROUPS)]
    page_table = jax.random.permutation(k[8], n_pool)[:DEC_BATCH * n_pages].reshape(DEC_BATCH, n_pages).astype(jnp.int32)
    return {
        'x_prompt': nrm(k[0], (BATCH, SEQ, D_MODEL), 1.0),
        'x_sample': nrm(k[1], (DEC_BATCH, DEC_SEQ, D_MODEL), 1.0),
        'cache_a_kv0': a_caches[0],
        'cache_a_kv1': a_caches[1],
        'cache_a_kv2': a_caches[2],
        'state_b_conv': nrm(k[5], (N_EVEN, DEC_BATCH, CONV_W - 1, B_WIDTH), 0.5),
        'cache_c_kv': nrm(k[6], (N_ODD, n_pool, PAGE_SIZE, 4, C_KV_HEADS, HEAD_DIM), 1.0),
        'cache_c_win': nrm(k[7], (N_ODD, DEC_BATCH, min(WIN, PAST_LEN), 2, C_KV_HEADS, HEAD_DIM), 1.0),
        'page_table': page_table,
        'rel_bias': nrm(k[9], (NUM_BUCKETS, BIAS_HEADS), 0.5),
        'norm_even': 1.0 + nrm(k[10], (N_EVEN, D_MODEL), 0.02),
        'w_in_even': nrm(k[11], (N_EVEN, D_MODEL, EVEN_IN), D_MODEL ** -0.5),
        'conv_w': nrm(k[12], (N_EVEN, CONV_W, B_WIDTH), CONV_W ** -0.5),
        'conv_b': nrm(k[13], (N_EVEN, B_WIDTH), 0.02),
        'conv_ln_g': 1.0 + nrm(k[14], (N_EVEN, B_WIDTH), 0.02),
        'conv_ln_b': nrm(k[15], (N_EVEN, B_WIDTH), 0.02),
        'conv_pw_w': nrm(k[16], (N_EVEN, B_WIDTH, B_WIDTH), B_WIDTH ** -0.5),
        'conv_pw_b': nrm(k[17], (N_EVEN, B_WIDTH), 0.02),
        'w_out_even': nrm(k[18], (N_EVEN, EVEN_MIX, D_MODEL), EVEN_MIX ** -0.5),
        'norm_odd': 1.0 + nrm(k[19], (N_ODD, D_MODEL), 0.02),
        'w_in_odd': nrm(k[20], (N_ODD, D_MODEL, ODD_IN), D_MODEL ** -0.5),
        'cmp_pos': nrm(k[21], (N_ODD, 2, CMP_BLK, HEAD_DIM), 0.1),
        'cmp_w1': nrm(k[22], (N_ODD, 2, CMP_BLK, HEAD_DIM, CMP_HID), (CMP_BLK * HEAD_DIM) ** -0.5),
        'cmp_b1': nrm(k[23], (N_ODD, 2, CMP_HID), 0.02),
        'cmp_w2': nrm(k[24], (N_ODD, 2, CMP_HID, HEAD_DIM), CMP_HID ** -0.5),
        'w_out_odd': nrm(k[25], (N_ODD, C_WIDTH, D_MODEL), C_WIDTH ** -0.5),
        'final_norm': 1.0 + nrm(k[26], (D_MODEL,), 0.02),
    }

def reference(x_prompt, x_sample, cache_a_kv0, cache_a_kv1, cache_a_kv2, state_b_conv, cache_c_kv, cache_c_win,
              page_table, rel_bias, norm_even, w_in_even, conv_w, conv_b, conv_ln_g, conv_ln_b, conv_pw_w,
              conv_pw_b, w_out_even, norm_odd, w_in_odd, cmp_pos, cmp_w1, cmp_b1, cmp_w2, w_out_odd, final_norm):
    weights = (rel_bias, norm_even, w_in_even, conv_w, conv_b, conv_ln_g, conv_ln_b, conv_pw_w, conv_pw_b,
               w_out_even, norm_odd, w_in_odd, cmp_pos, cmp_w1, cmp_b1, cmp_w2, w_out_odd, final_norm)
    b = x_prompt.shape[0]
    db = x_sample.shape[0]
    dt = x_prompt.dtype
    empty_a = [jnp.zeros((N_EVEN, b, 0, 2, A_HPG, HEAD_DIM), dt) for _ in A_GROUPS]
    zero_conv = jnp.zeros((N_EVEN, b, CONV_W - 1, B_WIDTH), dt)
    empty_c = jnp.zeros((b, 0, 4, C_KV_HEADS, HEAD_DIM), dt)
    empty_win = jnp.zeros((N_ODD, b, 0, 2, C_KV_HEADS, HEAD_DIM), dt)
    y_p, a_p, conv_p, rows_p, win_p = run_trunk(x_prompt, 0, empty_a, zero_conv, lambda i: empty_c, empty_win,
                                                *weights)
    n_pages = page_table.shape[1]
    past = n_pages * cache_c_kv.shape[2]

    def paged_past(i):
        return cache_c_kv[i][page_table].reshape(db, past, 4, C_KV_HEADS, HEAD_DIM)

    y_s, a_s, conv_s, rows_s, win_s = run_trunk(x_sample, past, [cache_a_kv0, cache_a_kv1, cache_a_kv2],
                                                state_b_conv, paged_past, cache_c_win, *weights)
    return (y_p, y_s, a_p[0], a_p[1], a_p[2], conv_p, rows_p, win_p, a_s[0], a_s[1], a_s[2], conv_s, rows_s, win_s)


_drawn_inputs = setup_inputs


def setup_inputs(seed=0):
    import zlib

    import numpy as np

    out = dict(_drawn_inputs(seed))
    spreads = {}
    factors = {'conv_b': 4.971,
     'conv_ln_g': 8.0,
     'conv_ln_b': 8.0,
     'conv_pw_b': 6.762,
     'norm_odd': 2.901,
     'cmp_pos': 3.738,
     'cmp_b1': 8.0,
     'final_norm': 2.895}
    for name, (base, spread) in spreads.items():
        noise = np.random.default_rng([zlib.crc32(name.encode()), seed]).standard_normal(out[name].shape)
        drawn = base * np.exp(spread * noise) if base else spread * noise
        out[name] = jnp.asarray(drawn.astype(out[name].dtype))
    for name, factor in factors.items():
        out[name] = (out[name] * factor).astype(out[name].dtype)
    return out
```

```python
import math
from contextlib import ExitStack

import numpy as np

import concourse.bass as bass
from concourse import mybir

F32 = mybir.dt.float32
I32 = mybir.dt.int32
ALU = mybir.AluOpType
ACT = mybir.ActivationFunctionType
AX = mybir.AxisListType.X

P = 128
D = 2048
NP = 256
NB, NQ = 8, 8
NS = NB * NQ
T = NP + NS
PAST = 2048
PAGE = 128
NPG = PAST // PAGE
HD = 128
SCALE = HD ** -0.5
EPS = 1e-6
MASK = -1.0e30
GROUPS = ((128, 1), (512, 4), (2048, 16))
NG, NH = 3, 8
QKV = NG * NH * HD
WB = 1024
TAPS = 31
EVEN_IN = 3 * QKV + NH * HD + 3 * WB
CH, CG = 16, 2
CHG = CH // CG
CW = CH * HD
CKV = CG * HD
CB, CS = 32, 16
NCS = PAST // CS - 1
NCP = NP // CS - 1
SELB = 64
NSEL = -(-(PAST + NQ) // SELB)
WIN = 512
NBUCK, MAXD = 32, 2048
KT = D // P
GW = 512
Z_GA, Z_A, Z_GT, Z_GB = 3 * QKV, 3 * QKV + 1024, 3 * QKV + 2048, 3 * QKV + 3072
C_KC, C_VC, C_KS, C_VS, C_KW, C_VW = (CW + i * CKV for i in range(6))
C_GL = CW + 6 * CKV
C_GP = C_GL + 3 * CH
ODD_IN = C_GP + CW
Z2_GP = C_GL
FW = 384
SA = NG * P + NG * NQ
HC = PAST + NQ + NQ - 1
HWC = WIN + NQ + NQ - 1


def host_constants():
    def onehot(dist, ok):
        d = np.maximum(dist, 0)
        ratio = np.log(np.maximum(d, 1).astype(np.float32) / np.float32(NBUCK // 2)) / np.float32(math.log(MAXD / (NBUCK // 2)))
        large = np.minimum(NBUCK // 2 + (ratio * np.float32(NBUCK // 2)).astype(np.int32), NBUCK - 1)
        b = np.where(d < NBUCK // 2, d, large)
        out = np.zeros((NBUCK + 1, dist.size), np.float32)
        n = np.arange(dist.size)
        out[b[ok], n[ok]] = 1.0
        out[NBUCK, ~ok] = MASK
        return out

    c = np.arange(FW)
    dist = 255 - c
    parts = [onehot(dist, (dist >= 0) & (dist <= w) & (dist % dil == 0)) for w, dil in GROUPS]
    parts.append(onehot(dist, dist >= 0))
    for i in range(NQ):
        j = np.arange(P)
        m = np.arange(NQ)
        for w, dil in GROUPS:
            dd = w + i - (dil * j + i % dil)
            parts.append(onehot(dd, (dd >= 0) & (dd <= w)))
        for w, dil in GROUPS:
            dd = i - m
            parts.append(onehot(dd, (dd >= 0) & (dd % dil == 0)))
    c = np.arange(HC)
    parts.append(onehot(PAST + NQ - 1 - c, PAST + NQ - 1 - c >= 0))
    c = np.arange(HWC)
    dd = WIN + NQ - 1 - c
    parts.append(onehot(dd, (dd >= 0) & (dd <= WIN)))
    ci, si = np.arange(NCS)[:, None], np.arange(NSEL)[None, :]
    overlap = ((ci * CS < (si + 1) * SELB) & (ci * CS + CB > si * SELB)).astype(np.float32)
    r = np.arange(P)
    hsum = (r[:, None] // CHG == r[None, :] // CHG).astype(np.float32)
    q = np.arange(NP).reshape(2, P)
    n = np.arange(NCP)
    cmask = np.where(n[None, None] * CS + CB - 1 <= q.T[:, :, None], 0.0, MASK).astype(np.float32)
    return {
        "c_ident": np.eye(P, dtype=np.float32),
        "c_onehot": np.concatenate(parts, axis=1),
        "c_overlap": overlap,
        "c_hsum": hsum,
        "c_cmask": np.ascontiguousarray(cmask),
    }


def ap_of(view, offset, dims):
    return bass.AP(tensor=view.tensor, offset=view.offset + offset, ap=[list(view.ap[0])] + [list(d) for d in dims])


def dram_ap(view, offset, dims):
    return bass.AP(tensor=view.tensor, offset=view.offset + offset, ap=[list(d) for d in dims])


class Chain:

    def __init__(self, eng, sem, base=0):
        self.eng, self.sem, self.base, self.n = eng, sem, base, 0

    def __call__(self, ins):
        self.n += 1
        ins.then_inc(self.sem, 1)
        self.eng.wait_ge(self.sem, self.base + self.n)


def wait(eng, sem, value):
    if not isinstance(value, int) or value > 0:
        eng.wait_ge(sem, value)


def settle(eng, k):
    eng.sem_inc(k.settled, 1)


class Norm:

    def __init__(self, k, tag, xT, xn, gcol, ps):
        self.k, self.xT, self.xn, self.gcol, self.ps = k, xT, xn, gcol, ps
        self.sq = k.sb("sq" + tag, [P, 4, T])
        self.rs = k.sb("rs" + tag, [P, T])
        self.sq_ready, self.sq_used, self.sum_done, self.root_done, self.chain, self.ready = (
            k.sem(n + tag) for n in ("sq_ready", "sq_used", "sum_done", "root_done", "norm_chain", "xn_ready"))

    def dve(self, dve, x_wait):
        k = self.k
        for t in range(KT):
            x_wait(dve, t)
            if t >= 4:
                dve.wait_ge(self.sq_used, t - 3)
            dve.tensor_tensor(self.sq[:, t % 4, :], self.xT[:, t, :], self.xT[:, t, :], ALU.mult).then_inc(self.sq_ready, 1)
        dve.wait_ge(self.root_done, 1)
        link = Chain(dve, self.chain)
        link(dve.reciprocal(self.rs[:, :], self.rs[:, :]))
        for t in range(KT):
            dve.scalar_tensor_tensor(self.xn[:, t, :], self.xT[:, t, :], self.gcol[:, t:t + 1], self.rs[:, :],
                                     ALU.mult, ALU.mult).then_inc(self.ready, 1)

    def pe(self, pe):
        for t in range(KT):
            pe.wait_ge(self.sq_ready, t + 1)
            pe.matmul(self.ps[:, 0:T], self.k.ones[:, :], self.sq[:, t % 4, :], start=(t == 0), stop=(t == KT - 1)
                      ).then_inc(self.sq_used, 1)

    def act(self, act):
        act.wait_ge(self.sq_used, KT)
        act.activation(self.rs[:, :], self.ps[:, 0:T], ACT.Sqrt, bias=self.k.eps[:, :], scale=1.0 / D).then_inc(self.root_done, 1)


class Proj:

    def __init__(self, k, tag, w, n_k, rhs, banks, segs, zt=None, rows=None, row_banks=None, residual=None):
        self.k, self.rhs, self.banks, self.segs, self.zt = k, rhs, banks, segs, zt
        self.w = w.rearrange("(k p) n -> p k n", p=P)
        self.nq, self.kq = 4, n_k // 4
        self.rows, self.row_banks, self.residual = rows, row_banks, residual
        self.wt = k.sb("w" + tag, [P, self.nq, self.kq, GW])
        self.loaded = [k.sem(f"w_loaded{q}" + tag) for q in range(self.nq)]
        self.freed = [k.sem(f"w_freed{q}" + tag) for q in range(self.nq - 1)]
        self.tile_done, self.z_ready, self.z_stored = (k.sem(n + tag) for n in ("tile_done", "z_ready", "z_stored"))
        if residual is None:
            self.z = k.sb("z" + tag, [P, 4, T])
        if rows is not None:
            self.rsb = k.sb("rows" + tag, [P, 3, GW])
            self.rows_done, self.rows_evac, self.rows_stored = (k.sem(n + tag) for n in ("rows_done", "rows_evac", "rows_stored"))

    def segments(self):
        g = r = 0
        for n, src, dst, rc in self.segs:
            yield n, src, dst, rc, g, r
            g += n
            r += n * (rc is not None)

    def sync(self, sp):
        for n, src, dst, rc, g0, r0 in self.segments():
            with sp.Fori(0, n) as it:
                for q in range(self.nq):
                    if q < self.nq - 1:
                        sp.wait_ge(self.freed[q], it + (g0 + 1))
                    else:
                        sp.wait_ge(self.tile_done, it * 4 + (4 * g0 + 4))
                    sp.dma_start(self.wt[:, q, :, :], self.w[:, q * self.kq:(q + 1) * self.kq, bass.ds(it * GW + src, GW)]
                                 ).then_inc(self.loaded[q], 16)

    def pe(self, pe, rhs_wait):
        for q in range(self.nq - 1):
            pe.sem_inc(self.freed[q], 1)
        pe.sem_inc(self.tile_done, 4)
        rhs_wait(pe)
        for n, src, dst, rc, g0, r0 in self.segments():
            with pe.Fori(0, n) as it:
                for q in range(self.nq):
                    pe.wait_ge(self.loaded[q], it * 16 + (16 * g0 + 16))
                    for c in range(4):
                        if q == 0:
                            pe.wait_ge(self.z_ready, it * 4 + (4 * g0 + c + 1))
                        for j in range(self.kq):
                            ins = pe.matmul(self.banks[c][:, 0:T], self.wt[:, q, j, c * P:(c + 1) * P],
                                            self.rhs[:, q * self.kq + j, :], start=(q == 0 and j == 0),
                                            stop=(q == self.nq - 1 and j == self.kq - 1))
                        if q == self.nq - 1:
                            ins.then_inc(self.tile_done, 1)
                        elif c == 3:
                            ins.then_inc(self.freed[q], 1)
                if rc is not None:
                    pe.wait_ge(self.z_ready, it * 4 + (4 * g0 + 8))
                    pe.wait_ge(self.rows_evac, it * 3 + (3 * r0 + 3))
                    for t, m in enumerate((P, P, NS)):
                        for c in range(4):
                            ins = pe.transpose(self.row_banks[t][0:m, c * P:(c + 1) * P], self.z[:, c, t * P:t * P + m],
                                               self.k.ident[:, :])
                        ins.then_inc(self.rows_done, 1)

    def act(self, act):
        act.sem_inc(self.z_ready, 4)
        act.sem_inc(self.z_stored, 16)
        if self.rows is not None:
            act.sem_inc(self.rows_done, 3)
        for n, src, dst, rc, g0, r0 in self.segments():
            r_end = r0 + n * (rc is not None)
            with act.Fori(0, n) as it:
                act.wait_ge(self.z_stored, it * 16 + (16 * g0 + 16))
                if rc is not None:
                    act.wait_ge(self.rows_done, it * 3 + (3 * r0 + 3))
                elif r0:
                    act.wait_ge(self.rows_done, 3 * r0 + 3)
                for c in range(4):
                    act.wait_ge(self.tile_done, it * 4 + (4 * g0 + 4 + c + 1))
                    act.copy(self.z[:, c, :], self.banks[c][:, 0:T]).then_inc(self.z_ready, 1)
                act.wait_ge(self.z_ready, it * 4 + (4 * g0 + 8))
                act.dma_start(self.zt[bass.ds(it * GW + dst, GW), :].rearrange("(c p) t -> p c t", p=P), self.z[:, :, :]
                              ).then_inc(self.z_stored, 16)
                if rc is not None:
                    act.wait_ge(self.rows_evac, it * 3 + (3 * r0 + 6))
                    act.dma_start(self.rows[0:NP, bass.ds(it * GW + rc, GW)].rearrange("(t p) n -> p t n", p=P), self.rsb[:, 0:2, :]
                                  ).then_inc(self.rows_stored, 16)
                    act.dma_start(self.rows[NP:T, bass.ds(it * GW + rc, GW)], self.rsb[0:NS, 2, :]).then_inc(self.rows_stored, 16)

    def dve_rows(self, dve):
        dve.sem_inc(self.rows_evac, 3)
        dve.sem_inc(self.rows_stored, 32)
        for n, src, dst, rc, g0, r0 in self.segments():
            if rc is None:
                continue
            with dve.Fori(0, n) as it:
                dve.wait_ge(self.rows_stored, it * 32 + (32 * r0 + 32))
                for t, m in enumerate((P, P, NS)):
                    dve.wait_ge(self.rows_done, it * 3 + (3 * r0 + 3 + t + 1))
                    dve.tensor_copy(self.rsb[0:m, t, :], self.row_banks[t][0:m, :]).then_inc(self.rows_evac, 1)

    def dve_residual(self, dve):
        dve.sem_inc(self.z_ready, 4)
        for n, src, dst, rc, g0, r0 in self.segments():
            with dve.Fori(0, n) as it:
                for c in range(4):
                    dve.wait_ge(self.tile_done, it * 4 + (4 * g0 + 4 + c + 1))
                    x = self.residual[:, bass.ds(it * 4 + (4 * g0 + c), 1), :]
                    dve.tensor_tensor(x, x, self.banks[c][:, 0:T].unsqueeze(1), ALU.add).then_inc(self.z_ready, 1)


def table_jobs(k):
    jobs, c = [], 0
    for g in range(NG):
        jobs.append(([(slice(g * NH, (g + 1) * NH), c, 0, FW)], NH, FW, k.tab_a[g]))
        c += FW
    jobs.append(([(slice(0, CH), c, 0, FW)], CH, FW, k.tab_c))
    c += FW
    for i in range(NQ):
        parts = []
        for g in range(NG):
            parts.append((slice(g * NH, (g + 1) * NH), c, g * P, P))
            c += P
        for g in range(NG):
            parts.append((slice(g * NH, (g + 1) * NH), c, NG * P + g * NQ, NQ))
            c += NQ
        jobs.append((parts, NH, SA, k.tab_sa[i]))
    for dst, width in ((k.tab_hc, HC), (k.tab_hw, HWC)):
        for o in range(0, width, 512):
            n = min(512, width - o)
            jobs.append(([(slice(0, CH), c + o, 0, n)], CH, n, dst[:, o:o + n]))
        c += width
    return jobs, c


def block_even_in(nc, k):
    with k.scope():
        xrow = k.sb("xrow", [P, 3, D])
        xT = k.sb("xT1", [P, KT, T])
        xn = k.sb("xn1", [P, KT, T])
        gcol = k.sb("gcol1", [P, KT])
        jobs, ncols = table_jobs(k)
        onehot = k.sb("onehot", [NBUCK + 1, ncols])
        relb = k.sb("relb", [NBUCK + 1, NG * NH])
        tab = k.sb("tab", [CH, 2, 512])
        banks = [k.ps(f"zb{i}", [P, 512]) for i in range(4)]
        rbanks = [k.ps(f"rb{i}", [P, 512]) for i in range(3)]
        nbank = k.ps("nb", [P, 512])
        x_loaded, g_loaded, tab_loaded, xt_stored = (k.sem(n) for n in ("x_loaded", "g1_loaded", "tab_loaded", "xt_stored"))
        consts_loaded, consts_set = k.sem("consts_loaded"), k.sem("consts_set")
        k.consts_set = consts_set
        turned, xT_ready = k.sem("x_turned"), k.sem("xT_ready")
        tab_done, tab_evac = k.sem("tab_done"), k.sem("tab_evac")
        tab_stored = [k.sem(f"tab_stored{i}") for i in range(2)]
        copied = k.sem("copied")
        norm = Norm(k, "1", xT, xn, gcol, nbank)
        proj = Proj(k, "1", k.w_in_even, KT, xn, banks,
                    [(6, Z_A, Z_A, None), (2, Z_GA, Z_GA, None), (6, 0, 0, None), (12, QKV, QKV, 0)],
                    zt=k.zt, rows=k.kv, row_banks=rbanks)
        with nc.Block() as block:
            @block.sync
            def _(sp):
                sp.dma_start(k.ident[:, :], k.c_ident).then_inc(consts_loaded, 16)
                sp.dma_start(xrow[:, 0:2, :], k.x_prompt.rearrange("(t p) n -> p t n", p=P)).then_inc(x_loaded, 16)
                sp.dma_start(xrow[0:NS, 2, :], k.x_sample).then_inc(x_loaded, 16)
                sp.dma_start(gcol[:, :], k.norm_even).then_inc(g_loaded, 16)
                sp.dma_start(onehot[:, :], k.c_onehot).then_inc(tab_loaded, 16)
                sp.dma_start(relb[0:NBUCK, :], k.rel_bias).then_inc(tab_loaded, 16)
                proj.sync(sp)
                sp.wait_ge(xT_ready, KT)
                sp.dma_start(k.xt.rearrange("(k p) t -> p k t", p=P), xT[:, :, :]).then_inc(xt_stored, 16)
                sp.wait_ge(xt_stored, 16)
                sp.wait_ge(proj.z_stored, 16 * 27)

            @block.gpsimd
            def _(pool):
                link = Chain(pool, consts_set)
                link(pool.memset(k.ones[:, :], 1.0))
                link(pool.memset(k.eps[:, :], EPS))
                link(pool.memset(relb[NBUCK:NBUCK + 1, :], 1.0))
                n = 0
                for g, (w, dil) in enumerate(GROUPS):
                    for b in range(NB):
                        keep = (w - NQ) * 2 * NH * HD
                        src = k.cache_a[g][b].rearrange("t a h d -> (t a h d)")[NQ * 2 * NH * HD:]
                        dst = k.out_a_s[g][b].rearrange("t a h d -> (t a h d)")[0:keep]
                        m = keep // 8192 if keep % 8192 == 0 else keep // 2048
                        pool.dma_start(dst.rearrange("(m n) -> m n", m=m), src.rearrange("(m n) -> m n", m=m)).then_inc(copied, 16)
                        n += 1
                pool.wait_ge(copied, 16 * n)
                pool.wait_ge(proj.rows_stored, 32 * 13)

            @block.scalar
            def _(act):
                for n, (parts, m, width, dst) in enumerate(jobs):
                    act.wait_ge(tab_done, n + 1)
                    if n >= 2:
                        act.wait_ge(tab_stored[n % 2], 16 * (n // 2))
                    act.copy(tab[0:m, n % 2, 0:width], rbanks[n % 2][0:m, 0:width]).then_inc(tab_evac, 1)
                    act.wait_ge(tab_evac, n + 1)
                    act.dma_start(dst, tab[0:m, n % 2, 0:width]).then_inc(tab_stored[n % 2], 16)
                norm.act(act)
                proj.act(act)
                for i in range(2):
                    act.wait_ge(tab_stored[i], 16 * len(jobs[i::2]))

            @block.tensor
            def _(pe):
                pe.wait_ge(tab_loaded, 32)
                pe.wait_ge(consts_set, 3)
                for n, (parts, m, width, dst) in enumerate(jobs):
                    if n >= 2:
                        pe.wait_ge(tab_evac, n - 1)
                    for heads, c, o, w in parts:
                        ins = pe.matmul(rbanks[n % 2][0:m, o:o + w], relb[:, heads], onehot[:, c:c + w], start=True, stop=True)
                    ins.then_inc(tab_done, 1)
                pe.wait_ge(consts_loaded, 16)
                pe.wait_ge(x_loaded, 32)
                for t in range(KT):
                    if t >= 4:
                        pe.wait_ge(xT_ready, t - 3)
                    for j, m in enumerate((P, P, NS)):
                        ins = pe.transpose(banks[t % 4][:, j * P:j * P + m], xrow[0:m, j, t * P:(t + 1) * P], k.ident[0:m, 0:m])
                    ins.then_inc(turned, 1)
                norm.pe(pe)
                pe.wait_ge(tab_evac, len(jobs))
                proj.pe(pe, lambda e: e.wait_ge(norm.ready, KT))

            @block.vector
            def _(dve):
                for t in range(KT):
                    dve.wait_ge(turned, t + 1)
                    dve.tensor_copy(xT[:, t, :], banks[t % 4][:, 0:T]).then_inc(xT_ready, 1)
                dve.wait_ge(g_loaded, 16)
                norm.dve(dve, lambda e, t: e.wait_ge(xT_ready, t + 1))
                proj.dve_rows(dve)


NR = NQ * NH
ZN = [0, NH * NR, 2 * NH * NR]
Z1 = 3 * NH * NR
Z2 = Z1 + 4 * NH * NR
ZQ = Z2 + NQ * NH * NR
TILES = [(0, 0)] + [(1, r) for r in range(4)] + [(2, i) for i in range(NQ)]


def z_block(g, r, h):
    o = (ZN[0], Z1, Z2)[g] + (r * NH + h) * NR
    return slice(o, o + NR)


def block_sample_a(nc, k):
    with k.scope():
        kt = [k.sb("ka0", [P, 1, NH * HD]), k.sb("ka1", [P, 4, NH * HD]), k.sb("ka2", [P, NQ, NH * HD])]
        vt = [k.sb("va0", [P, 1, NH * HD]), k.sb("va1", [P, 4, NH * HD]), k.sb("va2", [P, NQ, NH * HD])]
        vnew = k.sb("vnew", [NG * NQ, NH * HD])
        qs = k.sb("qsa", [P, NG * NH, NS])
        kn = k.sb("kna", [P, NG * NH, NS])
        qz = k.sb("qz", [P, ZQ])
        pz = k.sb("pz", [P, ZQ - 2 * NH * NR])
        pzn = k.sb("pzn", [NG * NQ, NH, NR])
        bias = k.sb("bias_sa", [NR, SA])
        s = k.sb("s_sa", [NR, SA])
        stat = k.sb("stat_sa", [NR, 4])
        ktt = k.sb("ktt", [P, 2, 4 * P])
        orow = k.sb("orow", [NR, HD])
        ot = k.sb("ot_sa", [P, NH, NS])
        kps = [k.ps(f"kps{i}", [P, 512]) for i in range(2)]
        sps, pps, ops, tps = (k.ps(n, [P, 512]) for n in ("sps", "pps", "ops", "tps"))
        pieces = [(0, 0, 1), (1, 0, 4), (2, 0, 4), (2, 4, 8)]
        k_in = [k.sem(f"ka_in{i}") for i in range(4)]
        v_in = [k.sem(f"va_in{i}") for i in range(4)]
        vn_in, q_in, b_in, zeroed = k.sem("vn_in"), k.sem("qa_in"), k.sem("ba_in"), k.sem("za_set")
        qz_ready, turned, evac_a, evac_d = k.sem("qz_ready"), k.sem("ka_turned"), k.sem("ka_evac_a"), k.sem("ka_evac_d")
        scored, score_tiles = k.sem("sa_done"), k.sem("sa_tiles")
        chain, max_done, exp_done, p_ready = k.sem("sa_chain"), k.sem("sa_max"), k.sem("sa_exp"), k.sem("sa_p")
        p_turned, pz_ready, pv_done, o_evac, o_turned, o_ready, o_stored = (
            k.sem(n) for n in ("pa_turned", "pza_ready", "pva_done", "oa_evac", "oa_turned", "oa_ready", "oa_stored"))
        pv_tiles = k.sem("pva_tiles")
        scaled, toe_stored = k.sem("qa_scaled"), k.sem("toe_stored")
        NQUAD = 2 * len(TILES)

        def tile_src(g, lo, hi, b, kv):
            w, dil = GROUPS[g]
            v = k.cache_a[g].rearrange("b (j r) a h d -> b j r a (h d)", r=dil)
            return v[bass.ds(b, 1), :, lo:hi, kv, :].rearrange("b j r n -> (b j) r n")

        with nc.Block() as block:
            @block.sync
            def _(sp):
                for i in range(NG):
                    sp.dma_start(qs[:, i * NH:(i + 1) * NH, :], k.zt[i * 1024:(i + 1) * 1024, NP:T].rearrange("(h d) t -> d h t", d=HD)).then_inc(q_in, 16)
                    sp.dma_start(kn[:, i * NH:(i + 1) * NH, :], k.zt[QKV + i * 1024:QKV + (i + 1) * 1024, NP:T].rearrange("(h d) t -> d h t", d=HD)).then_inc(q_in, 16)
                sp.dma_start(bias[:, :], k.tab_sa.rearrange("i h n -> (i h) n")).then_inc(b_in, 16)

                def load_k(b, first=False):
                    for n, (g, lo, hi) in enumerate(pieces):
                        if not first:
                            sp.wait_ge(turned, b * NQUAD - NQUAD + 2 * sum(t[2] - t[1] for t in pieces[:n + 1]))
                        sp.dma_start(kt[g][:, lo:hi, :], tile_src(g, lo, hi, b, 0)).then_inc(k_in[n], 16)

                def load_v(b, first=False):
                    for n, (g, lo, hi) in enumerate(pieces):
                        if not first:
                            sp.wait_ge(pv_tiles, b * 4 - 4 + (n + 1))
                        sp.dma_start(vt[g][:, lo:hi, :], tile_src(g, lo, hi, b, 1)).then_inc(v_in[n], 16)
                    if not first:
                        sp.wait_ge(pv_done, b * 1)
                    for g in range(NG):
                        c = QKV + g * NH * HD
                        sp.dma_start(vnew[g * NQ:(g + 1) * NQ, :], k.kv[bass.ds(b * NQ + NP, NQ), c:c + NH * HD]).then_inc(vn_in, 16)

                load_k(0, True)
                load_v(0, True)
                with sp.Fori(1, NB) as b:
                    load_k(b)
                    load_v(b)
                sp.wait_ge(o_ready, NB)
                sp.dma_start(k.mt[0:NH * HD, NP:T].rearrange("(h d) t -> d h t", d=HD), ot[:, :, :]).then_inc(o_stored, 16)
                sp.wait_ge(o_stored, 16)

            @block.gpsimd
            def _(pool):
                pool.dma_start(k.toe_a.rearrange("g h p n -> (g h) p n"), dram_ap(k.tab_a, P - 1, [(FW, NG * NH), (-1, P), (1, NP)])).then_inc(toe_stored, 16)
                pool.dma_start(k.toe_c, dram_ap(k.tab_c, P - 1, [(FW, CH), (-1, P), (1, NP)])).then_inc(toe_stored, 16)
                link = Chain(pool, zeroed)
                link(pool.memset(qz[:, :], 0.0))
                link(pool.memset(pz[:, :], 0.0))
                link(pool.memset(pzn[:, :, :], 0.0))
                pool.wait_ge(scaled, 1)

                def fill_q(b):
                    wait(pool, scored, b * 1)
                    for g in range(NG):
                        pool.tensor_copy(ap_of(qz[:, :], ZN[g], [(NR + 1, NH), (NH, NQ)]),
                                         qs[:, g * NH:(g + 1) * NH, bass.ds(b * NQ, NQ)]).then_inc(qz_ready, 1)
                    for h in range(2):
                        pool.tensor_copy(ap_of(qz[:, :], Z1 + h * 4 * NH, [(NH * NR + NH, 4), (NR + 1, NH)]),
                                         qs[:, NH:2 * NH, bass.ds(b * NQ + 4 * h, 4)].rearrange("p h i -> p i h")).then_inc(qz_ready, 1)
                    pool.tensor_copy(ap_of(qz[:, :], Z2, [(NH * NR + NH, NQ), (NR + 1, NH)]),
                                     qs[:, 2 * NH:3 * NH, bass.ds(b * NQ, NQ)].rearrange("p h i -> p i h")).then_inc(qz_ready, 1)

                fill_q(0)
                with pool.Fori(1, NB) as b:
                    fill_q(b)
                pool.wait_ge(toe_stored, 32)

            def evac_k(eng, b, odd, sem):
                copy = eng.tensor_copy if odd else eng.copy
                for q in range(odd, NQUAD, 2):
                    eng.wait_ge(turned, b * NQUAD + (q + 1))
                    wait(eng, score_tiles, b * NQUAD + (q - 1))
                    copy(ktt[:, q % 2, :], kps[q % 2][:, :]).then_inc(sem, 1)

            @block.scalar
            def _(act):
                def one(b):
                    evac_k(act, b, 0, evac_a)
                    act.wait_ge(max_done, b + 1)
                    act.activation(s[:, :], s[:, :], ACT.Exp, bias=stat[:, 1:2], accum_out=stat[:, 2:3]).then_inc(exp_done, 1)

                one(0)
                with act.Fori(1, NB) as b:
                    one(b)

            @block.tensor
            def _(pe):
                def quad_turn(b, q):
                    g, r = TILES[q // 2]
                    if q % 2 == 0 and (g, r) in [(p_[0], p_[1]) for p_ in pieces]:
                        pe.wait_ge(k_in[[(p_[0], p_[1]) for p_ in pieces].index((g, r))], b * 16 + 16)
                    if q >= 2:
                        pe.wait_ge((evac_a, evac_d)[q % 2], b * (NQUAD // 2) + q // 2)
                    for j in range(4):
                        h = 4 * (q % 2) + j
                        ins = pe.transpose(kps[q % 2][:, j * P:(j + 1) * P], kt[g][:, r, h * HD:(h + 1) * HD], k.ident[:, :])
                    ins.then_inc(turned, 1)

                def quad_score(b, q):
                    g, r = TILES[q // 2]
                    pe.wait_ge((evac_a, evac_d)[q % 2], b * (NQUAD // 2) + (q // 2 + 1))
                    for j in range(4):
                        h = 4 * (q % 2) + j
                        first = r == 0 and h == 0
                        last = r == (0, 3, NQ - 1)[g] and h == NH - 1
                        ins = pe.matmul(sps[0:NR, g * P:(g + 1) * P], qz[:, z_block(g, r, h)], ktt[:, q % 2, j * P:(j + 1) * P],
                                        start=first, stop=last)
                    ins.then_inc(score_tiles, 1)

                def scores(b):
                    quad_turn(b, 0)
                    pe.wait_ge(qz_ready, b * 6 + 6)
                    wait(pe, max_done, b * 1)
                    for q in range(NQUAD):
                        if q + 1 < NQUAD:
                            quad_turn(b, q + 1)
                        quad_score(b, q)
                    for g in range(NG):
                        for h in range(NH):
                            o = ZN[g] + h * NR
                            ins = pe.matmul(sps[0:NR, NG * P + g * NQ:NG * P + (g + 1) * NQ], qz[:, o:o + NR],
                                            kn[:, g * NH + h, bass.ds(b * NQ, NQ)], start=(h == 0), stop=(h == NH - 1))
                    ins.then_inc(scored, 1)

                def turn_p(b):
                    pe.wait_ge(p_ready, b + 1)
                    wait(pe, pz_ready, b * 5)
                    settle(pe, k)
                    for g in range(NG):
                        pe.transpose(pps[:, g * NR:(g + 1) * NR], s[:, g * P:(g + 1) * P], k.ident[0:NR, 0:NR])
                    pe.transpose(pps[0:NG * NQ, NG * NR:(NG + 1) * NR], s[:, NG * P:SA], k.ident[0:NR, 0:NR]).then_inc(p_turned, 1)

                def values(b):
                    pe.wait_ge(pz_ready, b * 5 + 5)
                    wait(pe, o_evac, b * 1)
                    n = 0
                    for g, r in TILES:
                        for m, (pg, lo, hi) in enumerate(pieces):
                            if (pg, lo) == (g, r):
                                pe.wait_ge(v_in[m], b * 16 + 16)
                        for h in range(NH):
                            c = z_block(g, r, h).start - (2 * NH * NR if g else 0)
                            ins = pe.matmul(ops[0:NR, 0:HD], pz[:, c:c + NR], vt[g][:, r, h * HD:(h + 1) * HD],
                                            start=(n == 0), stop=False)
                            n += 1
                        if (g, r + 1) in [(p_[0], p_[2]) for p_ in pieces]:
                            ins.then_inc(pv_tiles, 1)
                    pe.wait_ge(vn_in, b * 48 + 48)
                    for h in range(NH):
                        ins = pe.matmul(ops[0:NR, 0:HD], pzn[:, h, :], vnew[:, h * HD:(h + 1) * HD], start=False, stop=(h == NH - 1))
                    ins.then_inc(pv_done, 1)

                def turn_o(b):
                    pe.wait_ge(o_evac, b + 1)
                    wait(pe, o_ready, b * 1)
                    settle(pe, k)
                    pe.transpose(tps[:, 0:NR], orow[:, :], k.ident[0:NR, 0:NR]).then_inc(o_turned, 1)

                scores(0)
                turn_p(0)
                with pe.Fori(1, NB) as b:
                    scores(b)
                    values(b - 1)
                    turn_p(b)
                    turn_o(b - 1)
                values(NB - 1)
                turn_o(NB - 1)

            @block.vector
            def _(dve):
                dve.wait_ge(q_in, 96)
                dve.tensor_scalar(qs[:, :, :], qs[:, :, :], SCALE, None, ALU.mult).then_inc(scaled, 1)
                dve.wait_ge(b_in, 16)
                dve.wait_ge(zeroed, 3)

                def softmax(b):
                    link = Chain(dve, chain, b * 2)
                    dve.wait_ge(scored, b + 1)
                    wait(dve, p_turned, b * 1)
                    settle(dve, k)
                    link(dve.tensor_tensor_reduce(s[:, :], sps[0:NR, 0:SA], bias[:, :], 1.0, -3.0e38, ALU.add, ALU.max, stat[:, 0:1]))
                    dve.tensor_scalar(stat[:, 1:2], stat[:, 0:1], -1.0, None, ALU.mult).then_inc(max_done, 1)
                    dve.wait_ge(exp_done, b + 1)
                    link(dve.reciprocal(stat[:, 3:4], stat[:, 2:3]))
                    dve.tensor_scalar(s[:, :], s[:, :], stat[:, 3:4], None, ALU.mult).then_inc(p_ready, 1)

                def fill_p(b):
                    dve.wait_ge(p_turned, b + 1)
                    wait(dve, pv_done, b * 1)
                    dve.tensor_copy(ap_of(pz[:, :], 0, [(NR + 1, NH), (NH, NQ)]),
                                    ap_of(pps[:, :], 0, [(1, NH), (NH, NQ)])).then_inc(pz_ready, 1)
                    o1, o2 = Z1 - 2 * NH * NR, Z2 - 2 * NH * NR
                    for h in range(2):
                        dve.tensor_copy(ap_of(pz[:, :], o1 + h * 4 * NH, [(NH * NR + NH, 4), (NR + 1, NH)]),
                                        ap_of(pps[:, :], NR + h * 4 * NH, [(NH, 4), (1, NH)])).then_inc(pz_ready, 1)
                    dve.tensor_copy(ap_of(pz[:, :], o2, [(NH * NR + NH, NQ), (NR + 1, NH)]),
                                    ap_of(pps[:, :], 2 * NR, [(NH, NQ), (1, NH)])).then_inc(pz_ready, 1)
                    dve.tensor_copy(ap_of(pzn[:, :, :], 0, [(NR + 1, NH), (NH, NQ)]),
                                    ap_of(pps[0:NG * NQ, :], 3 * NR, [(1, NH), (NH, NQ)])).then_inc(pz_ready, 1)

                def out_rows(b):
                    dve.wait_ge(pv_done, b + 1)
                    wait(dve, o_turned, b * 1)
                    dve.tensor_copy(orow[:, :], ops[0:NR, 0:HD]).then_inc(o_evac, 1)

                def out_cols(b):
                    dve.wait_ge(o_turned, b + 1)
                    dve.tensor_copy(ot[:, :, bass.ds(b * NQ, NQ)], tps[:, 0:NR].rearrange("p (i h) -> p h i", h=NH)).then_inc(o_ready, 1)

                evac_k(dve, 0, 1, evac_d)
                softmax(0)
                fill_p(0)
                with dve.Fori(1, NB) as b:
                    evac_k(dve, b, 1, evac_d)
                    softmax(b)
                    out_rows(b - 1)
                    fill_p(b)
                    out_cols(b - 1)
                out_rows(NB - 1)
                out_cols(NB - 1)


def block_prompt_a(nc, k):
    with k.scope():
        U = 2
        q = k.sb("qpa", [P, U, NG, NP])
        kk = k.sb("kpa", [P, U, NG, NP])
        v = k.sb("vpa", [P, U, 2, NG, HD])
        tab = k.sb("tpa", [P, U, NG, NP])
        s = k.sb("spa", [P, 2, NG, NP])
        pt = k.sb("ptpa", [P, 2, 2 * NG, P])
        stat = k.sb("stpa", [P, 2, 4])
        ot = k.sb("otpa", [P, U, NP])
        sps = [k.ps(f"spa{i}", [P, 1024]) for i in range(2)]
        pps = [k.ps(f"ppa{i}", [P, 512]) for i in range(2)]
        ops = [k.ps(f"opa{i}", [P, 512]) for i in range(2)]
        loaded = [k.sem(f"pp_in{u}") for u in range(U)]
        q_scaled, scored, max_done, exp_done, p_ready, chain = (
            k.sem(n) for n in ("pp_scaled", "pp_scored", "pp_max", "pp_exp", "pp_p", "pp_chain"))
        turned, pt_ready, pv_done, o_ready = (k.sem(n) for n in ("pp_turned", "pp_pt", "pp_pv", "pp_o"))
        stored = [k.sem(f"pp_stored{u}") for u in range(U)]

        with nc.Block() as block:
            @block.sync
            def _(sp):
                with sp.Fori(0, NH // U) as it:
                    for u in range(U):
                        h = it * U + u
                        sp.wait_ge(pv_done, it * (2 * U) + (2 * u + 2))
                        for src, dst in ((0, q), (QKV, kk)):
                            sp.dma_start(dst[:, u, :, :], k.zt[src:src + QKV, 0:NP].rearrange("(g h d) t -> h d g t", g=NG, h=NH)
                                         [bass.ds(h, 1)].rearrange("a d g t -> (a d) g t")).then_inc(loaded[u], 16)
                        sp.dma_start(v[:, u, 0, :, :], k.kv[0:P, QKV:2 * QKV].rearrange("p (g h d) -> h p g d", g=NG, h=NH)
                                     [bass.ds(h, 1)].rearrange("a p g d -> (a p) g d")).then_inc(loaded[u], 16)
                        sp.dma_start(v[:, u, 1, :, :], k.kv[P:NP, QKV:2 * QKV].rearrange("p (g h d) -> h p g d", g=NG, h=NH)
                                     [bass.ds(h, 1)].rearrange("a p g d -> (a p) g d")).then_inc(loaded[u], 16)
                        for g in range(NG):
                            sp.dma_start(tab[:, u, g, :], k.toe_a[g][bass.ds(h, 1)].rearrange("a p n -> (a p) n")).then_inc(loaded[u], 16)

            @block.scalar
            def _(act):
                for u in range(U):
                    act.sem_inc(stored[u], 16)
                with act.Fori(0, NH // U) as it:
                    for u in range(U):
                        for qb in range(2):
                            n = 2 * u + qb
                            nk = P * (qb + 1)
                            act.wait_ge(max_done, it * (2 * U) + (n + 3))
                            act.activation(s[:, qb, :, 0:nk], s[:, qb, :, 0:nk], ACT.Exp, bias=stat[:, qb, 1:2],
                                           accum_out=stat[:, qb, 2:3]).then_inc(exp_done, 1)
                        act.wait_ge(o_ready, it * (2 * U) + (2 * u + 4))
                        act.dma_start(k.mt[bass.ds((it * U + u) * HD, HD), 0:NP], ot[:, u, :]).then_inc(stored[u], 16)
                for u in range(U):
                    act.wait_ge(stored[u], 16 * (NH // U) + 16)

            @block.tensor
            def _(pe):
                pe.sem_inc(pv_done, 2 * U)
                with pe.Fori(0, NH // U) as it:
                    for u in range(U):
                        pe.wait_ge(loaded[u], it * 112 + 112)
                        pe.wait_ge(q_scaled, it * U + (u + 1))
                        for qb in range(2):
                            n = 2 * u + qb
                            nk = P * (qb + 1)
                            pe.wait_ge(max_done, it * (2 * U) + (n + 1))
                            for g in range(NG):
                                ins = pe.matmul(sps[qb][:, g * NP:g * NP + nk], q[:, u, g, qb * P:(qb + 1) * P], kk[:, u, g, 0:nk],
                                                start=True, stop=True)
                            ins.then_inc(scored, 1)
                        for qb in range(2):
                            n = 2 * u + qb
                            pe.wait_ge(p_ready, it * (2 * U) + (n + 1))
                            for half in range(qb + 1):
                                for g in range(NG):
                                    ins = pe.transpose(pps[half][:, g * P:(g + 1) * P], s[:, qb, g, half * P:(half + 1) * P], k.ident[:, :])
                                ins.then_inc(turned, 1)
                            pe.wait_ge(pt_ready, it * (3 * U) + (3 * u + (1, 3)[qb]))
                            pe.wait_ge(o_ready, it * (2 * U) + (n + 1))
                            for half in range(qb + 1):
                                for g in range(NG):
                                    ins = pe.matmul(ops[qb][:, 0:P], v[:, u, half, g, :], pt[:, qb, half * NG + g, :],
                                                    start=(half == 0 and g == 0), stop=(half == qb and g == NG - 1))
                            ins.then_inc(pv_done, 1)

            @block.vector
            def _(dve):
                dve.sem_inc(max_done, 2)
                dve.sem_inc(o_ready, 2)
                with dve.Fori(0, NH // U) as it:
                    link = Chain(dve, chain, it * (4 * U))
                    for u in range(U):
                        dve.wait_ge(loaded[u], it * 112 + 112)
                        dve.tensor_scalar(q[:, u, :, :], q[:, u, :, :], SCALE, None, ALU.mult).then_inc(q_scaled, 1)
                        for qb in range(2):
                            n = 2 * u + qb
                            nk = P * (qb + 1)
                            lo = NP - nk
                            dve.wait_ge(scored, it * (2 * U) + (n + 1))
                            settle(dve, k)
                            link(dve.tensor_tensor_reduce(s[:, qb, :, 0:nk], sps[qb][:, 0:NG * NP].rearrange("p (g n) -> p g n", g=NG)[:, :, 0:nk],
                                                          tab[:, u, :, lo:NP], 1.0, -3.0e38, ALU.add, ALU.max, stat[:, qb, 0:1]))
                            dve.tensor_scalar(stat[:, qb, 1:2], stat[:, qb, 0:1], -1.0, None, ALU.mult).then_inc(max_done, 1)
                        for qb in range(2):
                            n = 2 * u + qb
                            nk = P * (qb + 1)
                            dve.wait_ge(exp_done, it * (2 * U) + (n + 1))
                            link(dve.reciprocal(stat[:, qb, 3:4], stat[:, qb, 2:3]))
                            dve.tensor_scalar(s[:, qb, :, 0:nk], s[:, qb, :, 0:nk], stat[:, qb, 3:4], None, ALU.mult).then_inc(p_ready, 1)
                        for qb in range(2):
                            n = 2 * u + qb
                            for half in range(qb + 1):
                                dve.wait_ge(turned, it * (3 * U) + (3 * u + qb + half + 1))
                                dve.tensor_copy(pt[:, qb, half * NG:(half + 1) * NG, :], pps[half][:, 0:NG * P].rearrange("p (g n) -> p g n", g=NG)).then_inc(pt_ready, 1)
                        for qb in range(2):
                            n = 2 * u + qb
                            dve.wait_ge(pv_done, it * (2 * U) + (2 * U + n + 1))
                            dve.wait_ge(stored[u], it * 16 + 16)
                            dve.tensor_copy(ot[:, u, qb * P:(qb + 1) * P], ops[qb][:, 0:P]).then_inc(o_ready, 1)


def block_conv(nc, k):
    KB = WB // P
    H = TAPS - 1
    with k.scope():
        u = k.sb("u", [P, KB, T])
        e = k.sb("e", [P, KB, T])
        up = k.sb("up", [P, KB, H + NP])
        us = k.sb("us", [P, KB, NB, H + NQ])
        y = k.sb("y", [P, KB, T])
        hrow = k.sb("hrow", [4 * H, 2, WB])
        crow = k.sb("crow", [NS, 2, WB])
        taps = k.sb("taps", [P, KB, TAPS])
        vec = k.sb("cvec", [P, 4, KB])
        pw = k.sb("pw", [P, KB, WB])
        mu = k.sb("mu", [P, T])
        rs = k.sb("rsb", [P, T])
        hps = [k.ps(f"hps{i}", [P, 512]) for i in range(2)]
        cps = [k.ps(f"cps{i}", [P, 512]) for i in range(2)]
        lps = [k.ps(f"lps{i}", [P, 512]) for i in range(2)]
        pps = [k.ps(f"pwp{i}", [P, 512]) for i in range(2)]
        g_in, h_in, v_in, pw_in = (k.sem(n) for n in ("glu_in", "hist_in", "cvec_in", "pw_in"))
        copied, padded, e_done, u_ready, chain, full = (k.sem(n) for n in ("conv_copied", "conv_padded", "glu_exp", "u_ready", "conv_chain", "conv_full"))
        h_turned, h_evac, c_turned, c_evac, c_stored = (k.sem(n) for n in ("h_turned", "h_evac", "c_turned", "c_evac", "c_stored"))
        taps_done, y_sum, yc_ready, var_sum, root, e2_done, act_ready, pw_done, o_ready, o_stored = (
            k.sem(n) for n in ("taps_done", "y_sum", "yc_ready", "var_sum", "ln_root", "silu_exp", "silu_ready", "pw_done", "ob_ready", "ob_stored"))
        ln_in = k.sem("ln_in")
        with nc.Block() as block:
            @block.sync
            def _(sp):
                sp.dma_start(u[:, :, :], k.zt[Z_A:Z_A + WB, :].rearrange("(c p) t -> p c t", p=P)).then_inc(g_in, 16)
                sp.dma_start(e[:, :, :], k.zt[Z_GT:Z_GT + WB, :].rearrange("(c p) t -> p c t", p=P)).then_inc(g_in, 16)
                for i in range(2):
                    sp.dma_start(hrow[:, i, :], k.state_b_conv[4 * i:4 * i + 4].rearrange("b t n -> (b t) n")).then_inc(h_in, 16)
                sp.dma_start(taps[:, :, :], k.conv_w).then_inc(v_in, 16)
                for i, v in enumerate((k.conv_b, k.conv_ln_g, k.conv_ln_b, k.conv_pw_b)):
                    sp.dma_start(vec[:, i, :], v).then_inc(v_in, 16)
                sp.dma_start(pw[:, :, :], k.conv_pw_w.rearrange("(c p) n -> p c n", p=P)).then_inc(pw_in, 16)
                for b in range(NB):
                    sp.dma_start(k.out_conv_s[b, 0:H - NQ, :], k.state_b_conv[b, NQ:H, :]).then_inc(copied, 16)
                sp.wait_ge(c_evac, 4)
                sp.dma_start(k.out_conv_p, crow[0:H, 0, :]).then_inc(c_stored, 16)
                for b in range(NB):
                    sp.dma_start(k.out_conv_s[b, H - NQ:H, :], crow[b * NQ:(b + 1) * NQ, 1, :]).then_inc(c_stored, 16)
                sp.wait_ge(o_ready, KB)
                sp.dma_start(k.mt[NH * HD:, :].rearrange("(c p) t -> p c t", p=P), y[:, :, :]).then_inc(o_stored, 16)
                sp.wait_ge(copied, 16 * NB)
                sp.wait_ge(c_stored, 16 * (NB + 1))
                sp.wait_ge(o_stored, 16)

            @block.gpsimd
            def _(pool):
                pool.memset(up[:, :, 0:H], 0.0).then_inc(padded, 1)

            @block.scalar
            def _(act):
                act.wait_ge(g_in, 32)
                act.activation(e[:, :, :], e[:, :, :], ACT.Exp, scale=-1.0).then_inc(e_done, 1)
                act.wait_ge(var_sum, 1)
                act.activation(rs[:, :], lps[1][:, 0:T], ACT.Sqrt, bias=k.eps[:, :], scale=1.0 / WB).then_inc(root, 1)
                for c in range(KB):
                    act.wait_ge(ln_in, c + 1)
                    act.activation(e[:, c, :], y[:, c, :], ACT.Exp, scale=-1.0).then_inc(e2_done, 1)

            @block.tensor
            def _(pe):
                pe.wait_ge(h_in, 32)
                for c in range(KB):
                    if c >= 2:
                        pe.wait_ge(h_evac, c - 1)
                    for i in range(2):
                        ins = pe.transpose(hps[c % 2][:, i * 4 * H:(i + 1) * 4 * H], hrow[:, i, c * P:(c + 1) * P], k.ident[0:4 * H, 0:4 * H])
                    ins.then_inc(h_turned, 1)
                pe.wait_ge(u_ready, 1)
                for j, (lo, m) in enumerate(((NP - H, H), (NP, NS))):
                    for half in range(2):
                        if j:
                            pe.wait_ge(c_evac, half + 1)
                        for c in range(4):
                            ins = pe.transpose(cps[half][0:m, c * P:(c + 1) * P], u[:, half * 4 + c, lo:lo + m], k.ident[:, :])
                        ins.then_inc(c_turned, 1)
                pe.wait_ge(taps_done, 2 * KB * TAPS)
                for c in range(KB):
                    ins = pe.matmul(lps[0][:, 0:T], k.ones[:, :], y[:, c, :], start=(c == 0), stop=(c == KB - 1))
                ins.then_inc(y_sum, 1)
                pe.wait_ge(yc_ready, 1)
                for c in range(KB):
                    ins = pe.matmul(lps[1][:, 0:T], k.ones[:, :], e[:, c, :], start=(c == 0), stop=(c == KB - 1))
                ins.then_inc(var_sum, 1)
                pe.wait_ge(act_ready, KB)
                pe.wait_ge(pw_in, 16)
                for n in range(KB):
                    if n >= 2:
                        pe.wait_ge(o_ready, n - 1)
                    for c in range(KB):
                        ins = pe.matmul(pps[n % 2][:, 0:T], pw[:, c, n * P:(n + 1) * P], u[:, c, :], start=(c == 0), stop=(c == KB - 1))
                    ins.then_inc(pw_done, 1)

            @block.vector
            def _(dve):
                link = Chain(dve, chain)
                dve.wait_ge(e_done, 1)
                link(dve.tensor_scalar(e[:, :, :], e[:, :, :], 1.0, None, ALU.add))
                link(dve.reciprocal(e[:, :, :], e[:, :, :]))
                dve.tensor_tensor(u[:, :, :], u[:, :, :], e[:, :, :], ALU.mult).then_inc(u_ready, 1)
                dve.wait_ge(u_ready, 1)
                link(dve.tensor_copy(up[:, :, H:], u[:, :, 0:NP]))
                link(dve.tensor_copy(us[:, :, :, H:], u[:, :, NP:T].rearrange("p c (b q) -> p c b q", q=NQ)))
                for c in range(KB):
                    dve.wait_ge(h_turned, c + 1)
                    dve.tensor_copy(us[:, c, :, 0:H], hps[c % 2][:, 0:NB * H].rearrange("p (b t) -> p b t", t=H)).then_inc(h_evac, 1)
                for j, m in enumerate((H, NS)):
                    for half in range(2):
                        dve.wait_ge(c_turned, 2 * j + half + 1)
                        dve.tensor_copy(crow[0:m, j, half * 512:(half + 1) * 512], cps[half][0:m, :]).then_inc(c_evac, 1)
                dve.wait_ge(h_evac, KB)
                dve.wait_ge(v_in, 80)
                dve.wait_ge(padded, 1)

                def views(c, j, t):
                    if j == 0:
                        return y[:, c, 0:NP], (up[:, c, bass.ds(t, NP)])
                    return y[:, c, NP:T].rearrange("p (b q) -> p b q", q=NQ), us[:, c, :, bass.ds(t, NQ)]

                for j in range(2):
                    for c in range(KB):
                        out, x = views(c, j, 0)
                        dve.tensor_scalar(out, x, taps[:, c, 0:1], vec[:, 0, c:c + 1], ALU.mult, ALU.add).then_inc(taps_done, 1)
                with dve.Fori(1, TAPS) as t:
                    for j in range(2):
                        for c in range(KB):
                            n = j * KB + c
                            dve.wait_ge(taps_done, t * (2 * KB) + (n + 1 - 2 * KB))
                            out, x = views(c, j, t)
                            dve.scalar_tensor_tensor(out, x, taps[:, c, bass.ds(t, 1)], out, ALU.mult, ALU.add).then_inc(taps_done, 1)
                dve.wait_ge(y_sum, 1)
                link(dve.tensor_scalar(mu[:, :], lps[0][:, 0:T], 1.0 / WB, None, ALU.mult))
                all_c = [P, KB, T]
                link(dve.tensor_tensor(y[:, :, :], y[:, :, :], mu[:, :].unsqueeze(1).broadcast_to(all_c), ALU.subtract))
                dve.tensor_tensor(e[:, :, :], y[:, :, :], y[:, :, :], ALU.mult).then_inc(yc_ready, 1)
                dve.wait_ge(root, 1)
                link(dve.reciprocal(rs[:, :], rs[:, :]))
                link(dve.tensor_tensor(y[:, :, :], y[:, :, :], rs[:, :].unsqueeze(1).broadcast_to(all_c), ALU.mult))
                for c in range(KB):
                    dve.tensor_scalar(y[:, c, :], y[:, c, :], vec[:, 1, c:c + 1], vec[:, 2, c:c + 1], ALU.mult, ALU.add).then_inc(ln_in, 1)
                for c in range(KB):
                    dve.wait_ge(e2_done, c + 1)
                    link(dve.tensor_scalar(e[:, c, :], e[:, c, :], 1.0, None, ALU.add))
                    link(dve.reciprocal(e[:, c, :], e[:, c, :]))
                    dve.tensor_tensor(u[:, c, :], y[:, c, :], e[:, c, :], ALU.mult).then_inc(act_ready, 1)
                for n in range(KB):
                    dve.wait_ge(pw_done, n + 1)
                    dve.tensor_scalar(y[:, n, :], pps[n % 2][:, 0:T], vec[:, 3, n:n + 1], None, ALU.add).then_inc(o_ready, 1)


def gate_mix(act, dve, mix, gate, e, loaded, exp_done, chain, done):
    if act is not None:
        act.wait_ge(loaded, 48)
        for c in range(4):
            act.activation(e[:, c * 4:(c + 1) * 4, :], gate[:, c * 4:(c + 1) * 4, :], ACT.Exp, scale=-1.0).then_inc(exp_done, 1)
    if dve is not None:
        link = Chain(dve, chain)
        dve.wait_ge(loaded, 48)
        for c in range(4):
            s = slice(c * 4, (c + 1) * 4)
            dve.wait_ge(exp_done, c + 1)
            link(dve.tensor_scalar(e[:, s, :], e[:, s, :], 1.0, None, ALU.add))
            link(dve.reciprocal(e[:, s, :], e[:, s, :]))
            link(dve.tensor_tensor(mix[:, s, :], mix[:, s, :], gate[:, s, :], ALU.mult))
            dve.tensor_tensor(mix[:, s, :], mix[:, s, :], e[:, s, :], ALU.mult).then_inc(done, 1)


def block_even_out_odd_in(nc, k):
    with k.scope():
        mix = k.sb("mix2", [P, KT, T])
        gate = k.sb("gate2", [P, KT, T])
        xT = k.sb("xT2", [P, KT, T])
        xn = k.sb("xn2", [P, KT, T])
        gcol = k.sb("gcol2", [P, KT])
        wg = k.sb("wg", [P, KT, 3 * CH])
        gr = k.sb("gr", [P, 3, 3 * CH])
        banks = [k.ps(f"zc{i}", [P, 512]) for i in range(4)]
        rbanks = [k.ps(f"rc{i}", [P, 512]) for i in range(3)]
        nbank = k.ps("nc2", [P, 512])
        loaded, x_in, g_in, wg_in, exp_done, chain, mixed = (k.sem(n) for n in (
            "mix2_in", "xT2_in", "g2_in", "wg_in", "mix2_exp", "mix2_chain", "mixed2"))
        gs = k.sb("gs", [3 * CH, NQ, NB])
        gs_turned, gs_ready = k.sem("gs_turned"), k.sem("gs_ready")
        gl_done, gl_exp, gl_chain, gl_stored, xt_stored = (k.sem(n) for n in ("gl_done", "gl_exp", "gl_chain", "gl_stored", "xt2_stored"))
        norm = Norm(k, "2", xT, xn, gcol, nbank)
        out = Proj(k, "2", k.w_out_even, KT, mix, banks, [(4, 0, 0, None)], residual=xT)
        proj = Proj(k, "3", k.w_in_odd, KT, xn, banks, [(4, 0, 0, None), (3, CW, CW, 0), (4, C_GP, Z2_GP, None)],
                    zt=k.z2, rows=k.kv2, row_banks=rbanks)
        with nc.Block() as block:
            @block.sync
            def _(sp):
                view = lambda a: a.rearrange("(k p) t -> p k t", p=P)
                sp.dma_start(mix[:, :, :], view(k.mt)).then_inc(loaded, 16)
                sp.dma_start(gate[:, 0:8, :], view(k.zt[Z_GA:Z_GA + 1024, :])).then_inc(loaded, 16)
                sp.dma_start(gate[:, 8:16, :], view(k.zt[Z_GB:Z_GB + 1024, :])).then_inc(loaded, 16)
                sp.dma_start(xT[:, :, :], view(k.xt)).then_inc(x_in, 16)
                sp.dma_start(gcol[:, :], k.norm_odd).then_inc(g_in, 16)
                out.sync(sp)
                sp.dma_start(wg[:, :, :], k.w_in_odd[:, C_GL:C_GL + 3 * CH].rearrange("(k p) n -> p k n", p=P)).then_inc(wg_in, 16)
                proj.sync(sp)
                sp.dma_start(view(k.xt), xT[:, :, :]).then_inc(xt_stored, 16)
                sp.dma_start(k.gates.rearrange("(t p) n -> p t n", p=P), gr[:, 0:2, :]).then_inc(gl_stored, 16)
                sp.wait_ge(gs_ready, 1)
                sp.dma_start(k.gates_s, gs[:, :, :]).then_inc(gl_stored, 16)
                sp.wait_ge(gl_stored, 32)
                sp.wait_ge(xt_stored, 16)
                sp.wait_ge(proj.z_stored, 16 * 12)
                sp.wait_ge(proj.rows_stored, 32 * 4)

            @block.scalar
            def _(act):
                gate_mix(act, None, mix, gate, xn, loaded, exp_done, chain, mixed)
                norm.act(act)
                for t, m in enumerate((P, P, NS)):
                    act.wait_ge(gl_done, t + 1)
                    act.activation(gr[0:m, t, :], rbanks[t][0:m, 0:3 * CH], ACT.Exp, scale=-1.0).then_inc(gl_exp, 1)
                proj.act(act)

            @block.tensor
            def _(pe):
                out.pe(pe, lambda e: e.wait_ge(mixed, 4))
                norm.pe(pe)
                pe.wait_ge(wg_in, 16)
                pe.wait_ge(norm.ready, KT)
                for t, m in enumerate((P, P, NS)):
                    for j in range(KT):
                        ins = pe.matmul(rbanks[t][0:m, 0:3 * CH], xn[:, j, t * P:t * P + m], wg[:, j, :], start=(j == 0), stop=(j == KT - 1))
                    ins.then_inc(gl_done, 1)
                pe.wait_ge(gl_chain, 6)
                pe.transpose(nbank[0:3 * CH, 0:NS], gr[0:NS, 2, :], k.ident[0:NS, 0:NS]).then_inc(gs_turned, 1)
                proj.pe(pe, lambda e: None)

            @block.vector
            def _(dve):
                gate_mix(None, dve, mix, gate, xn, loaded, exp_done, chain, mixed)
                dve.wait_ge(x_in, 16)
                out.dve_residual(dve)
                dve.wait_ge(out.z_ready, 20)
                dve.wait_ge(g_in, 16)
                norm.dve(dve, lambda e, t: None)
                link = Chain(dve, gl_chain)
                for t, m in enumerate((P, P, NS)):
                    dve.wait_ge(gl_exp, t + 1)
                    link(dve.tensor_scalar(gr[0:m, t, :], gr[0:m, t, :], 1.0, None, ALU.add))
                    link(dve.reciprocal(gr[0:m, t, :], gr[0:m, t, :]))
                dve.wait_ge(gs_turned, 1)
                dve.tensor_copy(gs[:, :, :], nbank[0:3 * CH, 0:NS].rearrange("p (b i) -> p i b", b=NB)).then_inc(gs_ready, 1)
                proj.dve_rows(dve)


def block_final(nc, k):
    with k.scope():
        mix = k.sb("mix4", [P, KT, T])
        gate = k.sb("gate4", [P, KT, T])
        xT = k.sb("xT4", [P, KT, T])
        xn = k.sb("xn4", [P, KT, T])
        gcol = k.sb("gcol4", [P, KT])
        yrow = k.sb("yrow", [P, 3, D])
        banks = [k.ps(f"zd{i}", [P, 512]) for i in range(4)]
        ybanks = [k.ps(f"yb{i}", [P, 512]) for i in range(3)]
        nbank = k.ps("nd", [P, 512])
        loaded, x_in, g_in, exp_done, chain, mixed = (k.sem(n) for n in ("mix4_in", "xT4_in", "g4_in", "mix4_exp", "mix4_chain", "mixed4"))
        turned, y_ready, y_stored = (k.sem(n) for n in ("y_turned", "y_ready", "y_stored"))
        norm = Norm(k, "4", xT, xn, gcol, nbank)
        out = Proj(k, "4", k.w_out_odd, KT, mix, banks, [(4, 0, 0, None)], residual=xT)
        sizes = (P, P, NS)
        with nc.Block() as block:
            @block.sync
            def _(sp):
                view = lambda a: a.rearrange("(k p) t -> p k t", p=P)
                sp.dma_start(mix[:, :, :], view(k.mt)).then_inc(loaded, 16)
                sp.dma_start(gate[:, 0:8, :], view(k.z2[Z2_GP:Z2_GP + 1024, :])).then_inc(loaded, 16)
                sp.dma_start(gate[:, 8:16, :], view(k.z2[Z2_GP + 1024:, :])).then_inc(loaded, 16)
                sp.dma_start(xT[:, :, :], view(k.xt)).then_inc(x_in, 16)
                sp.dma_start(gcol[:, :], k.final_norm).then_inc(g_in, 16)
                out.sync(sp)
                for t in range(3):
                    sp.wait_ge(y_ready, 4 * t + 4)
                    dst = k.out_y_p[t * P:(t + 1) * P, :] if t < 2 else k.out_y_s
                    sp.dma_start(dst, yrow[0:sizes[t], t, :]).then_inc(y_stored, 16)
                sp.wait_ge(y_stored, 48)

            @block.scalar
            def _(act):
                gate_mix(act, None, mix, gate, xn, loaded, exp_done, chain, mixed)
                norm.act(act)

            @block.tensor
            def _(pe):
                out.pe(pe, lambda e: e.wait_ge(mixed, 4))
                norm.pe(pe)
                pe.wait_ge(norm.ready, KT)
                for n in range(12):
                    t, f = n // 4, n % 4
                    m = sizes[t]
                    if n >= 3:
                        pe.wait_ge(y_ready, n - 2)
                    for c in range(4):
                        ins = pe.transpose(ybanks[n % 3][0:m, c * P:(c + 1) * P], xn[:, 4 * f + c, t * P:t * P + m], k.ident[:, :])
                    ins.then_inc(turned, 1)

            @block.vector
            def _(dve):
                gate_mix(None, dve, mix, gate, xn, loaded, exp_done, chain, mixed)
                dve.wait_ge(x_in, 16)
                out.dve_residual(dve)
                dve.wait_ge(out.z_ready, 20)
                dve.wait_ge(g_in, 16)
                norm.dve(dve, lambda e, t: None)
                for n in range(12):
                    t, f = n // 4, n % 4
                    m = sizes[t]
                    dve.wait_ge(turned, n + 1)
                    dve.tensor_copy(yrow[0:m, t, f * 512:(f + 1) * 512], ybanks[n % 3][0:m, :]).then_inc(y_ready, 1)


O_W, O_WN, O_S = 0, WIN, WIN + NQ
O_SN = O_S + PAST
O_C = O_SN + NQ
NSC = O_C + NCS


class Compress:

    def __init__(self, k, tag):
        self.k = k
        self.w1 = k.sb("cw1" + tag, [P, 2, CB, HD])
        self.w2 = k.sb("cw2" + tag, [P, 2, HD])
        self.pos = k.sb("cpos" + tag, [P, 2 * CB])
        self.b1 = k.sb("cb1" + tag, [P, 2])
        self.bias = k.sb("cbias" + tag, [P, 2])
        self.nbias = k.sb("cnbias" + tag, [P, 2])
        self.loaded, self.done, self.ready = (k.sem(n + tag) for n in ("cmp_in", "cmp_pos_done", "cmp_bias"))

    def sync(self, sp):
        for i in range(2):
            sp.dma_start(self.w1[:, i, :, :], self.k.cmp_w1[i].rearrange("l d e -> d l e")).then_inc(self.loaded, 16)
        sp.dma_start(self.w2[:, :, :], self.k.cmp_w2.rearrange("a e d -> e a d")).then_inc(self.loaded, 16)
        sp.dma_start(self.pos[:, :], self.k.cmp_pos).then_inc(self.loaded, 16)
        sp.dma_start(self.b1[:, :], self.k.cmp_b1).then_inc(self.loaded, 16)

    def pe(self, pe, bank):
        pe.wait_ge(self.loaded, 80)
        for i in range(2):
            for l in range(CB):
                ins = pe.matmul(bank[:, i:i + 1], self.w1[:, i, l, :], self.pos[:, i * CB + l:i * CB + l + 1], start=(l == 0), stop=(l == CB - 1))
        ins.then_inc(self.done, 1)

    def dve(self, dve, bank):
        dve.wait_ge(self.done, 1)
        link = Chain(dve, self.ready)
        link(dve.tensor_tensor(self.bias[:, :], bank[:, 0:2], self.b1[:, :], ALU.add))
        link(dve.tensor_scalar(self.nbias[:, :], self.bias[:, :], -1.0, None, ALU.mult))


def block_sample_c(nc, k):
    with k.scope():
        pk = k.sb("pk", [P, NPG, 3 * CKV])
        pv = k.sb("pv", [P, NPG, CKV])
        win = k.sb("win", [P, WIN // P, 2 * CKV])
        xt = k.sb("xtc", [P, 4, PAST])
        cmp = Compress(k, "s")
        qs = k.sb("qsc", [P, CH, NS])
        kn = k.sb("knc", [P, 2, CG, NS])
        vn = k.sb("vnc", [NQ, 2, CKV])
        qc = k.sb("qc", [P, CG, P])
        ktt = k.sb("kttc", [P, 2, 4, P])
        ptt = k.sb("pttc", [P, 2, 4, P])
        bias = k.sb("bias_sc", [P, O_C])
        s = k.sb("s_sc", [P, NSC])
        hh = k.sb("hh", [P, 2, CG * NCS])
        he = k.sb("he", [P, CG * NCS])
        kc = k.sb("kc", [P, CG * NCS])
        vc = k.sb("vc", [NCS, CKV])
        pct = k.sb("pct", [NCS, P])
        t1 = k.sb("t1", [P, NSEL])
        rank = k.sb("rank", [P, 3, NSEL])
        m8 = k.sb("m8", [P, 2, 8])
        st = k.sb("st_sc", [P, 3, 4])
        ov = k.sb("ov", [NCS, NSEL])
        hs = k.sb("hs", [P, P])
        gt = k.sb("gt", [P, 3, NB])
        oc = k.sb("oc", [P, HD])
        orow = k.sb("orowc", [P, HD])
        ot = k.sb("otc", [P, CH, NS])
        xb = [k.ps(f"xb{i}", [P, 512]) for i in range(2)]
        sb_ = [k.ps(f"scb{i}", [P, 512]) for i in range(2)]
        hb, mb, m2, ob = (k.ps(n, [P, 512]) for n in ("hb", "mb", "m2", "ob"))
        MC, MT1, MIMP = 16, 144, 184

        NPIECE = 4
        pt_in = k.sem("pt_in")
        pk_in = [k.sem(f"pk_in{i}") for i in range(NPIECE)]
        pv_in = [k.sem(f"pv_in{i}") for i in range(NPIECE)]
        win_in, vn_in, small_in, bias_in, gt_in = (k.sem(n) for n in ("win_in", "vnc_in", "smallc_in", "biasc_in", "gt_in"))
        zeroed, scaled, qc_ready, turned, evac_a, evac_d, score_q, s_evac = (
            k.sem(n) for n in ("zc_set", "qsc_scaled", "qc_ready", "c_turns", "c_evac_a", "c_evac_d", "c_scoreq", "c_sevac"))
        h_done, h_exp, hh_ready, w2_done, kc_ready, cs_done, new_done = (
            k.sem(n) for n in ("h_done", "h_exp", "hh_ready", "w2_done", "kc_ready", "cs_done", "new_done"))
        max_c, exp_c, pc_ready, pct_done, pct_ready, t1_done, t1_ready, imp_done = (
            k.sem(n) for n in ("max_c", "exp_c", "pc_ready", "pct_done", "pct_ready", "t1_done", "t1_ready", "imp_done"))
        max_w, exp_w, pw_ready, max_s, exp_s, ps_ready = (k.sem(n) for n in ("max_w", "exp_w", "pw_ready", "max_s", "exp_s", "ps_ready"))
        imp_seen = k.sem("imp_seen")
        chain, pv_q, o_evac, o_turned, o_ready, o_stored, rows_out = (
            k.sem(n) for n in ("sc_chain", "pv_q", "oc_evac", "oc_turned", "oc_ready", "oc_stored", "rows_out"))
        TX, TW, TS, TP = 0, NPG, NPG + 2, NPG + 10
        NT = TP + 6
        CHAIN = 21

        with nc.Block() as block:
            @block.sync
            def _(sp):
                cmp.sync(sp)
                for i in range(4):
                    sp.dma_start(qs[:, 4 * i:4 * i + 4, :], k.z2[i * 512:(i + 1) * 512, NP:T].rearrange("(h d) t -> d h t", d=HD)).then_inc(small_in, 16)
                for i, c in enumerate((C_KS, C_KW)):
                    sp.dma_start(kn[:, i, :, :], k.z2[c:c + CKV, NP:T].rearrange("(g d) t -> d g t", d=HD)).then_inc(small_in, 16)
                sp.dma_start(ov[:, :], k.c_overlap).then_inc(small_in, 16)
                sp.dma_start(hs[:, :], k.c_hsum).then_inc(small_in, 16)

                def load(b, first=False):
                    def pages(dst, sems, lo, hi, frees, free_at):
                        for pg in range(NPG):
                            n = pg * NPIECE // NPG
                            if not first and pg % (NPG // NPIECE) == 0:
                                sp.wait_ge(frees, free_at(n))
                                settle(sp, k)
                            page = sp.value_load(k.page_table[bass.ds(b, 1), pg:pg + 1], min_val=0, max_val=k.cache_c_kv.shape[0] - 1)
                            sp.dma_start(dst[:, pg, :], k.cache_c_kv[bass.ds(page, 1)].rearrange("a t c g d -> (a t) (c g d)")[:, lo:hi]
                                         ).then_inc(sems[n], 16)

                    pages(pk, pk_in, 0, 3 * CKV, turned, lambda n: b * NT - NT + (TS + 2 * n + 2))
                    sp.dma_start(win[:, :, :], k.cache_c_win[bass.ds(b, 1)].rearrange("a (r p) c g d -> p (a r) (c g d)", p=P)).then_inc(win_in, 16)
                    if not first:
                        sp.wait_ge(pv_q, b * 6)
                    sp.dma_start(vn[:, 0, :], k.kv2[bass.ds(b * NQ + NP, NQ), 3 * CKV:4 * CKV]).then_inc(vn_in, 16)
                    sp.dma_start(vn[:, 1, :], k.kv2[bass.ds(b * NQ + NP, NQ), 5 * CKV:6 * CKV]).then_inc(vn_in, 16)
                    pages(pv, pv_in, 3 * CKV, 4 * CKV, pv_q, lambda n: b * 6 - 6 + (2 + n))

                load(0, True)
                with sp.Fori(1, NB) as b:
                    sp.wait_ge(pv_q, b * 6 - 5)
                    load(b)
                sp.wait_ge(o_ready, NB)
                sp.dma_start(k.mt[:, NP:T].rearrange("(h d) t -> d h t", d=HD), ot[:, :, :]).then_inc(o_stored, 16)
                sp.wait_ge(o_stored, 16)

            @block.gpsimd
            def _(pool):
                link = Chain(pool, zeroed)
                link(pool.memset(qc[:, :, :], 0.0))
                link(pool.memset(rank[:, 0, :], 1.0e30))
                for g in range(CG):
                    for i in range(NQ):
                        r = (g * NQ + i) * CHG
                        pool.dma_start(bias[r:r + CHG, O_S:O_S + PAST + NQ], k.tab_hc[g * CHG:(g + 1) * CHG, NQ - 1 - i:NQ - 1 - i + PAST + NQ]).then_inc(bias_in, 16)
                        pool.dma_start(bias[r:r + CHG, O_W:O_W + WIN + NQ], k.tab_hw[g * CHG:(g + 1) * CHG, NQ - 1 - i:NQ - 1 - i + WIN + NQ]).then_inc(bias_in, 16)
                    for br in range(3):
                        pool.dma_start(gt[g * 64:(g + 1) * 64, br, :],
                                       dram_ap(k.gates_s, (br * CH + g * CHG) * NS, [(NB, NQ), (NS, CHG), (1, NB)])).then_inc(gt_in, 16)
                n = 0
                for dst, c0, c1 in ((k.out_rows_p, 0, 4 * CKV), (k.out_win_p, 4 * CKV, 6 * CKV)):
                    pool.dma_start(dst.rearrange("t c g d -> t (c g d)"), k.kv2[0:NP, c0:c1]).then_inc(rows_out, 16)
                    n += 1
                pool.dma_start(k.out_rows_s.rearrange("b t c g d -> (b t) (c g d)"), k.kv2[NP:T, 0:4 * CKV]).then_inc(rows_out, 16)
                n += 1
                for b in range(NB):
                    pool.dma_start(k.out_win_s[b, 0:WIN - NQ].rearrange("t c g d -> t (c g d)"), k.cache_c_win[b, NQ:WIN].rearrange("t c g d -> t (c g d)")).then_inc(rows_out, 16)
                    pool.dma_start(k.out_win_s[b, WIN - NQ:WIN].rearrange("t c g d -> t (c g d)"), k.kv2[NP + b * NQ:NP + (b + 1) * NQ, 4 * CKV:]).then_inc(rows_out, 16)
                    n += 2
                pool.wait_ge(scaled, 1)

                def fill_q(b):
                    wait(pool, score_q, b * 10)
                    wait(pool, cs_done, b * 1)
                    for g in range(CG):
                        pool.tensor_copy(qc[:, g, g * 64:(g + 1) * 64].rearrange("p (i h) -> p h i", h=CHG),
                                         qs[:, g * CHG:(g + 1) * CHG, bass.ds(b * NQ, NQ)]).then_inc(qc_ready, 1)

                fill_q(0)
                with pool.Fori(1, NB) as b:
                    fill_q(b)
                pool.wait_ge(rows_out, 16 * n)

            def evac(eng, b, q, copy, sem):
                eng.wait_ge(turned, b * NT + (q + 1))
                bank = xb[q % 2]
                if q < TW:
                    copy(xt[:, :, q * P:(q + 1) * P], bank[:, :].rearrange("p (c n) -> p c n", c=4)).then_inc(sem, 1)
                elif q < TP:
                    if q >= TW + 2:
                        eng.wait_ge(score_q, b * 10 + (q - TW - 1))
                    copy(ktt[:, q % 2, :, :], bank[:, :].rearrange("p (c n) -> p c n", c=4)).then_inc(sem, 1)
                else:
                    if q >= TP + 2:
                        eng.wait_ge(pv_q, b * 6 + (q - TP - 1))
                    if q < TP + 5:
                        copy(ptt[:, q % 2, :, :], bank[:, :].rearrange("p (c n) -> p c n", c=4)).then_inc(sem, 1)
                    else:
                        copy(ptt[0:NQ, q % 2, 0:2, :], bank[0:NQ, 0:2 * P].rearrange("p (c n) -> p c n", c=2)).then_inc(sem, 1)

            @block.scalar
            def _(act):
                act.wait_ge(cmp.ready, 2)

                def one(b):
                    def ev(q):
                        evac(act, b, q, act.copy, evac_a)

                    for q in range(0, TW, 2):
                        ev(q)
                    for i in range(2):
                        act.wait_ge(h_done, b * 2 + (i + 1))
                        if i:
                            act.wait_ge(hh_ready, b * 2 + i)
                        else:
                            wait(act, hh_ready, b * 2)
                        act.activation(he[:, :], (hb, m2)[i][:, 0:CG * NCS], ACT.Exp, bias=cmp.nbias[:, i:i + 1], scale=-1.0).then_inc(h_exp, 1)
                    for q in (16, 18, 20, 22):
                        ev(q)
                    act.wait_ge(max_c, b + 1)
                    act.activation(s[:, O_C:], mb[:, MC:MC + NCS], ACT.Exp, bias=st[:, 0, 1:2], accum_out=st[:, 0, 2:3]).then_inc(exp_c, 1)
                    ev(24)
                    act.wait_ge(max_w, b + 1)
                    act.activation(s[:, O_W:O_S], s[:, O_W:O_S], ACT.Exp, bias=st[:, 1, 1:2], accum_out=st[:, 1, 2:3]).then_inc(exp_w, 1)
                    ev(26)
                    act.wait_ge(max_s, b + 1)
                    act.activation(s[:, O_S:O_C], s[:, O_S:O_C], ACT.Exp, bias=st[:, 2, 1:2], accum_out=st[:, 2, 2:3]).then_inc(exp_s, 1)
                    ev(28)
                    ev(30)

                one(0)
                with act.Fori(1, NB) as b:
                    one(b)

            @block.tensor
            def _(pe):
                cmp.pe(pe, hb)
                pe.wait_ge(cmp.ready, 2)
                pe.wait_ge(small_in, 128)

                def turn(b, q):
                    if q >= 2:
                        pe.wait_ge((evac_a, evac_d)[q % 2], b * (NT // 2) + q // 2)
                    else:
                        wait(pe, (evac_a, evac_d)[q % 2], b * (NT // 2))
                    if q < TW:
                        if q % (NPG // NPIECE) == 0:
                            pe.wait_ge(pk_in[q * NPIECE // NPG], b * 64 + 64)
                        src = [pk[:, q, j * P:(j + 1) * P] for j in range(4)]
                    elif q < TS:
                        if q == TW:
                            pe.wait_ge(win_in, b * 16 + 16)
                        src = [win[:, 2 * (q - TW) + j, g * P:(g + 1) * P] for j in range(2) for g in range(CG)]
                    elif q < TP:
                        src = [pk[:, 2 * (q - TS) + j, 2 * CKV + g * P:2 * CKV + (g + 1) * P] for j in range(2) for g in range(CG)]
                    elif q == TP:
                        pe.wait_ge(pw_ready, b + 1)
                        src = [s[:, O_W + j * P:O_W + (j + 1) * P] for j in range(4)]
                    elif q < TP + 5:
                        if q == TP + 1:
                            pe.wait_ge(ps_ready, b + 1)
                        o = O_S + (q - TP - 1) * 4 * P
                        src = [s[:, o + j * P:o + (j + 1) * P] for j in range(4)]
                    else:
                        settle(pe, k)
                        for j, o in enumerate((O_SN, O_WN)):
                            ins = pe.transpose(xb[q % 2][0:NQ, j * P:(j + 1) * P], s[:, o:o + NQ], k.ident[:, :])
                        ins.then_inc(turned, 1)
                        return
                    for j in range(4):
                        ins = pe.transpose(xb[q % 2][:, j * P:(j + 1) * P], src[j], k.ident[:, :])
                    ins.then_inc(turned, 1)

                def score(b, n):
                    q = TW + n
                    fill = n // 2
                    pe.wait_ge((evac_a, evac_d)[q % 2], b * (NT // 2) + (q // 2 + 1))
                    if n % 2 == 0:
                        if fill >= 2:
                            pe.wait_ge(s_evac, b * 5 + (fill - 1))
                        else:
                            wait(pe, s_evac, b * 5)
                    for j in range(2):
                        o = (n % 2) * 2 * P + j * P
                        for g in range(CG):
                            ins = pe.matmul(sb_[fill % 2][:, o:o + P], qc[:, g, :], ktt[:, q % 2, 2 * j + g, :], start=(g == 0), stop=(g == CG - 1))
                    ins.then_inc(score_q, 1)

                def values(b, n):
                    q = TP + n
                    pe.wait_ge((evac_a, evac_d)[q % 2], b * (NT // 2) + (q // 2 + 1))
                    if 1 <= n <= 4:
                        pe.wait_ge(pv_in[n - 1], b * 64 + 64)
                    if n == 5:
                        pe.wait_ge(vn_in, b * 32 + 32)
                    for j in range(4 if n < 5 else 2):
                        if n == 0:
                            w, v = ptt[:, q % 2, j, :], win[:, j, CKV:2 * CKV]
                        elif n < 5:
                            w, v = ptt[:, q % 2, j, :], pv[:, (n - 1) * 4 + j, :]
                        else:
                            w, v = ptt[0:NQ, q % 2, j, :], vn[:, j, :]
                        ins = pe.matmul(ob[:, CKV:2 * CKV], w, v, start=(n == 0 and j == 0), stop=(n == 5 and j == 1))
                    ins.then_inc(pv_q, 1)

                def one(b):
                    for q in range(TW):
                        turn(b, q)
                    for i in range(2):
                        if i == 0:
                            pe.wait_ge(evac_a, b * (NT // 2) + TW // 2)
                            pe.wait_ge(evac_d, b * (NT // 2) + TW // 2)
                            wait(pe, o_ready, b * 1)
                        for l in range(CB):
                            ins = pe.matmul((hb, m2)[i][:, 0:CG * NCS], cmp.w1[:, i, l, :],
                                            xt[:, 2 * i:2 * i + 2, l:l + CS * (NCS - 1) + 1:CS], start=(l == 0), stop=(l == CB - 1))
                        ins.then_inc(h_done, 1)
                    turn(b, TW)
                    turn(b, TW + 1)
                    pe.wait_ge(qc_ready, b * 2 + 2)
                    wait(pe, imp_seen, b * 1)
                    for i, o in ((1, 0), (0, NQ)):
                        for g in range(CG):
                            ins = pe.matmul(mb[:, o:o + NQ], qc[:, g, :], kn[:, i, g, bass.ds(b * NQ, NQ)], start=(g == 0), stop=(g == CG - 1))
                    ins.then_inc(new_done, 1)
                    for n in range(10):
                        score(b, n)
                        if n == 3:
                            pe.wait_ge(hh_ready, b * 2 + 2)
                            pe.matmul(hb[:, 0:CG * NCS], cmp.w2[:, 0, :], hh[:, 0, :], start=True, stop=True)
                            for g in range(CG):
                                ins = pe.matmul(hb[0:NCS, CG * NCS + g * HD:CG * NCS + (g + 1) * HD], hh[:, 1, g * NCS:(g + 1) * NCS], cmp.w2[:, 1, :], start=True, stop=True)
                            ins.then_inc(w2_done, 1)
                        if n == 5:
                            pe.wait_ge(kc_ready, b * 2 + 2)
                            for g in range(CG):
                                ins = pe.matmul(mb[:, MC:MC + NCS], qc[:, g, :], kc[:, g * NCS:(g + 1) * NCS], start=(g == 0), stop=(g == CG - 1))
                            ins.then_inc(cs_done, 1)
                        if n + 2 < 10:
                            turn(b, TW + n + 2)
                    pe.wait_ge(pc_ready, b + 1)
                    settle(pe, k)
                    pe.transpose(m2[0:NCS, 0:P], s[:, O_C:], k.ident[:, :]).then_inc(pct_done, 1)
                    turn(b, TP)
                    pe.wait_ge(pct_ready, b + 1)
                    pe.matmul(mb[:, MT1:MT1 + NSEL], pct[:, :], ov[:, :], start=True, stop=True).then_inc(t1_done, 1)
                    wait(pe, o_evac, b * 2)
                    pe.matmul(ob[:, 0:CKV], pct[:, :], vc[:, :], start=True, stop=True)
                    pe.wait_ge(t1_ready, b + 1)
                    pe.matmul(mb[:, MIMP:MIMP + NSEL], hs[:, :], t1[:, :], start=True, stop=True).then_inc(imp_done, 1)
                    values(b, 0)
                    turn(b, TP + 1)
                    for n in range(1, 6):
                        if n < 5:
                            turn(b, TP + n + 1)
                        values(b, n)
                    pe.wait_ge(o_evac, b * 2 + 2)
                    settle(pe, k)
                    pe.transpose(m2[:, 0:P], orow[:, :], k.ident[:, :]).then_inc(o_turned, 1)

                one(0)
                with pe.Fori(1, NB) as b:
                    one(b)

            @block.vector
            def _(dve):
                cmp.dve(dve, hb)
                dve.wait_ge(small_in, 128)
                dve.tensor_scalar(qs[:, :, :], qs[:, :, :], SCALE, None, ALU.mult).then_inc(scaled, 1)
                dve.wait_ge(zeroed, 2)
                dve.wait_ge(bias_in, 16 * 32)
                dve.wait_ge(gt_in, 16 * 6)

                def one(b):
                    link = Chain(dve, chain, b * CHAIN)

                    def ev(q):
                        evac(dve, b, q, dve.tensor_copy, evac_d)

                    def hidden(i):
                        dve.wait_ge(h_exp, b * 2 + (i + 1))
                        wait(dve, w2_done, b * 1)
                        link(dve.tensor_scalar(he[:, :], he[:, :], 1.0, None, ALU.add))
                        link(dve.reciprocal(he[:, :], he[:, :]))
                        dve.scalar_tensor_tensor(hh[:, i, :], (hb, m2)[i][:, 0:CG * NCS], cmp.bias[:, i:i + 1], he[:, :],
                                                 ALU.add, ALU.mult).then_inc(hh_ready, 1)

                    def fill(f):
                        dve.wait_ge(score_q, b * 10 + (2 * f + 2))
                        o = O_W if f == 0 else O_S + (f - 1) * 4 * P
                        dve.tensor_tensor(s[:, o:o + 4 * P], sb_[f % 2][:, :], bias[:, o:o + 4 * P], ALU.add).then_inc(s_evac, 1)

                    for q in range(1, TW, 2):
                        ev(q)
                    hidden(0)
                    ev(17)
                    hidden(1)
                    fill(0)
                    dve.wait_ge(new_done, b + 1)
                    link(dve.tensor_tensor(s[:, O_WN:O_WN + NQ], mb[:, 0:NQ], bias[:, O_WN:O_WN + NQ], ALU.add))
                    link(dve.tensor_tensor(s[:, O_SN:O_SN + NQ], mb[:, NQ:2 * NQ], bias[:, O_SN:O_SN + NQ], ALU.add))
                    ev(19)
                    fill(1)
                    dve.wait_ge(w2_done, b + 1)
                    dve.tensor_copy(kc[:, :], hb[:, 0:CG * NCS]).then_inc(kc_ready, 1)
                    dve.tensor_copy(vc[:, :], hb[0:NCS, CG * NCS:CG * NCS + CKV]).then_inc(kc_ready, 1)
                    ev(21)
                    dve.wait_ge(s_evac, b * 5 + 1)
                    link(dve.tensor_reduce(st[:, 1, 0:1], s[:, O_W:O_S], AX, ALU.max))
                    dve.tensor_scalar(st[:, 1, 1:2], st[:, 1, 0:1], -1.0, None, ALU.mult).then_inc(max_w, 1)
                    fill(2)
                    dve.wait_ge(cs_done, b + 1)
                    link(dve.tensor_reduce(st[:, 0, 0:1], mb[:, MC:MC + NCS], AX, ALU.max))
                    dve.tensor_scalar(st[:, 0, 1:2], st[:, 0, 0:1], -1.0, None, ALU.mult).then_inc(max_c, 1)
                    ev(23)
                    fill(3)
                    dve.wait_ge(exp_c, b + 1)
                    link(dve.reciprocal(st[:, 0, 3:4], st[:, 0, 2:3]))
                    dve.tensor_scalar(s[:, O_C:], s[:, O_C:], st[:, 0, 3:4], None, ALU.mult).then_inc(pc_ready, 1)
                    ev(25)
                    fill(4)
                    dve.wait_ge(exp_w, b + 1)
                    link(dve.reciprocal(st[:, 1, 3:4], st[:, 1, 2:3]))
                    dve.tensor_scalar(s[:, O_W:O_S], s[:, O_W:O_S], st[:, 1, 3:4], gt[:, 2, bass.ds(b, 1)],
                                      ALU.mult, ALU.mult).then_inc(pw_ready, 1)
                    dve.wait_ge(pct_done, b + 1)
                    dve.tensor_copy(pct[:, :], m2[0:NCS, 0:P]).then_inc(pct_ready, 1)
                    dve.wait_ge(t1_done, b + 1)
                    dve.tensor_copy(t1[:, :], mb[:, MT1:MT1 + NSEL]).then_inc(t1_ready, 1)
                    dve.wait_ge(imp_done, b + 1)
                    dve.tensor_copy(rank[:, 0, 1:NSEL - 2], mb[:, MIMP + 1:MIMP + NSEL - 2]).then_inc(imp_seen, 1)
                    dve.wait_ge(imp_seen, b + 1)
                    for i in range(2):
                        settle(dve, k)
                        link(dve.max(m8[:, i, :], rank[:, i, :]))
                        settle(dve, k)
                        link(dve.match_replace(rank[:, i + 1, :], m8[:, i, :], rank[:, i, :], -1.0))
                    link(dve.tensor_scalar(rank[:, 2, :], rank[:, 2, :], 0.0, MASK, ALU.is_ge, ALU.mult))
                    link(dve.tensor_reduce(st[:, 2, 0:1], s[:, O_SN:O_SN + NQ], AX, ALU.max))
                    dve.wait_ge(s_evac, b * 5 + 5)
                    settle(dve, k)
                    sv = s[:, O_S:O_S + PAST].rearrange("p (n c) -> p n c", c=SELB)
                    link(dve.tensor_tensor_reduce(sv, sv, rank[:, 2, 0:NSEL - 1].unsqueeze(2).broadcast_to([P, NSEL - 1, SELB]), 1.0,
                                                  st[:, 2, 0:1], ALU.add, ALU.max, st[:, 2, 1:2]))
                    link(dve.tensor_scalar(st[:, 2, 1:2], st[:, 2, 1:2], -1.0, None, ALU.mult))
                    dve.sem_inc(max_s, 1)
                    dve.wait_ge(exp_s, b + 1)
                    link(dve.reciprocal(st[:, 2, 3:4], st[:, 2, 2:3]))
                    dve.tensor_scalar(s[:, O_S:O_C], s[:, O_S:O_C], st[:, 2, 3:4], gt[:, 1, bass.ds(b, 1)],
                                      ALU.mult, ALU.mult).then_inc(ps_ready, 1)
                    for q in (27, 29, 31):
                        ev(q)
                    dve.wait_ge(pv_q, b * 6 + 6)
                    for g in range(CG):
                        rows = slice(g * 64, (g + 1) * 64)
                        link(dve.tensor_scalar(oc[rows, :], ob[rows, g * HD:(g + 1) * HD], gt[rows, 0, bass.ds(b, 1)], None, ALU.mult))
                        dve.tensor_tensor(orow[rows, :], ob[rows, CKV + g * HD:CKV + (g + 1) * HD], oc[rows, :], ALU.add).then_inc(o_evac, 1)
                    dve.wait_ge(o_turned, b + 1)
                    dve.tensor_copy(ot[:, :, bass.ds(b * NQ, NQ)].rearrange("p (g h) i -> p g h i", g=CG),
                                    m2[:, 0:P].rearrange("p (g i h) -> p g h i", g=CG, h=CHG)).then_inc(o_ready, 1)
                    assert link.n == CHAIN, link.n

                one(0)
                with dve.Fori(1, NB) as b:
                    one(b)


def block_prompt_c(nc, k):
    with k.scope():
        U = 2
        cmp = Compress(k, "p")
        xk = k.sb("xkp", [P, 4, NP])
        kk = k.sb("kkp", [P, 2, CG, NP])
        v = k.sb("vvp", [P, 2, 2, CKV])
        q = k.sb("qpc", [P, U, NP])
        tab = k.sb("tpc", [P, U, NP])
        cmask = k.sb("cmask", [P, 2, NCP])
        gr = k.sb("gpc", [P, 2, 3, CH])
        hh = k.sb("hhp", [P, 2, CG * NCP])
        he = k.sb("hep", [P, CG * NCP])
        kc = k.sb("kcp", [P, CG * NCP])
        vc = k.sb("vcp", [NCP, CKV])
        sc = k.sb("scp", [P, 2, 3, NP])
        pt = k.sb("ptpc", [P, 2, 5, P])
        st = k.sb("stpc", [P, 2, 4, 3])
        ot = k.sb("otpc", [P, U, NP])
        sps = [k.ps(f"spc{i}", [P, 1024]) for i in range(2)]
        tps = [k.ps(f"tpp{i}", [P, 512]) for i in range(2)]
        ops = [k.ps(f"opc{i}", [P, 512]) for i in range(2)]
        in_, kv_in, gates_in = k.sem("pc_in"), k.sem("pc_kv_in"), k.sem("pc_gates_in")
        h_done, h_exp, hh_ready, w2_done, kc_ready = (k.sem(n) for n in ("hp_done", "hp_exp", "hhp_ready", "w2p_done", "kcp_ready"))
        loaded = [k.sem(f"pc_loaded{u}") for u in range(U)]
        stored = [k.sem(f"pc_stored{u}") for u in range(U)]
        scaled, scored, max_done, exp_done, p_ready, chain, turned, pt_ready, pv_done, o_ready = (
            k.sem(n) for n in ("pc_scaled", "pc_scored", "pc_max", "pc_exp", "pc_p", "pc_chain", "pc_turned", "pc_pt", "pc_pv", "pc_o"))
        HG = CHG // U
        LINKS = 2 * U * 6

        def rounds():
            return [(g, g * HG) for g in range(CG)]

        with nc.Block() as block:
            @block.sync
            def _(sp):
                cmp.sync(sp)
                sp.dma_start(xk[:, :, :], k.z2[C_KC:C_KC + 2 * CKV, 0:NP].rearrange("(c p) t -> p c t", p=P)).then_inc(in_, 16)
                for i, c in enumerate((C_KS, C_KW)):
                    sp.dma_start(kk[:, i, :, :], k.z2[c:c + CKV, 0:NP].rearrange("(g d) t -> d g t", d=HD)).then_inc(kv_in, 16)
                for i, c in enumerate((3 * CKV, 5 * CKV)):
                    sp.dma_start(v[:, :, i, :], k.kv2[0:NP, c:c + CKV].rearrange("(t p) n -> p t n", p=P)).then_inc(kv_in, 16)
                sp.dma_start(cmask[:, :, :], k.c_cmask).then_inc(gates_in, 16)
                sp.dma_start(gr[:, :, :, :].rearrange("p t r h -> p t (r h)"), k.gates.rearrange("(t p) n -> p t n", p=P)).then_inc(gates_in, 16)
                for g, g0 in rounds():
                    with sp.Fori(g0, g0 + HG) as it:
                        for u in range(U):
                            sp.wait_ge(pv_done, it * (2 * U) + (2 * u + 2))
                            sp.dma_start(q[:, u, :], k.z2[bass.ds((it * U + u) * HD, HD), 0:NP]).then_inc(loaded[u], 16)
                            sp.dma_start(tab[:, u, :], k.toe_c[bass.ds(it * U + u, 1)].rearrange("a p n -> (a p) n")).then_inc(loaded[u], 16)

            @block.scalar
            def _(act):
                for u in range(U):
                    act.sem_inc(stored[u], 16)
                act.wait_ge(cmp.ready, 2)
                for i in range(2):
                    act.wait_ge(h_done, i + 1)
                    wait(act, hh_ready, i)
                    act.activation(he[:, :], (tps[1], sps[0])[i][:, 0:CG * NCP], ACT.Exp, bias=cmp.nbias[:, i:i + 1], scale=-1.0).then_inc(h_exp, 1)
                for g, g0 in rounds():
                    with act.Fori(g0, g0 + HG) as it:
                        for u in range(U):
                            for qb in range(2):
                                n = 2 * u + qb
                                nk = P * (qb + 1)
                                act.wait_ge(max_done, it * (2 * U) + (n + 3))
                                for r, w in enumerate((NCP, nk, nk)):
                                    act.activation(sc[:, qb, r, 0:w], sc[:, qb, r, 0:w], ACT.Exp, bias=st[:, qb, 1, r:r + 1],
                                                   accum_out=st[:, qb, 2, r:r + 1]).then_inc(exp_done, 1)
                            act.wait_ge(o_ready, it * (2 * U) + (2 * u + 4))
                            act.dma_start(k.mt[bass.ds((it * U + u) * HD, HD), 0:NP], ot[:, u, :]).then_inc(stored[u], 16)
                for u in range(U):
                    act.wait_ge(stored[u], 16 * (CH // U) + 16)

            @block.tensor
            def _(pe):
                pe.sem_inc(pv_done, 2 * U)
                cmp.pe(pe, tps[0])
                pe.wait_ge(in_, 16)
                for i in range(2):
                    for l in range(CB):
                        ins = pe.matmul((tps[1], sps[0])[i][:, 0:CG * NCP], cmp.w1[:, i, l, :],
                                        xk[:, 2 * i:2 * i + 2, l:l + CS * (NCP - 1) + 1:CS], start=(l == 0), stop=(l == CB - 1))
                    ins.then_inc(h_done, 1)
                pe.wait_ge(hh_ready, 2)
                pe.matmul(ops[0][:, 0:CG * NCP], cmp.w2[:, 0, :], hh[:, 0, :], start=True, stop=True)
                for g in range(CG):
                    ins = pe.matmul(ops[1][0:NCP, g * HD:(g + 1) * HD], hh[:, 1, g * NCP:(g + 1) * NCP], cmp.w2[:, 1, :], start=True, stop=True)
                ins.then_inc(w2_done, 1)
                pe.wait_ge(kc_ready, 2)
                pe.wait_ge(kv_in, 64)
                for g, g0 in rounds():
                    with pe.Fori(g0, g0 + HG) as it:
                        for u in range(U):
                            pe.wait_ge(scaled, it * U + (u + 1))
                            for qb in range(2):
                                n = 2 * u + qb
                                nk = P * (qb + 1)
                                qq = q[:, u, qb * P:(qb + 1) * P]
                                pe.wait_ge(max_done, it * (2 * U) + (n + 1))
                                pe.matmul(sps[qb][:, 0:NCP], qq, kc[:, g * NCP:(g + 1) * NCP], start=True, stop=True)
                                pe.matmul(sps[qb][:, 16:16 + nk], qq, kk[:, 0, g, 0:nk], start=True, stop=True)
                                pe.matmul(sps[qb][:, 512:512 + nk], qq, kk[:, 1, g, 0:nk], start=True, stop=True).then_inc(scored, 1)
                            for qb in range(2):
                                n = 2 * u + qb
                                pe.wait_ge(p_ready, it * (2 * U) + (n + 1))
                                settle(pe, k)
                                pe.transpose(tps[0][0:NCP, 0:P], sc[:, qb, 0, 0:NCP], k.ident[:, :])
                                for h in range(qb + 1):
                                    ins = pe.transpose(tps[0][:, (1 + h) * P:(2 + h) * P], sc[:, qb, 1, h * P:(h + 1) * P], k.ident[:, :])
                                ins.then_inc(turned, 1)
                                for h in range(qb + 1):
                                    ins = pe.transpose(tps[1][:, h * P:(h + 1) * P], sc[:, qb, 2, h * P:(h + 1) * P], k.ident[:, :])
                                ins.then_inc(turned, 1)
                                pe.wait_ge(pt_ready, it * (6 * U) + (6 * u + 3 * qb + 3))
                                pe.wait_ge(o_ready, it * (2 * U) + (n + 1))
                                pe.matmul(ops[qb][:, 0:P], vc[:, g * HD:(g + 1) * HD], pt[0:NCP, qb, 0, :], start=True, stop=False)
                                for r in range(2):
                                    for h in range(qb + 1):
                                        ins = pe.matmul(ops[qb][:, 0:P], v[:, h, r, g * HD:(g + 1) * HD], pt[:, qb, 1 + 2 * r + h, :],
                                                        start=False, stop=(r == 1 and h == qb))
                                ins.then_inc(pv_done, 1)

            @block.vector
            def _(dve):
                dve.sem_inc(max_done, 2)
                dve.sem_inc(o_ready, 2)
                cmp.dve(dve, tps[0])
                link = Chain(dve, chain)
                for i in range(2):
                    dve.wait_ge(h_exp, i + 1)
                    link(dve.tensor_scalar(he[:, :], he[:, :], 1.0, None, ALU.add))
                    link(dve.reciprocal(he[:, :], he[:, :]))
                    dve.scalar_tensor_tensor(hh[:, i, :], (tps[1], sps[0])[i][:, 0:CG * NCP], cmp.bias[:, i:i + 1], he[:, :],
                                             ALU.add, ALU.mult).then_inc(hh_ready, 1)
                dve.wait_ge(w2_done, 1)
                dve.tensor_copy(kc[:, :], ops[0][:, 0:CG * NCP]).then_inc(kc_ready, 1)
                dve.tensor_copy(vc[:, :], ops[1][0:NCP, 0:CKV]).then_inc(kc_ready, 1)
                dve.wait_ge(gates_in, 32)
                for g, g0 in rounds():
                    with dve.Fori(g0, g0 + HG) as it:
                        link = Chain(dve, chain, it * LINKS + 4)
                        for u in range(U):
                            dve.wait_ge(loaded[u], it * 32 + 32)
                            dve.tensor_scalar(q[:, u, :], q[:, u, :], SCALE, None, ALU.mult).then_inc(scaled, 1)
                            for qb in range(2):
                                n = 2 * u + qb
                                nk = P * (qb + 1)
                                dve.wait_ge(scored, it * (2 * U) + (n + 1))
                                settle(dve, k)
                                link(dve.tensor_tensor_reduce(sc[:, qb, 0, 0:NCP], sps[qb][:, 0:NCP], cmask[:, qb, :], 1.0, MASK / 10,
                                                              ALU.add, ALU.max, st[:, qb, 0, 0:1]))
                                for r, o in ((1, 16), (2, 512)):
                                    settle(dve, k)
                                    link(dve.tensor_tensor_reduce(sc[:, qb, r, 0:nk], sps[qb][:, o:o + nk], tab[:, u, NP - nk:NP], 1.0, -3.0e38,
                                                                  ALU.add, ALU.max, st[:, qb, 0, r:r + 1]))
                                dve.tensor_scalar(st[:, qb, 1, :], st[:, qb, 0, :], -1.0, None, ALU.mult).then_inc(max_done, 1)
                            for qb in range(2):
                                n = 2 * u + qb
                                nk = P * (qb + 1)
                                dve.wait_ge(exp_done, it * (6 * U) + (3 * n + 3))
                                link(dve.tensor_scalar(st[:, qb, 2, :], st[:, qb, 2, :], 1.0e-30, None, ALU.max))
                                link(dve.reciprocal(st[:, qb, 3, :], st[:, qb, 2, :]))
                                link(dve.tensor_tensor(st[:, qb, 3, :], st[:, qb, 3, :],
                                                       gr[:, qb, :, bass.ds(it * U + u, 1)].rearrange("p r a -> p (r a)"), ALU.mult))
                                for r, w in enumerate((NCP, nk, nk)):
                                    ins = dve.tensor_scalar(sc[:, qb, r, 0:w], sc[:, qb, r, 0:w], st[:, qb, 3, r:r + 1], None, ALU.mult)
                                ins.then_inc(p_ready, 1)
                            for qb in range(2):
                                dve.wait_ge(turned, it * (4 * U) + (4 * u + 2 * qb + 1))
                                dve.tensor_copy(pt[0:NCP, qb, 0, :], tps[0][0:NCP, 0:P]).then_inc(pt_ready, 1)
                                dve.tensor_copy(pt[:, qb, 1:2 + qb, :], tps[0][:, P:(2 + qb) * P].rearrange("p (c n) -> p c n", n=P)).then_inc(pt_ready, 1)
                                dve.wait_ge(turned, it * (4 * U) + (4 * u + 2 * qb + 2))
                                dve.tensor_copy(pt[:, qb, 3:4 + qb, :], tps[1][:, 0:(1 + qb) * P].rearrange("p (c n) -> p c n", n=P)).then_inc(pt_ready, 1)
                            for qb in range(2):
                                n = 2 * u + qb
                                dve.wait_ge(pv_done, it * (2 * U) + (2 * U + n + 1))
                                dve.wait_ge(stored[u], it * 16 + 16)
                                dve.tensor_copy(ot[:, u, qb * P:(qb + 1) * P], ops[qb][:, 0:P]).then_inc(o_ready, 1)
                        assert link.n == LINKS


def block_cache_rows(nc, k):
    with k.scope():
        done = k.sem("cache_rows_done")
        with nc.Block() as block:
            @block.sync
            def _(sp):
                n = 0
                for g, (w, _) in enumerate(GROUPS):
                    keep = min(w, NP)
                    for kv in range(2):
                        c = kv * QKV + g * NH * HD
                        sp.dma_start(k.out_a_p[g][:, kv, :, :].rearrange("t h d -> t (h d)"), k.kv[NP - keep:NP, c:c + NH * HD]).then_inc(done, 16)
                        for b in range(NB):
                            sp.dma_start(k.out_a_s[g][b, w - NQ:w, kv, :, :].rearrange("t h d -> t (h d)"),
                                         k.kv[NP + b * NQ:NP + (b + 1) * NQ, c:c + NH * HD]).then_inc(done, 16)
                        n += 1 + NB
                sp.wait_ge(done, 16 * n)


PHASES = (block_even_in, block_sample_a, block_prompt_a, block_cache_rows, block_conv, block_even_out_odd_in, block_sample_c, block_prompt_c, block_final,)


class Kit:

    def __init__(self, nc):
        self.nc = nc
        self.stacks = [ExitStack()]
        self.sems = []
        self.phase = 0

    def sem(self, name):
        self.sems.append(self.nc.alloc_semaphore(name))
        return self.sems[-1]

    def sb(self, name, shape, dt=F32):
        return self.stacks[-1].enter_context(self.nc.sbuf_tensor(name, shape, dt))

    def ps(self, name, shape):
        return self.stacks[-1].enter_context(self.nc.psum_tensor(name, shape, F32))

    def scope(self):
        return Scope(self)


class Scope:

    def __init__(self, kit):
        self.kit = kit

    def __enter__(self):
        self.kit.stacks.append(ExitStack())
        self.kit.phase += 1
        self.kit.settled = self.kit.sem(f"settled{self.kit.phase}")

    def __exit__(self, *exc):
        self.kit.stacks.pop().close()
        self.kit.nc.clear_and_free_semaphores(self.kit.sems)
        self.kit.sems = []
        self.kit.nc.all_engine_barrier()


def build(nc, ins, outs):
    def scratch(name, *shape):
        return nc.dram_tensor(name, list(shape), F32, kind="Internal").ap()

    k = Kit(nc)
    k.x_prompt = ins["x_prompt"][0]
    k.norm_even = ins["norm_even"][0]
    k.w_in_even = ins["w_in_even"][0]
    k.conv_w = ins["conv_w"][0]
    k.conv_b = ins["conv_b"][0]
    k.conv_ln_g = ins["conv_ln_g"][0]
    k.conv_ln_b = ins["conv_ln_b"][0]
    k.conv_pw_w = ins["conv_pw_w"][0]
    k.conv_pw_b = ins["conv_pw_b"][0]
    k.w_out_even = ins["w_out_even"][0]
    k.norm_odd = ins["norm_odd"][0]
    k.w_in_odd = ins["w_in_odd"][0]
    k.cmp_w1 = ins["cmp_w1"][0]
    k.cmp_w2 = ins["cmp_w2"][0]
    k.w_out_odd = ins["w_out_odd"][0]
    k.state_b_conv = ins["state_b_conv"][0]
    k.cache_c_kv = ins["cache_c_kv"][0]
    k.cache_c_win = ins["cache_c_win"][0]
    k.cmp_pos = ins["cmp_pos"]
    k.cmp_b1 = ins["cmp_b1"]
    k.final_norm = ins["final_norm"]
    k.rel_bias = ins["rel_bias"]
    k.page_table = ins["page_table"]
    k.c_ident = ins["c_ident"]
    k.c_onehot = ins["c_onehot"]
    k.c_overlap = ins["c_overlap"]
    k.c_hsum = ins["c_hsum"]
    k.c_cmask = ins["c_cmask"]
    k.x_sample = ins["x_sample"].rearrange("b t d -> (b t) d")
    k.cache_a = [ins[f"cache_a_kv{g}"][0] for g in range(NG)]
    k.out_y_p, k.out_y_s = outs[0][0], outs[1].rearrange("b t d -> (b t) d")
    k.out_a_p = [outs[2 + g][0, 0] for g in range(NG)]
    k.out_conv_p, k.out_rows_p, k.out_win_p = outs[5][0, 0], outs[6][0, 0], outs[7][0, 0]
    k.out_a_s = [outs[8 + g][0] for g in range(NG)]
    k.out_conv_s, k.out_rows_s, k.out_win_s = outs[11][0], outs[12][0], outs[13][0]
    k.zt = scratch("zt", EVEN_IN, T)
    k.kv = scratch("kv", T, 2 * QKV)
    k.xt = scratch("xt", D, T)
    k.mt = scratch("mt", D, T)
    k.z2 = scratch("z2", Z2_GP + CW, T)
    k.kv2 = scratch("kv2", T, 6 * CKV)
    k.gates = scratch("gates", NP, 3 * CH)
    k.gates_s = scratch("gates_s", 3 * CH, NQ, NB)
    k.tab_a = scratch("tab_a", NG, NH, FW)
    k.tab_c = scratch("tab_c", CH, FW)
    k.tab_sa = scratch("tab_sa", NQ, NH, SA)
    k.tab_hc = scratch("tab_hc", CH, HC)
    k.tab_hw = scratch("tab_hw", CH, HWC)
    k.toe_a = scratch("toe_a", NG, NH, P, NP)
    k.toe_c = scratch("toe_c", CH, P, NP)
    with k.stacks[0]:
        k.ident = k.sb("ident", [P, P])
        k.ones = k.sb("ones", [P, P])
        k.eps = k.sb("eps", [P, 1])
        for phase in PHASES:
            phase(nc, k)


_NAMES = ['x_prompt', 'x_sample', 'cache_a_kv0', 'cache_a_kv1', 'cache_a_kv2', 'state_b_conv', 'cache_c_kv', 'cache_c_win',
          'page_table', 'rel_bias', 'norm_even', 'w_in_even', 'conv_w', 'conv_b', 'conv_ln_g', 'conv_ln_b', 'conv_pw_w',
          'conv_pw_b', 'w_out_even', 'norm_odd', 'w_in_odd', 'cmp_pos', 'cmp_w1', 'cmp_b1', 'cmp_w2', 'w_out_odd', 'final_norm']
_OUTS = [(1, NP, D), (NB, NQ, D),
         (1, 1, 128, 2, 8, 128), (1, 1, NP, 2, 8, 128), (1, 1, NP, 2, 8, 128),
         (1, 1, 30, 1024), (1, 1, NP, 4, 2, 128), (1, 1, NP, 2, 2, 128),
         (1, NB, 128, 2, 8, 128), (1, NB, 512, 2, 8, 128), (1, NB, 2048, 2, 8, 128),
         (1, NB, 30, 1024), (1, NB, NQ, 4, 2, 128), (1, NB, 512, 2, 2, 128)]


def kernel(**inputs):
    import concourse.bacc as _bacc
    from concourse.bass_utils import run_bass_kernel_spmd as _run

    nc = _bacc.Bacc("TRN2", target_bir_lowering=False, num_devices=1)
    arrays, ins = {}, {}
    given = {name: np.ascontiguousarray(inputs[name]) for name in _NAMES}
    given.update(host_constants())
    for name in ("norm_even", "conv_b", "conv_ln_g", "conv_ln_b", "conv_pw_b", "norm_odd", "final_norm"):
        a = given[name]
        given[name] = np.ascontiguousarray(a.reshape(*a.shape[:-1], -1, P).swapaxes(-1, -2))
    given["conv_w"] = np.ascontiguousarray(given["conv_w"].reshape(1, TAPS, -1, P).transpose(0, 3, 2, 1))
    for name in ("cmp_pos", "cmp_b1"):
        a = given[name]
        given[name] = np.ascontiguousarray(np.moveaxis(a.reshape(2, -1, HD), 2, 0))
    for name, a in given.items():
        arrays[f"in_{name}"] = a
        ins[name] = nc.dram_tensor(f"in_{name}", a.shape, mybir.dt.from_np(a.dtype), kind="ExternalInput").ap()
    outs = [nc.dram_tensor(f"out_{i}", shape, F32, kind="ExternalOutput").ap() for i, shape in enumerate(_OUTS)]
    build(nc, ins, outs)
    r = _run(nc, [arrays], core_ids=[0])
    return tuple(r.results[0][f"out_{i}"] for i in range(len(_OUTS)))
```

```python
import math
from contextlib import ExitStack

import numpy as np

import concourse.bass as bass
from concourse import mybir

F32 = mybir.dt.float32
F32R = mybir.dt.float32r
I32 = mybir.dt.int32
ALU = mybir.AluOpType
ACT = mybir.ActivationFunctionType
AX = mybir.AxisListType.X

P = 128
D = 2048
NP = 256
NB, NQ = 8, 8
NS = NB * NQ
T = NP + NS
PAST = 2048
PAGE = 128
NPG = PAST // PAGE
HD = 128
SCALE = HD ** -0.5
EPS = 1e-6
MASK = -1.0e30
GROUPS = ((128, 1), (512, 4), (2048, 16))
NG, NH = 3, 8
QKV = NG * NH * HD
WB = 1024
TAPS = 31
EVEN_IN = 3 * QKV + NH * HD + 3 * WB
CH, CG = 16, 2
CHG = CH // CG
CW = CH * HD
CKV = CG * HD
CB, CS = 32, 16
NCS = PAST // CS - 1
NCP = NP // CS - 1
SELB = 64
NSEL = -(-(PAST + NQ) // SELB)
WIN = 512
NBUCK, MAXD = 32, 2048
KT = D // P
GW = 512
Z_GA, Z_A, Z_GT, Z_GB = 3 * QKV, 3 * QKV + 1024, 3 * QKV + 2048, 3 * QKV + 3072
C_KC, C_VC, C_KS, C_VS, C_KW, C_VW = (CW + i * CKV for i in range(6))
C_GL = CW + 6 * CKV
C_GP = C_GL + 3 * CH
ODD_IN = C_GP + CW
Z2_GP = C_GL
FW = 384
SA = NG * P + NG * NQ
HC = PAST + NQ + NQ - 1
HWC = WIN + NQ + NQ - 1


def host_constants():
    def onehot(dist, ok):
        d = np.maximum(dist, 0)
        ratio = np.log(np.maximum(d, 1).astype(np.float32) / np.float32(NBUCK // 2)) / np.float32(math.log(MAXD / (NBUCK // 2)))
        large = np.minimum(NBUCK // 2 + (ratio * np.float32(NBUCK // 2)).astype(np.int32), NBUCK - 1)
        b = np.where(d < NBUCK // 2, d, large)
        out = np.zeros((NBUCK + 1, dist.size), np.float32)
        n = np.arange(dist.size)
        out[b[ok], n[ok]] = 1.0
        out[NBUCK, ~ok] = MASK
        return out

    c = np.arange(FW)
    dist = 255 - c
    parts = [onehot(dist, (dist >= 0) & (dist <= w) & (dist % dil == 0)) for w, dil in GROUPS]
    parts.append(onehot(dist, dist >= 0))
    for i in range(NQ):
        j = np.arange(P)
        m = np.arange(NQ)
        for w, dil in GROUPS:
            dd = w + i - (dil * j + i % dil)
            parts.append(onehot(dd, (dd >= 0) & (dd <= w)))
        for w, dil in GROUPS:
            dd = i - m
            parts.append(onehot(dd, (dd >= 0) & (dd % dil == 0)))
    c = np.arange(HC)
    parts.append(onehot(PAST + NQ - 1 - c, PAST + NQ - 1 - c >= 0))
    c = np.arange(HWC)
    dd = WIN + NQ - 1 - c
    parts.append(onehot(dd, (dd >= 0) & (dd <= WIN)))
    ci, si = np.arange(NCS)[:, None], np.arange(NSEL)[None, :]
    overlap = ((ci * CS < (si + 1) * SELB) & (ci * CS + CB > si * SELB)).astype(np.float32)
    r = np.arange(P)
    hsum = (r[:, None] // CHG == r[None, :] // CHG).astype(np.float32)
    q = np.arange(NP).reshape(2, P)
    n = np.arange(NCP)
    cmask = np.where(n[None, None] * CS + CB - 1 <= q.T[:, :, None], 0.0, MASK).astype(np.float32)
    return {
        "c_ident": np.eye(P, dtype=np.float32),
        "c_onehot": np.concatenate(parts, axis=1),
        "c_overlap": overlap,
        "c_hsum": hsum,
        "c_cmask": np.ascontiguousarray(cmask),
    }


def ap_of(view, offset, dims):
    return bass.AP(tensor=view.tensor, offset=view.offset + offset, ap=[list(view.ap[0])] + [list(d) for d in dims])


def dram_ap(view, offset, dims):
    return bass.AP(tensor=view.tensor, offset=view.offset + offset, ap=[list(d) for d in dims])


class Chain:

    def __init__(self, eng, sem, base=0):
        self.eng, self.sem, self.base, self.n = eng, sem, base, 0

    def __call__(self, ins):
        self.n += 1
        ins.then_inc(self.sem, 1)
        self.eng.wait_ge(self.sem, self.base + self.n)


def wait(eng, sem, value):
    if not isinstance(value, int) or value > 0:
        eng.wait_ge(sem, value)


def settle(eng, k):
    eng.sem_inc(k.settled, 1)


def cache_pieces(k):
    pieces = []
    row = 2 * NH * HD
    for g, parts in ((2, 4), (0, 1)):
        keep = (GROUPS[g][0] - NQ) // parts
        m = 816 if g == 2 else keep * 2
        for b in range(NB):
            src = k.cache_a[g][b].rearrange("t a h d -> (t a h d)")
            dst = k.out_a_s[g][b].rearrange("t a h d -> (t a h d)")
            for i in range(max(parts - 1, 1)):
                lo = i * keep * row
                pieces.append((dst[lo:lo + keep * row].rearrange("(m n) -> m n", m=m),
                               src[lo + NQ * row:lo + (NQ + keep) * row].rearrange("(m n) -> m n", m=m)))
    return pieces




class Norm:

    def __init__(self, k, tag, xT, xn, gcol, ps, hi=None, lo=None):
        self.k, self.xT, self.xn, self.gcol, self.ps, self.hi, self.lo = k, xT, xn, gcol, ps, hi, lo
        self.sq = k.sb("sq" + tag, [P, 4, T])
        self.rs = k.sb("rs" + tag, [P, T])
        self.sq_ready, self.sq_used, self.sum_done, self.root_done, self.chain, self.full, self.hi_made, self.ready = (
            k.sem(n + tag) for n in ("sq_ready", "sq_used", "sum_done", "root_done", "norm_chain", "xn_full", "xn_hi", "xn_ready"))

    def dve(self, dve, x_wait, free=None):
        k = self.k
        for t in range(KT):
            x_wait(dve, t)
            if t >= 4:
                dve.wait_ge(self.sq_used, t - 3)
            dve.tensor_tensor(self.sq[:, t % 4, :], self.xT[:, t, :], self.xT[:, t, :], ALU.mult).then_inc(self.sq_ready, 1)
        dve.wait_ge(self.root_done, 1)
        link = Chain(dve, self.chain)
        link(dve.reciprocal(self.rs[:, :], self.rs[:, :]))
        if free:
            free(dve)

        def lo(t):
            dve.wait_ge(self.hi_made, t + 1)
            dve.tensor_tensor(self.lo[:, t, :], self.xn[:, t, :], self.hi[:, t, :], ALU.subtract).then_inc(self.ready, 1)

        for t in range(KT):
            dve.scalar_tensor_tensor(self.xn[:, t, :], self.xT[:, t, :], self.gcol[:, t:t + 1], self.rs[:, :],
                                     ALU.mult, ALU.mult).then_inc(self.full if self.hi is not None else self.ready, 1)
            if self.hi is not None and t >= 2:
                lo(t - 2)
        if self.hi is not None:
            lo(KT - 2)
            lo(KT - 1)

    def pe(self, pe):
        for t in range(KT):
            pe.wait_ge(self.sq_ready, t + 1)
            pe.matmul(self.ps[:, 0:T], self.k.ones[:, :], self.sq[:, t % 4, :], start=(t == 0), stop=(t == KT - 1)
                      ).then_inc(self.sq_used, 1)

    def act(self, act):
        act.wait_ge(self.sq_used, KT)
        act.activation(self.rs[:, :], self.ps[:, 0:T], ACT.Sqrt, bias=self.k.eps[:, :], scale=1.0 / D).then_inc(self.root_done, 1)
        if self.hi is not None:
            for t in range(KT):
                act.wait_ge(self.full, t + 1)
                act.copy(self.hi[:, t, :], self.xn[:, t, :]).then_inc(self.hi_made, 1)


class Proj:

    def __init__(self, k, tag, w, rhs_hi, rhs_lo, banks, segs, zt=None, rows=None, row_banks=None, residual=None, after=None):
        self.k, self.banks, self.segs, self.zt, self.after = k, banks, segs, zt, after
        self.xh, self.xl = rhs_hi, rhs_lo
        self.w = w.rearrange("(k p) n -> p k n", p=P)
        self.nq, self.kq = 4, KT // 4
        self.rows, self.row_banks, self.residual = rows, row_banks, residual
        if after is None:
            self.wt, self.lo = k.sb_and_lo("w" + tag, [P, self.nq, self.kq, GW])
            self.hi = k.sb("w_hi" + tag, [P, 2, self.kq, GW], F32R)
        else:
            self.wt, self.hi, self.lo = after.wt, after.hi, after.lo
        self.n_groups = sum(s[0] for s in segs)
        self.loaded = [k.sem(f"w_loaded{q}" + tag) for q in range(self.nq)]
        self.freed = [k.sem(f"w_freed{q}" + tag) for q in range(self.nq - 1)]
        self.tile_done, self.z_ready, self.z_stored, self.hi_ready, self.hi_used, self.lo_ready = (
            k.sem(n + tag) for n in ("tile_done", "z_ready", "z_stored", "w_hi_ready", "w_hi_used", "w_lo_ready"))
        if residual is None:
            self.z = k.sb("z" + tag, [P, 4, T])
        if rows is not None:
            self.rsb = k.sb("rows" + tag, [P, 3, GW])
            self.rows_done, self.rows_evac, self.rows_stored = (k.sem(n + tag) for n in ("rows_done", "rows_evac", "rows_stored"))

    def segments(self):
        g = r = 0
        for i, (n, src, dst, rc) in enumerate(self.segs):
            yield i, n, src, dst, rc, g, r
            g += n
            r += n * (rc is not None)

    def sync(self, sp):
        if self.after is not None:
            sp.wait_ge(self.after.tile_done, 4 * self.after.n_groups + 4)
        for _, n, src, dst, rc, g0, r0 in self.segments():
            with sp.Fori(0, n) as it:
                for q in range(self.nq):
                    if q < self.nq - 1:
                        sp.wait_ge(self.freed[q], it + (g0 + 1))
                    else:
                        sp.wait_ge(self.tile_done, it * 4 + (4 * g0 + 4))
                    sp.dma_start(self.wt[:, q, :, :], self.w[:, q * self.kq:(q + 1) * self.kq, bass.ds(it * GW + src, GW)]
                                 ).then_inc(self.loaded[q], 16)

    def pe(self, pe, quarter_wait=None, before=None):
        for q in range(self.nq - 1):
            pe.sem_inc(self.freed[q], 1)
        pe.sem_inc(self.tile_done, 4)
        pe.sem_inc(self.hi_used, 2)
        for i, n, src, dst, rc, g0, r0 in self.segments():
            if before and i in before:
                before[i](pe)
            with pe.Fori(0, n) as it:
                for q in range(self.nq):
                    if quarter_wait:
                        quarter_wait(pe, q)
                    pe.wait_ge(self.hi_ready, it * 4 + (4 * g0 + q + 1))
                    for c in range(4):
                        if q == 0:
                            pe.wait_ge(self.z_ready, it * 4 + (4 * g0 + c + 1))
                        for j in range(self.kq):
                            for m, x in enumerate((self.xh, self.xl)):
                                ins = pe.matmul(self.banks[c][:, 0:T], self.hi[:, q % 2, j, c * P:(c + 1) * P],
                                                x[:, q * self.kq + j, :], start=(q == 0 and j == 0 and m == 0), stop=False)
                    ins.then_inc(self.hi_used, 1)
                    pe.wait_ge(self.lo_ready, it * 4 + (4 * g0 + q + 3))
                    for c in range(4):
                        for j in range(self.kq):
                            ins = pe.matmul(self.banks[c][:, 0:T], self.lo[:, q, j, c * P:(c + 1) * P],
                                            self.xh[:, q * self.kq + j, :], start=False, stop=(q == self.nq - 1 and j == self.kq - 1))
                        if q == self.nq - 1:
                            ins.then_inc(self.tile_done, 1)
                        elif c == 3:
                            ins.then_inc(self.freed[q], 1)
                if rc is not None:
                    pe.wait_ge(self.z_ready, it * 4 + (4 * g0 + 8))
                    pe.wait_ge(self.rows_evac, it * 3 + (3 * r0 + 3))
                    for t, m in enumerate((P, P, NS)):
                        for c in range(4):
                            ins = pe.transpose(self.row_banks[t][0:m, c * P:(c + 1) * P], self.z[:, c, t * P:t * P + m],
                                               self.k.ident[:, :])
                        ins.then_inc(self.rows_done, 1)

    def act(self, act, before=None):
        if self.residual is None:
            act.sem_inc(self.z_ready, 4)
            act.sem_inc(self.z_stored, 16)
        if self.rows is not None:
            act.sem_inc(self.rows_evac, 3)
            act.sem_inc(self.rows_stored, 32)

        def hi(it, g0, q):
            act.wait_ge(self.loaded[q % 4], it * 16 + (16 * (g0 + q // 4) + 16))
            act.wait_ge(self.hi_used, it * 4 + (4 * g0 + q + 1))
            act.wait_ge(self.lo_ready, it * 4 + (4 * g0 + q + 1))
            act.copy(self.hi[:, q % 2, :, :], self.wt[:, q % 4, :, :]).then_inc(self.hi_ready, 1)

        def group(it, seg, more):
            _, n, src, dst, rc, g0, r0 = seg
            for q in range(1, 5 if more else 4):
                hi(it, g0, q)
            if self.residual is not None:
                return
            act.wait_ge(self.z_stored, it * 16 + (16 * g0 + 16))
            for c in range(4):
                act.wait_ge(self.tile_done, it * 4 + (4 * g0 + 4 + c + 1))
                act.copy(self.z[:, c, :], self.banks[c][:, 0:T]).then_inc(self.z_ready, 1)
            act.wait_ge(self.z_ready, it * 4 + (4 * g0 + 8))
            act.dma_start(self.zt[bass.ds(it * GW + dst, GW), :].rearrange("(c p) t -> p c t", p=P), self.z[:, :, :]
                          ).then_inc(self.z_stored, 16)
            if rc is not None:
                act.wait_ge(self.rows_stored, it * 32 + (32 * r0 + 32))
                for t, m in enumerate((P, P, NS)):
                    act.wait_ge(self.rows_done, it * 3 + (3 * r0 + t + 1))
                    act.copy(self.rsb[0:m, t, :], self.row_banks[t][0:m, :]).then_inc(self.rows_evac, 1)
                act.wait_ge(self.rows_evac, it * 3 + (3 * r0 + 6))
                act.dma_start(self.rows[0:NP, bass.ds(it * GW + rc, GW)].rearrange("(t p) n -> p t n", p=P), self.rsb[:, 0:2, :]
                              ).then_inc(self.rows_stored, 16)
                act.dma_start(self.rows[NP:T, bass.ds(it * GW + rc, GW)], self.rsb[0:NS, 2, :]).then_inc(self.rows_stored, 16)

        hi(0, 0, 0)
        for seg in self.segments():
            i, n, last = seg[0], seg[1], seg[5] + seg[1] == self.n_groups
            if before and i in before:
                before[i](act)
            if n - last > 0:
                with act.Fori(0, n - last) as it:
                    group(it, seg, True)
            if last:
                group(n - 1, seg, False)

    def dve(self, dve, before=None, beside=None):
        if self.residual is not None:
            dve.sem_inc(self.z_ready, 4)
        dve.sem_inc(self.lo_ready, 2)
        for i, n, src, dst, rc, g0, r0 in self.segments():
            if before and i in before:
                before[i](dve)
            with dve.Fori(0, n) as it:
                for q in range(self.nq):
                    dve.wait_ge(self.hi_ready, it * 4 + (4 * g0 + q + 1))
                    dve.tensor_tensor(self.lo[:, q, :, :], self.wt[:, q, :, :], self.hi[:, q % 2, :, :], ALU.subtract).then_inc(self.lo_ready, 1)
                    if beside and i in beside:
                        beside[i](it * 4 + q)
                if self.residual is not None:
                    for c in range(4):
                        dve.wait_ge(self.tile_done, it * 4 + (4 * g0 + 4 + c + 1))
                        x = self.residual[:, bass.ds(it * 4 + (4 * g0 + c), 1), :]
                        dve.tensor_tensor(x, x, self.banks[c][:, 0:T].unsqueeze(1), ALU.add).then_inc(self.z_ready, 1)


def table_jobs(k):
    jobs, c = [], 0
    for g in range(NG):
        jobs.append(([(slice(g * NH, (g + 1) * NH), c, 0, FW)], NH, FW, k.tab_a[g]))
        c += FW
    jobs.append(([(slice(0, CH), c, 0, FW)], CH, FW, k.tab_c))
    c += FW
    for i in range(NQ):
        parts = []
        for g in range(NG):
            parts.append((slice(g * NH, (g + 1) * NH), c, g * P, P))
            c += P
        for g in range(NG):
            parts.append((slice(g * NH, (g + 1) * NH), c, NG * P + g * NQ, NQ))
            c += NQ
        jobs.append((parts, NH, SA, k.tab_sa[i]))
    for dst, width in ((k.tab_hc, HC), (k.tab_hw, HWC)):
        for o in range(0, width, 512):
            n = min(512, width - o)
            jobs.append(([(slice(0, CH), c + o, 0, n)], CH, n, dst[:, o:o + n]))
        c += width
    return jobs, c


def silu_tile(dve, k, sem, x, e, out, t):
    at = lambda v: v[:, bass.ds(t, 1), :]
    link = Chain(dve, sem, t * 2)
    link(dve.tensor_scalar(at(e), at(e), 1.0, None, ALU.add))
    settle(dve, k)
    link(dve.reciprocal(at(e), at(e)))
    return dve.tensor_tensor(at(out), at(x), at(e), ALU.mult)


def block_even_in(nc, k):
    KB = WB // P
    H = TAPS - 1
    with k.scope():
        xrow = k.sb("xrow", [P, 3, D])
        flat = xrow[:, :, :].rearrange("p a n -> p (a n)")
        u = flat[:, 0:KB * T].rearrange("p (c t) -> p c t", t=T)
        e = flat[:, KB * T:2 * KB * T].rearrange("p (c t) -> p c t", t=T)
        xT, xl = k.sb_and_lo("xT1", [P, KT, T])
        xh = k.sb("xh1", [P, KT, T], F32R)
        gcol = k.sb("gcol1", [P, KT])
        jobs, ncols = table_jobs(k)
        wide = k.sb("wide", [P, KB * WB])
        onehot = wide[0:NBUCK + 1, 0:ncols]
        pw = wide[:, :].rearrange("p (c n) -> p c n", n=WB)
        relb = k.sb("relb", [NBUCK + 1, NG * NH])
        up = k.sb("up", [P, KB, H + NP])
        us = k.sb("us", [P, KB, NB, H + NQ])
        y = k.sb("y", [P, KB, T])
        tab = y[0:CH, :, :].rearrange("p c t -> p (c t)")[:, 0:1024].rearrange("p (s n) -> p s n", s=2)
        hrow = k.sb("hrow", [4 * H, 2, WB])
        crow = hrow[0:NS, :, :]
        taps = k.sb("taps", [P, KB, TAPS])
        vec = k.sb("cvec", [P, 4, KB])
        mu = k.sb("mu", [P, T])
        rs = k.sb("rsb", [P, T])
        banks = [k.ps(f"zb{i}", [P, 512]) for i in range(4)]
        rbanks = [k.ps(f"rb{i}", [P, 512]) for i in range(3)]
        nbank = k.ps("nb", [P, 512])
        x_loaded, g_loaded, tab_loaded, xt_stored = (k.sem(n) for n in ("x_loaded", "g1_loaded", "tab_loaded", "xt_stored"))
        consts_loaded, consts_set = k.sem("consts_loaded"), k.sem("consts_set")
        turned, xT_ready = k.sem("x_turned"), k.sem("xT_ready")
        tab_done, tab_evac = k.sem("tab_done"), k.sem("tab_evac")
        tab_stored = [k.sem(f"tab_stored{i}") for i in range(2)]
        copied = k.sem("copied")
        u_in, h_in, v_in, pw_in = (k.sem(n) for n in ("glu_in", "hist_in", "cvec_in", "pw_in"))
        s_copied, padded, e_done, u_ready, chain = (k.sem(n) for n in ("conv_copied", "conv_padded", "glu_exp", "u_ready", "conv_chain"))
        h_turned, h_evac, c_turned, c_evac, c_stored = (k.sem(n) for n in ("h_turned", "h_evac", "c_turned", "c_evac", "c_stored"))
        taps_done, y_sum, yc_ready, var_sum, root, e2_done, act_ready, pw_done, o_ready, o_stored = (
            k.sem(n) for n in ("taps_done", "y_sum", "yc_ready", "var_sum", "ln_root", "silu_exp", "silu_ready", "pw_done", "ob_ready", "ob_stored"))
        ln_in, gate_in, gate_exp, gate_ready, gate_stored = (k.sem(n) for n in ("ln_in", "gate_in", "gate_exp", "gate_ready", "gate_stored"))
        glu_chain, silu_chain, gate_chain0, gate_chain1 = (k.sem(n) for n in ("glu_chain", "silu_chain", "gate_chain0", "gate_chain1"))
        norm = Norm(k, "1", xT, xT, gcol, nbank, hi=xh, lo=xl)
        GLU, GB, GB2, GA, GA2, Q, K0, K1, K2, K3, K4, K5, K6, K7, K8, K9 = range(16)
        proj = Proj(k, "1", k.w_in_even, xh, xl, banks,
                    [(4, Z_A, Z_A, None), (1, Z_GB, Z_GB, None), (1, Z_GB + GW, Z_GB + GW, None), (1, Z_GA, Z_GA, None),
                     (1, Z_GA + GW, Z_GA + GW, None), (6, 0, 0, None)]
                    + [(1, QKV + n * GW, QKV + n * GW, n * GW) for n in range(7)]
                    + [(n, QKV + g * GW, QKV + g * GW, g * GW) for g, n in ((7, 2), (9, 2), (11, 1))],
                    zt=k.zt, rows=k.kv, row_banks=rbanks)
        with nc.Block() as block:
            @block.sync
            def _(sp):
                sp.dma_start(k.ident[:, :], k.c_ident).then_inc(consts_loaded, 16)
                sp.dma_start(xrow[:, 0:2, :], k.x_prompt.rearrange("(t p) n -> p t n", p=P)).then_inc(x_loaded, 16)
                sp.dma_start(xrow[0:NS, 2, :], k.x_sample).then_inc(x_loaded, 16)
                sp.dma_start(gcol[:, :], k.norm_even).then_inc(g_loaded, 16)
                sp.dma_start(onehot, k.c_onehot).then_inc(tab_loaded, 16)
                sp.dma_start(relb[0:NBUCK, :], k.rel_bias).then_inc(tab_loaded, 16)
                proj.sync(sp)
                sp.wait_ge(proj.z_stored, 16 * 27)
                sp.wait_ge(proj.rows_stored, 32 * 13)

            @block.gpsimd
            def _(pool):
                link = Chain(pool, consts_set)
                link(pool.memset(k.ones[:, :], 1.0))
                link(pool.memset(k.eps[:, :], EPS))
                link(pool.memset(relb[NBUCK:NBUCK + 1, :], 1.0))
                pool.memset(up[:, :, 0:H], 0.0).then_inc(padded, 1)
                for i in range(2):
                    pool.dma_start(hrow[:, i, :], k.state_b_conv[4 * i:4 * i + 4].rearrange("b t n -> (b t) n")).then_inc(h_in, 16)
                pool.dma_start(taps[:, :, :], k.conv_w).then_inc(v_in, 16)
                for i, v in enumerate((k.conv_b, k.conv_ln_g, k.conv_ln_b, k.conv_pw_b)):
                    pool.dma_start(vec[:, i, :], v).then_inc(v_in, 16)
                pool.wait_ge(xT_ready, KT)
                pool.dma_start(k.xt.rearrange("(k p) t -> p k t", p=P), xT[:, :, :]).then_inc(xt_stored, 16)
                pool.wait_ge(tab_done, len(jobs))
                pool.dma_start(pw[:, :, :], k.conv_pw_w.rearrange("(c p) n -> p c n", p=P)).then_inc(pw_in, 16)
                for b in range(NB):
                    pool.dma_start(k.out_conv_s[b, 0:H - NQ, :], k.state_b_conv[b, NQ:H, :]).then_inc(s_copied, 16)
                pieces = k.cache_pieces[0:16]
                sent = 0

                def send(groups):
                    n = 0
                    for g in groups:
                        pool.wait_ge(proj.tile_done, 4 * g + 4)
                        pool.dma_start(*pieces[sent + n]).then_inc(copied, 16)
                        n += 1
                    return n

                pool.wait_ge(proj.z_stored, 16 * 5)
                pool.dma_start(u, k.zt[Z_A:Z_A + WB, :].rearrange("(c p) t -> p c t", p=P)).then_inc(u_in, 16)
                pool.dma_start(e, k.zt[Z_GT:Z_GT + WB, :].rearrange("(c p) t -> p c t", p=P)).then_inc(u_in, 16)
                sent += send((6,))
                pool.wait_ge(c_evac, 4)
                pool.dma_start(k.out_conv_p, crow[0:H, 0, :]).then_inc(c_stored, 16)
                for b in range(NB):
                    pool.dma_start(k.out_conv_s[b, H - NQ:H, :], crow[b * NQ:(b + 1) * NQ, 1, :]).then_inc(c_stored, 16)
                sent += send((8, 9, 10, 11, 12, 13, 14, 15, 17))
                pool.wait_ge(o_ready, KB)
                pool.dma_start(k.mt[NH * HD:, :].rearrange("(c p) t -> p c t", p=P), y[:, :, :]).then_inc(o_stored, 16)
                pool.wait_ge(o_stored, 16)
                for buf, z in ((u, Z_GA), (y[:, :, :], Z_GB)):
                    pool.dma_start(buf, k.zt[z:z + WB, :].rearrange("(c p) t -> p c t", p=P)).then_inc(gate_in, 16)
                sent += send((21, 22, 23))
                for i, buf in enumerate((u, y[:, :, :])):
                    pool.wait_ge(gate_ready, KB * (i + 1))
                    pool.dma_start(k.gate[i * WB:(i + 1) * WB, :].rearrange("(c p) t -> p c t", p=P), buf).then_inc(gate_stored, 16)
                sent += send((24, 25, 26))
                pool.wait_ge(copied, 16 * sent)
                pool.wait_ge(s_copied, 16 * NB)
                pool.wait_ge(c_stored, 16 * (NB + 1))
                pool.wait_ge(gate_stored, 32)

            @block.scalar
            def _(act):
                for n, (parts, m, width, dst) in enumerate(jobs):
                    act.wait_ge(tab_done, n + 1)
                    if n >= 2:
                        act.wait_ge(tab_stored[n % 2], 16 * (n // 2))
                    act.copy(tab[0:m, n % 2, 0:width], rbanks[n % 2][0:m, 0:width]).then_inc(tab_evac, 1)
                    act.wait_ge(tab_evac, n + 1)
                    act.dma_start(dst, tab[0:m, n % 2, 0:width]).then_inc(tab_stored[n % 2], 16)
                norm.act(act)

                def glu_exp(act):
                    act.wait_ge(u_in, 32)
                    act.activation(e, e, ACT.Exp, scale=-1.0).then_inc(e_done, 1)

                def deviation(act):
                    act.wait_ge(var_sum, 1)
                    act.activation(rs[:, :], nbank[:, 0:T], ACT.Sqrt, bias=k.eps[:, :], scale=1.0 / WB).then_inc(root, 1)

                def silu_exps(act):
                    for c in range(KB):
                        act.wait_ge(ln_in, c + 1)
                        act.activation(e[:, c, :], y[:, c, :], ACT.Exp, scale=-1.0).then_inc(e2_done, 1)

                def gate_exps(act, i):
                    act.wait_ge(gate_in, 32)
                    if i:
                        act.wait_ge(gate_ready, KB)
                    act.activation(e, (u, y[:, :, :])[i], ACT.Exp, scale=-1.0).then_inc(gate_exp, 1)

                proj.act(act, {GB2: glu_exp, K3: deviation, K4: silu_exps, K7: lambda e: gate_exps(e, 0), K8: lambda e: gate_exps(e, 1)})
                for i in range(2):
                    act.wait_ge(tab_stored[i], 16 * len(jobs[i::2]))

            @block.tensor
            def _(pe):
                pe.wait_ge(consts_loaded, 16)
                pe.wait_ge(x_loaded, 32)
                for t in range(KT):
                    if t >= 4:
                        pe.wait_ge(xT_ready, t - 3)
                    for j, m in enumerate((P, P, NS)):
                        ins = pe.transpose(banks[t % 4][:, j * P:j * P + m], xrow[0:m, j, t * P:(t + 1) * P], k.ident[0:m, 0:m])
                    ins.then_inc(turned, 1)
                pe.wait_ge(consts_set, 3)
                norm.pe(pe)
                pe.wait_ge(tab_loaded, 32)

                def tables(pe):
                    for n, (parts, m, width, dst) in enumerate(jobs):
                        if n >= 2:
                            pe.wait_ge(tab_evac, n - 1)
                        for heads, c, o, w in parts:
                            ins = pe.matmul(rbanks[n % 2][0:m, o:o + w], relb[:, heads], onehot[:, c:c + w], start=True, stop=True)
                        ins.then_inc(tab_done, 1)

                def history(pe):
                    pe.wait_ge(h_in, 32)
                    pe.wait_ge(tab_evac, len(jobs))
                    for c in range(KB):
                        if c >= 2:
                            pe.wait_ge(h_evac, c - 1)
                        for i in range(2):
                            ins = pe.transpose(rbanks[c % 2][:, i * 4 * H:(i + 1) * 4 * H], hrow[:, i, c * P:(c + 1) * P], k.ident[0:4 * H, 0:4 * H])
                        ins.then_inc(h_turned, 1)

                def new_rows(pe):
                    pe.wait_ge(u_ready, KB)
                    pe.wait_ge(h_evac, KB)
                    for j, (lo, m) in enumerate(((NP - H, H), (NP, NS))):
                        for half in range(2):
                            if j:
                                pe.wait_ge(c_evac, half + 1)
                            for c in range(4):
                                ins = pe.transpose(rbanks[half][0:m, c * P:(c + 1) * P], u[:, half * 4 + c, lo:lo + m], k.ident[:, :])
                            ins.then_inc(c_turned, 1)

                def sum_y(pe):
                    pe.wait_ge(taps_done, 2 * KB * TAPS)
                    for c in range(KB):
                        ins = pe.matmul(nbank[:, 0:T], k.ones[:, :], y[:, c, :], start=(c == 0), stop=(c == KB - 1))
                    ins.then_inc(y_sum, 1)

                def sum_var(pe):
                    pe.wait_ge(yc_ready, 1)
                    for c in range(KB):
                        ins = pe.matmul(nbank[:, 0:T], k.ones[:, :], e[:, c, :], start=(c == 0), stop=(c == KB - 1))
                    ins.then_inc(var_sum, 1)

                def pointwise(pe):
                    pe.wait_ge(act_ready, KB)
                    pe.wait_ge(pw_in, 16)
                    pe.wait_ge(proj.rows_evac, 3 * 6 + 3)
                    for n in range(KB):
                        if n >= 2:
                            pe.wait_ge(o_ready, n - 1)
                        for c in range(KB):
                            ins = pe.matmul(rbanks[n % 2][:, 0:T], pw[:, c, n * P:(n + 1) * P], u[:, c, :], start=(c == 0), stop=(c == KB - 1))
                        ins.then_inc(pw_done, 1)
                    pe.wait_ge(o_ready, KB)

                tables(pe)
                proj.pe(pe, lambda e, q: e.wait_ge(norm.ready, 4 * q + 4), {GB: history, Q: new_rows, K2: sum_y, K3: sum_var, K6: pointwise})

            @block.vector
            def _(dve):
                for t in range(KT):
                    dve.wait_ge(turned, t + 1)
                    dve.tensor_copy(xT[:, t, :], banks[t % 4][:, 0:T]).then_inc(xT_ready, 1)
                dve.wait_ge(g_loaded, 16)
                norm.dve(dve, lambda e, t: e.wait_ge(xT_ready, t + 1), lambda e: e.wait_ge(xt_stored, 16))
                link = Chain(dve, chain)

                def history(dve):
                    for c in range(KB):
                        dve.wait_ge(h_turned, c + 1)
                        dve.tensor_copy(us[:, c, :, 0:H], rbanks[c % 2][:, 0:NB * H].rearrange("p (b t) -> p b t", t=H)).then_inc(h_evac, 1)

                def glu(t):
                    dve.wait_ge(e_done, 1)
                    silu_tile(dve, k, glu_chain, u, e, u, t).then_inc(u_ready, 1)

                def spread_u(dve):
                    dve.wait_ge(u_ready, KB)
                    link(dve.tensor_copy(up[:, :, H:], u[:, :, 0:NP]))
                    link(dve.tensor_copy(us[:, :, :, H:], u[:, :, NP:T].rearrange("p c (b q) -> p c b q", q=NQ)))

                def views(c, j, t):
                    if j == 0:
                        return y[:, c, 0:NP], up[:, c, bass.ds(t, NP)]
                    return y[:, c, NP:T].rearrange("p (b q) -> p b q", q=NQ), us[:, c, :, bass.ds(t, NQ)]

                def first_tap(dve):
                    for j, m in enumerate((H, NS)):
                        for half in range(2):
                            dve.wait_ge(c_turned, 2 * j + half + 1)
                            dve.tensor_copy(crow[0:m, j, half * 512:(half + 1) * 512], rbanks[half][0:m, :]).then_inc(c_evac, 1)
                    dve.wait_ge(v_in, 80)
                    dve.wait_ge(padded, 1)
                    for i in range(2):
                        dve.wait_ge(tab_stored[i], 16 * len(jobs[i::2]))
                    for j in range(2):
                        for c in range(KB):
                            out, x = views(c, j, 0)
                            dve.tensor_scalar(out, x, taps[:, c, 0:1], vec[:, 0, c:c + 1], ALU.mult, ALU.add).then_inc(taps_done, 1)

                def tap(t):
                    for j in range(2):
                        for c in range(KB):
                            n = j * KB + c
                            dve.wait_ge(taps_done, t * (2 * KB) + (n + 1 - 2 * KB))
                            out, x = views(c, j, t)
                            dve.scalar_tensor_tensor(out, x, taps[:, c, bass.ds(t, 1)], out, ALU.mult, ALU.add).then_inc(taps_done, 1)

                def last_taps(dve):
                    tap(TAPS - 2)
                    tap(TAPS - 1)

                all_c = [P, KB, T]

                def centre(dve):
                    dve.wait_ge(y_sum, 1)
                    link(dve.tensor_scalar(mu[:, :], nbank[:, 0:T], 1.0 / WB, None, ALU.mult))
                    link(dve.tensor_tensor(y[:, :, :], y[:, :, :], mu[:, :].unsqueeze(1).broadcast_to(all_c), ALU.subtract))
                    dve.tensor_tensor(e, y[:, :, :], y[:, :, :], ALU.mult).then_inc(yc_ready, 1)

                def scale(dve):
                    dve.wait_ge(root, 1)
                    link(dve.reciprocal(rs[:, :], rs[:, :]))
                    link(dve.tensor_tensor(y[:, :, :], y[:, :, :], rs[:, :].unsqueeze(1).broadcast_to(all_c), ALU.mult))
                    for c in range(KB):
                        dve.tensor_scalar(y[:, c, :], y[:, c, :], vec[:, 1, c:c + 1], vec[:, 2, c:c + 1], ALU.mult, ALU.add).then_inc(ln_in, 1)

                def silu(t):
                    dve.wait_ge(e2_done, t + 1)
                    silu_tile(dve, k, silu_chain, y, e, u, t).then_inc(act_ready, 1)

                def pointwise(dve):
                    for n in range(KB):
                        dve.wait_ge(pw_done, n + 1)
                        dve.tensor_scalar(y[:, n, :], rbanks[n % 2][:, 0:T], vec[:, 3, n:n + 1], None, ALU.add).then_inc(o_ready, 1)

                def gate(i, t):
                    buf = (u, y)[i]
                    dve.wait_ge(gate_exp, i + 1)
                    silu_tile(dve, k, (gate_chain0, gate_chain1)[i], buf, e, buf, t).then_inc(gate_ready, 1)

                proj.dve(dve, {GB: history, GA2: spread_u, Q: first_tap, K1: last_taps, K2: centre, K3: scale, K6: pointwise},
                         {GB2: lambda n: glu(n), GA: lambda n: glu(n + 4), Q: lambda n: tap(n + 1), K0: lambda n: tap(n + 25),
                          K4: lambda n: silu(n), K5: lambda n: silu(n + 4), K7: lambda n: gate(0, n), K8: lambda n: gate(1, n)})


NR = NQ * NH
ZN = [0, NH * NR, 2 * NH * NR]
Z1 = 3 * NH * NR
Z2 = Z1 + 4 * NH * NR
ZQ = Z2 + NQ * NH * NR
TILES = [(0, 0)] + [(1, r) for r in range(4)] + [(2, i) for i in range(NQ)]


def z_block(g, r, h):
    o = (ZN[0], Z1, Z2)[g] + (r * NH + h) * NR
    return slice(o, o + NR)


def block_sample_a(nc, k):
    with k.scope():
        kt = [k.sb("ka0", [P, 1, NH * HD]), k.sb("ka1", [P, 4, NH * HD]), k.sb("ka2", [P, NQ, NH * HD])]
        vt = [k.sb("va0", [P, 1, NH * HD]), k.sb("va1", [P, 4, NH * HD]), k.sb("va2", [P, NQ, NH * HD])]
        vnew = k.sb("vnew", [NG * NQ, NH * HD])
        qs = k.sb("qsa", [P, NG * NH, NS])
        kn = k.sb("kna", [P, NG * NH, NS])
        qz = k.sb("qz", [P, ZQ])
        pz = k.sb("pz", [P, ZQ - 2 * NH * NR])
        pzn = k.sb("pzn", [NG * NQ, NH, NR])
        bias = k.sb("bias_sa", [NR, SA])
        s = k.sb("s_sa", [NR, SA])
        stat = k.sb("stat_sa", [NR, 4])
        ktt = k.sb("ktt", [P, 2, 4 * P])
        orow = k.sb("orow", [NR, HD])
        ot = k.sb("ot_sa", [P, NH, NS])
        kps = [k.ps(f"kps{i}", [P, 512]) for i in range(2)]
        sps, pps, ops, tps = (k.ps(n, [P, 512]) for n in ("sps", "pps", "ops", "tps"))
        pieces = [(0, 0, 1), (1, 0, 4), (2, 0, 4), (2, 4, 8)]
        k_in = [k.sem(f"ka_in{i}") for i in range(4)]
        v_in = [k.sem(f"va_in{i}") for i in range(4)]
        vn_in, q_in, b_in, zeroed = k.sem("vn_in"), k.sem("qa_in"), k.sem("ba_in"), k.sem("za_set")
        qz_ready, turned, evac_a, evac_d = k.sem("qz_ready"), k.sem("ka_turned"), k.sem("ka_evac_a"), k.sem("ka_evac_d")
        scored, score_tiles = k.sem("sa_done"), k.sem("sa_tiles")
        chain, max_done, exp_done, p_ready = k.sem("sa_chain"), k.sem("sa_max"), k.sem("sa_exp"), k.sem("sa_p")
        p_turned, pz_ready, pv_done, o_evac, o_turned, o_ready, o_stored = (
            k.sem(n) for n in ("pa_turned", "pza_ready", "pva_done", "oa_evac", "oa_turned", "oa_ready", "oa_stored"))
        pv_tiles = k.sem("pva_tiles")
        scaled, toe_stored, rows_out = k.sem("qa_scaled"), k.sem("toe_stored"), k.sem("rows_a_out")
        NQUAD = 2 * len(TILES)

        def tile_src(g, lo, hi, b, kv):
            w, dil = GROUPS[g]
            v = k.cache_a[g].rearrange("b (j r) a h d -> b j r a (h d)", r=dil)
            return v[bass.ds(b, 1), :, lo:hi, kv, :].rearrange("b j r n -> (b j) r n")

        with nc.Block() as block:
            @block.sync
            def _(sp):
                for i in range(NG):
                    sp.dma_start(qs[:, i * NH:(i + 1) * NH, :], k.zt[i * 1024:(i + 1) * 1024, NP:T].rearrange("(h d) t -> d h t", d=HD)).then_inc(q_in, 16)
                    sp.dma_start(kn[:, i * NH:(i + 1) * NH, :], k.zt[QKV + i * 1024:QKV + (i + 1) * 1024, NP:T].rearrange("(h d) t -> d h t", d=HD)).then_inc(q_in, 16)
                sp.dma_start(bias[:, :], k.tab_sa.rearrange("i h n -> (i h) n")).then_inc(b_in, 16)

                def load_k(b, first=False):
                    for n, (g, lo, hi) in enumerate(pieces):
                        if not first:
                            sp.wait_ge(turned, b * NQUAD - NQUAD + 2 * sum(t[2] - t[1] for t in pieces[:n + 1]))
                        sp.dma_start(kt[g][:, lo:hi, :], tile_src(g, lo, hi, b, 0)).then_inc(k_in[n], 16)

                def load_v(b, first=False):
                    for n, (g, lo, hi) in enumerate(pieces):
                        if not first:
                            sp.wait_ge(pv_tiles, b * 4 - 4 + (n + 1))
                        sp.dma_start(vt[g][:, lo:hi, :], tile_src(g, lo, hi, b, 1)).then_inc(v_in[n], 16)
                    if not first:
                        sp.wait_ge(pv_done, b * 1)
                    for g in range(NG):
                        c = QKV + g * NH * HD
                        sp.dma_start(vnew[g * NQ:(g + 1) * NQ, :], k.kv[bass.ds(b * NQ + NP, NQ), c:c + NH * HD]).then_inc(vn_in, 16)

                load_k(0, True)
                load_v(0, True)
                with sp.Fori(1, NB) as b:
                    load_k(b)
                    load_v(b)
                sp.wait_ge(o_ready, NB)
                sp.dma_start(k.mt[0:NH * HD, NP:T].rearrange("(h d) t -> d h t", d=HD), ot[:, :, :]).then_inc(o_stored, 16)
                sp.wait_ge(o_stored, 16)

            @block.gpsimd
            def _(pool):
                pool.dma_start(k.toe_a.rearrange("g h p n -> (g h) p n"), dram_ap(k.tab_a, P - 1, [(FW, NG * NH), (-1, P), (1, NP)])).then_inc(toe_stored, 16)
                pool.dma_start(k.toe_c, dram_ap(k.tab_c, P - 1, [(FW, CH), (-1, P), (1, NP)])).then_inc(toe_stored, 16)
                link = Chain(pool, zeroed)
                link(pool.memset(qz[:, :], 0.0))
                link(pool.memset(pz[:, :], 0.0))
                link(pool.memset(pzn[:, :, :], 0.0))
                pool.wait_ge(scaled, 1)

                def fill_q(b):
                    wait(pool, scored, b * 1)
                    for g in range(NG):
                        pool.tensor_copy(ap_of(qz[:, :], ZN[g], [(NR + 1, NH), (NH, NQ)]),
                                         qs[:, g * NH:(g + 1) * NH, bass.ds(b * NQ, NQ)]).then_inc(qz_ready, 1)
                    for h in range(2):
                        pool.tensor_copy(ap_of(qz[:, :], Z1 + h * 4 * NH, [(NH * NR + NH, 4), (NR + 1, NH)]),
                                         qs[:, NH:2 * NH, bass.ds(b * NQ + 4 * h, 4)].rearrange("p h i -> p i h")).then_inc(qz_ready, 1)
                    pool.tensor_copy(ap_of(qz[:, :], Z2, [(NH * NR + NH, NQ), (NR + 1, NH)]),
                                     qs[:, 2 * NH:3 * NH, bass.ds(b * NQ, NQ)].rearrange("p h i -> p i h")).then_inc(qz_ready, 1)

                fill_q(0)
                n_rows = 0
                for g, (w, _) in enumerate(GROUPS):
                    keep = min(w, NP)
                    for kv in range(2):
                        c = kv * QKV + g * NH * HD
                        pool.dma_start(k.out_a_p[g][:, kv, :, :].rearrange("t h d -> t (h d)"), k.kv[NP - keep:NP, c:c + NH * HD]).then_inc(rows_out, 16)
                        for b in range(NB):
                            pool.dma_start(k.out_a_s[g][b, w - NQ:w, kv, :, :].rearrange("t h d -> t (h d)"),
                                           k.kv[NP + b * NQ:NP + (b + 1) * NQ, c:c + NH * HD]).then_inc(rows_out, 16)
                        n_rows += 1 + NB

                with pool.Fori(1, NB) as b:
                    fill_q(b)
                pool.wait_ge(toe_stored, 32)
                pool.wait_ge(rows_out, 16 * n_rows)

            def evac_k(eng, b, odd, sem):
                copy = eng.tensor_copy if odd else eng.copy
                for q in range(odd, NQUAD, 2):
                    eng.wait_ge(turned, b * NQUAD + (q + 1))
                    wait(eng, score_tiles, b * NQUAD + (q - 1))
                    copy(ktt[:, q % 2, :], kps[q % 2][:, :]).then_inc(sem, 1)

            @block.scalar
            def _(act):
                def one(b):
                    evac_k(act, b, 0, evac_a)
                    act.wait_ge(max_done, b + 1)
                    act.activation(s[:, :], s[:, :], ACT.Exp, bias=stat[:, 1:2], accum_out=stat[:, 2:3]).then_inc(exp_done, 1)

                one(0)
                with act.Fori(1, NB) as b:
                    one(b)

            @block.tensor
            def _(pe):
                def quad_turn(b, q):
                    g, r = TILES[q // 2]
                    if q % 2 == 0 and (g, r) in [(p_[0], p_[1]) for p_ in pieces]:
                        pe.wait_ge(k_in[[(p_[0], p_[1]) for p_ in pieces].index((g, r))], b * 16 + 16)
                    if q >= 2:
                        pe.wait_ge((evac_a, evac_d)[q % 2], b * (NQUAD // 2) + q // 2)
                    for j in range(4):
                        h = 4 * (q % 2) + j
                        ins = pe.transpose(kps[q % 2][:, j * P:(j + 1) * P], kt[g][:, r, h * HD:(h + 1) * HD], k.ident[:, :])
                    ins.then_inc(turned, 1)

                def quad_score(b, q):
                    g, r = TILES[q // 2]
                    pe.wait_ge((evac_a, evac_d)[q % 2], b * (NQUAD // 2) + (q // 2 + 1))
                    for j in range(4):
                        h = 4 * (q % 2) + j
                        first = r == 0 and h == 0
                        last = r == (0, 3, NQ - 1)[g] and h == NH - 1
                        ins = pe.matmul(sps[0:NR, g * P:(g + 1) * P], qz[:, z_block(g, r, h)], ktt[:, q % 2, j * P:(j + 1) * P],
                                        start=first, stop=last)
                    ins.then_inc(score_tiles, 1)

                def scores(b):
                    quad_turn(b, 0)
                    pe.wait_ge(qz_ready, b * 6 + 6)
                    wait(pe, max_done, b * 1)
                    for q in range(NQUAD):
                        if q + 1 < NQUAD:
                            quad_turn(b, q + 1)
                        quad_score(b, q)
                    for g in range(NG):
                        for h in range(NH):
                            o = ZN[g] + h * NR
                            ins = pe.matmul(sps[0:NR, NG * P + g * NQ:NG * P + (g + 1) * NQ], qz[:, o:o + NR],
                                            kn[:, g * NH + h, bass.ds(b * NQ, NQ)], start=(h == 0), stop=(h == NH - 1))
                    ins.then_inc(scored, 1)

                def turn_p(b):
                    pe.wait_ge(p_ready, b + 1)
                    wait(pe, pz_ready, b * 5)
                    settle(pe, k)
                    for g in range(NG):
                        pe.transpose(pps[:, g * NR:(g + 1) * NR], s[:, g * P:(g + 1) * P], k.ident[0:NR, 0:NR])
                    pe.transpose(pps[0:NG * NQ, NG * NR:(NG + 1) * NR], s[:, NG * P:SA], k.ident[0:NR, 0:NR]).then_inc(p_turned, 1)

                def values(b):
                    pe.wait_ge(pz_ready, b * 5 + 5)
                    wait(pe, o_evac, b * 1)
                    n = 0
                    for g, r in TILES:
                        for m, (pg, lo, hi) in enumerate(pieces):
                            if (pg, lo) == (g, r):
                                pe.wait_ge(v_in[m], b * 16 + 16)
                        for h in range(NH):
                            c = z_block(g, r, h).start - (2 * NH * NR if g else 0)
                            ins = pe.matmul(ops[0:NR, 0:HD], pz[:, c:c + NR], vt[g][:, r, h * HD:(h + 1) * HD],
                                            start=(n == 0), stop=False)
                            n += 1
                        if (g, r + 1) in [(p_[0], p_[2]) for p_ in pieces]:
                            ins.then_inc(pv_tiles, 1)
                    pe.wait_ge(vn_in, b * 48 + 48)
                    for h in range(NH):
                        ins = pe.matmul(ops[0:NR, 0:HD], pzn[:, h, :], vnew[:, h * HD:(h + 1) * HD], start=False, stop=(h == NH - 1))
                    ins.then_inc(pv_done, 1)

                def turn_o(b):
                    pe.wait_ge(o_evac, b + 1)
                    wait(pe, o_ready, b * 1)
                    settle(pe, k)
                    pe.transpose(tps[:, 0:NR], orow[:, :], k.ident[0:NR, 0:NR]).then_inc(o_turned, 1)

                scores(0)
                turn_p(0)
                with pe.Fori(1, NB) as b:
                    scores(b)
                    values(b - 1)
                    turn_p(b)
                    turn_o(b - 1)
                values(NB - 1)
                turn_o(NB - 1)

            @block.vector
            def _(dve):
                dve.wait_ge(q_in, 96)
                dve.tensor_scalar(qs[:, :, :], qs[:, :, :], SCALE, None, ALU.mult).then_inc(scaled, 1)
                dve.wait_ge(b_in, 16)
                dve.wait_ge(zeroed, 3)

                def softmax(b):
                    link = Chain(dve, chain, b * 2)
                    dve.wait_ge(scored, b + 1)
                    wait(dve, p_turned, b * 1)
                    settle(dve, k)
                    link(dve.tensor_tensor_reduce(s[:, :], sps[0:NR, 0:SA], bias[:, :], 1.0, -3.0e38, ALU.add, ALU.max, stat[:, 0:1]))
                    dve.tensor_scalar(stat[:, 1:2], stat[:, 0:1], -1.0, None, ALU.mult).then_inc(max_done, 1)
                    dve.wait_ge(exp_done, b + 1)
                    link(dve.reciprocal(stat[:, 3:4], stat[:, 2:3]))
                    dve.tensor_scalar(s[:, :], s[:, :], stat[:, 3:4], None, ALU.mult).then_inc(p_ready, 1)

                def fill_p(b):
                    dve.wait_ge(p_turned, b + 1)
                    wait(dve, pv_done, b * 1)
                    dve.tensor_copy(ap_of(pz[:, :], 0, [(NR + 1, NH), (NH, NQ)]),
                                    ap_of(pps[:, :], 0, [(1, NH), (NH, NQ)])).then_inc(pz_ready, 1)
                    o1, o2 = Z1 - 2 * NH * NR, Z2 - 2 * NH * NR
                    for h in range(2):
                        dve.tensor_copy(ap_of(pz[:, :], o1 + h * 4 * NH, [(NH * NR + NH, 4), (NR + 1, NH)]),
                                        ap_of(pps[:, :], NR + h * 4 * NH, [(NH, 4), (1, NH)])).then_inc(pz_ready, 1)
                    dve.tensor_copy(ap_of(pz[:, :], o2, [(NH * NR + NH, NQ), (NR + 1, NH)]),
                                    ap_of(pps[:, :], 2 * NR, [(NH, NQ), (1, NH)])).then_inc(pz_ready, 1)
                    dve.tensor_copy(ap_of(pzn[:, :, :], 0, [(NR + 1, NH), (NH, NQ)]),
                                    ap_of(pps[0:NG * NQ, :], 3 * NR, [(1, NH), (NH, NQ)])).then_inc(pz_ready, 1)

                def out_rows(b):
                    dve.wait_ge(pv_done, b + 1)
                    wait(dve, o_turned, b * 1)
                    dve.tensor_copy(orow[:, :], ops[0:NR, 0:HD]).then_inc(o_evac, 1)

                def out_cols(b):
                    dve.wait_ge(o_turned, b + 1)
                    dve.tensor_copy(ot[:, :, bass.ds(b * NQ, NQ)], tps[:, 0:NR].rearrange("p (i h) -> p h i", h=NH)).then_inc(o_ready, 1)

                evac_k(dve, 0, 1, evac_d)
                softmax(0)
                fill_p(0)
                with dve.Fori(1, NB) as b:
                    evac_k(dve, b, 1, evac_d)
                    softmax(b)
                    out_rows(b - 1)
                    fill_p(b)
                    out_cols(b - 1)
                out_rows(NB - 1)
                out_cols(NB - 1)


def block_prompt_a(nc, k):
    with k.scope():
        U = 2
        q = k.sb("qpa", [P, U, NG, NP])
        kk = k.sb("kpa", [P, U, NG, NP])
        v = k.sb("vpa", [P, U, 2, NG, HD])
        tab = k.sb("tpa", [P, U, NG, NP])
        s = k.sb("spa", [P, 2, NG, NP])
        pt = k.sb("ptpa", [P, 2, 2 * NG, P])
        stat = k.sb("stpa", [P, 2, 4])
        ot = k.sb("otpa", [P, U, NP])
        sps = [k.ps(f"spa{i}", [P, 1024]) for i in range(2)]
        pps = [k.ps(f"ppa{i}", [P, 512]) for i in range(2)]
        ops = [k.ps(f"opa{i}", [P, 512]) for i in range(2)]
        loaded = [k.sem(f"pp_in{u}") for u in range(U)]
        q_scaled, scored, max_done, exp_done, p_ready, chain = (
            k.sem(n) for n in ("pp_scaled", "pp_scored", "pp_max", "pp_exp", "pp_p", "pp_chain"))
        turned, pt_ready, pv_done, o_ready = (k.sem(n) for n in ("pp_turned", "pp_pt", "pp_pv", "pp_o"))
        stored = [k.sem(f"pp_stored{u}") for u in range(U)]

        with nc.Block() as block:
            @block.sync
            def _(sp):
                with sp.Fori(0, NH // U) as it:
                    for u in range(U):
                        h = it * U + u
                        sp.wait_ge(pv_done, it * (2 * U) + (2 * u + 2))
                        for src, dst in ((0, q), (QKV, kk)):
                            sp.dma_start(dst[:, u, :, :], k.zt[src:src + QKV, 0:NP].rearrange("(g h d) t -> h d g t", g=NG, h=NH)
                                         [bass.ds(h, 1)].rearrange("a d g t -> (a d) g t")).then_inc(loaded[u], 16)
                        sp.dma_start(v[:, u, 0, :, :], k.kv[0:P, QKV:2 * QKV].rearrange("p (g h d) -> h p g d", g=NG, h=NH)
                                     [bass.ds(h, 1)].rearrange("a p g d -> (a p) g d")).then_inc(loaded[u], 16)
                        sp.dma_start(v[:, u, 1, :, :], k.kv[P:NP, QKV:2 * QKV].rearrange("p (g h d) -> h p g d", g=NG, h=NH)
                                     [bass.ds(h, 1)].rearrange("a p g d -> (a p) g d")).then_inc(loaded[u], 16)
                        for g in range(NG):
                            sp.dma_start(tab[:, u, g, :], k.toe_a[g][bass.ds(h, 1)].rearrange("a p n -> (a p) n")).then_inc(loaded[u], 16)

            @block.scalar
            def _(act):
                for u in range(U):
                    act.sem_inc(stored[u], 16)
                with act.Fori(0, NH // U) as it:
                    for u in range(U):
                        for qb in range(2):
                            n = 2 * u + qb
                            nk = P * (qb + 1)
                            act.wait_ge(max_done, it * (2 * U) + (n + 3))
                            act.activation(s[:, qb, :, 0:nk], s[:, qb, :, 0:nk], ACT.Exp, bias=stat[:, qb, 1:2],
                                           accum_out=stat[:, qb, 2:3]).then_inc(exp_done, 1)
                        act.wait_ge(o_ready, it * (2 * U) + (2 * u + 4))
                        act.dma_start(k.mt[bass.ds((it * U + u) * HD, HD), 0:NP], ot[:, u, :]).then_inc(stored[u], 16)
                for u in range(U):
                    act.wait_ge(stored[u], 16 * (NH // U) + 16)

            @block.tensor
            def _(pe):
                pe.sem_inc(pv_done, 2 * U)
                with pe.Fori(0, NH // U) as it:
                    for u in range(U):
                        pe.wait_ge(loaded[u], it * 112 + 112)
                        pe.wait_ge(q_scaled, it * U + (u + 1))
                        for qb in range(2):
                            n = 2 * u + qb
                            nk = P * (qb + 1)
                            pe.wait_ge(max_done, it * (2 * U) + (n + 1))
                            for g in range(NG):
                                ins = pe.matmul(sps[qb][:, g * NP:g * NP + nk], q[:, u, g, qb * P:(qb + 1) * P], kk[:, u, g, 0:nk],
                                                start=True, stop=True)
                            ins.then_inc(scored, 1)
                        for qb in range(2):
                            n = 2 * u + qb
                            pe.wait_ge(p_ready, it * (2 * U) + (n + 1))
                            for half in range(qb + 1):
                                for g in range(NG):
                                    ins = pe.transpose(pps[half][:, g * P:(g + 1) * P], s[:, qb, g, half * P:(half + 1) * P], k.ident[:, :])
                                ins.then_inc(turned, 1)
                            pe.wait_ge(pt_ready, it * (3 * U) + (3 * u + (1, 3)[qb]))
                            pe.wait_ge(o_ready, it * (2 * U) + (n + 1))
                            for half in range(qb + 1):
                                for g in range(NG):
                                    ins = pe.matmul(ops[qb][:, 0:P], v[:, u, half, g, :], pt[:, qb, half * NG + g, :],
                                                    start=(half == 0 and g == 0), stop=(half == qb and g == NG - 1))
                            ins.then_inc(pv_done, 1)

            @block.vector
            def _(dve):
                dve.sem_inc(max_done, 2)
                dve.sem_inc(o_ready, 2)
                with dve.Fori(0, NH // U) as it:
                    link = Chain(dve, chain, it * (4 * U))
                    for u in range(U):
                        dve.wait_ge(loaded[u], it * 112 + 112)
                        dve.tensor_scalar(q[:, u, :, :], q[:, u, :, :], SCALE, None, ALU.mult).then_inc(q_scaled, 1)
                        for qb in range(2):
                            n = 2 * u + qb
                            nk = P * (qb + 1)
                            lo = NP - nk
                            dve.wait_ge(scored, it * (2 * U) + (n + 1))
                            settle(dve, k)
                            link(dve.tensor_tensor_reduce(s[:, qb, :, 0:nk], sps[qb][:, 0:NG * NP].rearrange("p (g n) -> p g n", g=NG)[:, :, 0:nk],
                                                          tab[:, u, :, lo:NP], 1.0, -3.0e38, ALU.add, ALU.max, stat[:, qb, 0:1]))
                            dve.tensor_scalar(stat[:, qb, 1:2], stat[:, qb, 0:1], -1.0, None, ALU.mult).then_inc(max_done, 1)
                        for qb in range(2):
                            n = 2 * u + qb
                            nk = P * (qb + 1)
                            dve.wait_ge(exp_done, it * (2 * U) + (n + 1))
                            link(dve.reciprocal(stat[:, qb, 3:4], stat[:, qb, 2:3]))
                            dve.tensor_scalar(s[:, qb, :, 0:nk], s[:, qb, :, 0:nk], stat[:, qb, 3:4], None, ALU.mult).then_inc(p_ready, 1)
                        for qb in range(2):
                            n = 2 * u + qb
                            for half in range(qb + 1):
                                dve.wait_ge(turned, it * (3 * U) + (3 * u + qb + half + 1))
                                dve.tensor_copy(pt[:, qb, half * NG:(half + 1) * NG, :], pps[half][:, 0:NG * P].rearrange("p (g n) -> p g n", g=NG)).then_inc(pt_ready, 1)
                        for qb in range(2):
                            n = 2 * u + qb
                            dve.wait_ge(pv_done, it * (2 * U) + (2 * U + n + 1))
                            dve.wait_ge(stored[u], it * 16 + 16)
                            dve.tensor_copy(ot[:, u, qb * P:(qb + 1) * P], ops[qb][:, 0:P]).then_inc(o_ready, 1)


class Mix:

    def __init__(self, k, tag):
        self.mix, self.lo = k.sb_and_lo("mix" + tag, [P, KT, T])
        self.gate, self.hi = k.sb_and_lo("gate" + tag, [P, KT, T])
        self.loaded = [k.sem(f"mix_in{c}" + tag) for c in range(4)]
        self.full, self.hi_made, self.ready = (k.sem(n + tag) for n in ("mix_full", "mix_hi", "mix_ready"))

    def sync(self, sp, k):
        for c in range(4):
            for dst, src in ((self.mix, k.mt), (self.gate, k.gate)):
                sp.dma_start(dst[:, c * 4:(c + 1) * 4, :], src[c * 512:(c + 1) * 512, :].rearrange("(k p) t -> p k t", p=P)).then_inc(self.loaded[c], 16)

    def dve(self, dve):
        def lo(c):
            s = slice(c * 4, (c + 1) * 4)
            dve.wait_ge(self.hi_made, c + 1)
            dve.tensor_tensor(self.lo[:, s, :], self.mix[:, s, :], self.hi[:, s, :], ALU.subtract).then_inc(self.ready, 1)

        for c in range(4):
            s = slice(c * 4, (c + 1) * 4)
            dve.wait_ge(self.loaded[c], 32)
            dve.tensor_tensor(self.mix[:, s, :], self.mix[:, s, :], self.gate[:, s, :], ALU.mult).then_inc(self.full, 1)
            if c:
                lo(c - 1)
        lo(3)

    def act(self, act):
        for c in range(4):
            s = slice(c * 4, (c + 1) * 4)
            act.wait_ge(self.full, c + 1)
            act.copy(self.hi[:, s, :], self.mix[:, s, :]).then_inc(self.hi_made, 1)


def block_even_out_odd_in(nc, k):
    with k.scope():
        mixed = Mix(k, "2")
        mix, gate = mixed.mix, mixed.gate
        xT = k.sb("xT2", [P, KT, T])
        xn, xl = k.sb_and_lo("xn2", [P, KT, T])
        xh = k.sb("xh2", [P, KT, T], F32R)
        gcol = k.sb("gcol2", [P, KT])
        wg = k.sb("wg", [P, KT, 3 * CH])
        gr = k.sb("gr", [P, 3, 3 * CH])
        banks = [k.ps(f"zc{i}", [P, 512]) for i in range(4)]
        rbanks = [k.ps(f"rc{i}", [P, 512]) for i in range(3)]
        nbank = k.ps("nc2", [P, 512])
        x_in, g_in, wg_in = (k.sem(n) for n in ("xT2_in", "g2_in", "wg_in"))
        gate_in, gate_exp, gate_chain, gate_ready, gate_stored, copied = (
            k.sem(n) for n in ("gate3_in", "gate3_exp", "gate3_chain", "gate3_ready", "gate3_stored", "copied3"))
        gs = k.sb("gs", [3 * CH, NQ, NB])
        gs_turned, gs_ready = k.sem("gs_turned"), k.sem("gs_ready")
        gl_done, gl_exp, gl_chain, gl_stored, xt_stored = (k.sem(n) for n in ("gl_done", "gl_exp", "gl_chain", "gl_stored", "xt2_stored"))
        norm = Norm(k, "2", xT, xn, gcol, nbank, hi=xh, lo=xl)
        out = Proj(k, "2", k.w_out_even, mixed.hi, mixed.lo, banks, [(4, 0, 0, None)], residual=xT)
        proj = Proj(k, "3", k.w_in_odd, xh, xl, banks, [(4, C_GP, Z2_GP, None), (1, 0, 0, None), (3, GW, GW, None), (1, CW, CW, 0), (2, CW + GW, CW + GW, GW)],
                    zt=k.z2, rows=k.kv2, row_banks=rbanks, after=out)
        with nc.Block() as block:
            @block.sync
            def _(sp):
                view = lambda a: a.rearrange("(k p) t -> p k t", p=P)
                mixed.sync(sp, k)
                sp.dma_start(gcol[:, :], k.norm_odd).then_inc(g_in, 16)
                out.sync(sp)
                sp.dma_start(wg[:, :, :], k.w_in_odd[:, C_GL:C_GL + 3 * CH].rearrange("(k p) n -> p k n", p=P)).then_inc(wg_in, 16)
                proj.sync(sp)
                sp.dma_start(view(k.xt), xT[:, :, :]).then_inc(xt_stored, 16)
                sp.dma_start(k.gates.rearrange("(t p) n -> p t n", p=P), gr[:, 0:2, :]).then_inc(gl_stored, 16)
                sp.wait_ge(gs_ready, 1)
                sp.dma_start(k.gates_s, gs[:, :, :]).then_inc(gl_stored, 16)
                sp.wait_ge(gl_stored, 32)
                sp.wait_ge(xt_stored, 16)
                sp.wait_ge(proj.z_stored, 16 * 12)
                sp.wait_ge(proj.rows_stored, 32 * 4)

            @block.scalar
            def _(act):
                mixed.act(act)
                out.act(act)
                norm.act(act)
                for t, m in enumerate((P, P, NS)):
                    act.wait_ge(gl_done, t + 1)
                    act.activation(gr[0:m, t, :], rbanks[t][0:m, 0:3 * CH], ACT.Exp, scale=-1.0).then_inc(gl_exp, 1)

                def gate_exps(act):
                    act.wait_ge(gate_in, 16)
                    act.activation(gate[:, :, :], mix[:, :, :], ACT.Exp, scale=-1.0).then_inc(gate_exp, 1)

                proj.act(act, {2: gate_exps})

            @block.gpsimd
            def _(pool):
                pool.dma_start(xT[:, :, :], k.xt.rearrange("(k p) t -> p k t", p=P)).then_inc(x_in, 16)
                pieces = k.cache_pieces[16:22]
                for n, p in enumerate(pieces):
                    pool.wait_ge(out.tile_done if n < 3 else proj.tile_done, 4 * n + 8 if n < 3 else 4 * (n - 3) + 8)
                    pool.dma_start(*p).then_inc(copied, 16)
                    if n == 5:
                        pool.wait_ge(proj.z_stored, 16 * 5)
                        pool.dma_start(mix[:, :, :], k.z2[Z2_GP:, :].rearrange("(k p) t -> p k t", p=P)).then_inc(gate_in, 16)
                pool.wait_ge(gate_ready, KT)
                pool.dma_start(k.gate.rearrange("(k p) t -> p k t", p=P), mix[:, :, :]).then_inc(gate_stored, 16)
                pool.wait_ge(gate_stored, 16)
                pool.wait_ge(copied, 16 * len(pieces))

            @block.tensor
            def _(pe):
                out.pe(pe, lambda e, q: e.wait_ge(mixed.ready, q + 1))
                norm.pe(pe)
                pe.wait_ge(wg_in, 16)
                pe.wait_ge(norm.ready, KT)
                for t, m in enumerate((P, P, NS)):
                    for j in range(KT):
                        for i, x in enumerate((xh[:, j, :].bitcast(F32), xl[:, j, :].bitcast(F32))):
                            ins = pe.matmul(rbanks[t][0:m, 0:3 * CH], x[:, t * P:t * P + m], wg[:, j, :],
                                            start=(j == 0 and i == 0), stop=(j == KT - 1 and i == 1))
                    ins.then_inc(gl_done, 1)
                pe.wait_ge(gl_chain, 6)
                pe.transpose(nbank[0:3 * CH, 0:NS], gr[0:NS, 2, :], k.ident[0:NS, 0:NS]).then_inc(gs_turned, 1)
                proj.pe(pe)

            @block.vector
            def _(dve):
                mixed.dve(dve)
                dve.wait_ge(x_in, 16)
                out.dve(dve)
                dve.wait_ge(out.z_ready, 20)
                dve.wait_ge(g_in, 16)
                norm.dve(dve, lambda e, t: None)
                link = Chain(dve, gl_chain)
                for t, m in enumerate((P, P, NS)):
                    dve.wait_ge(gl_exp, t + 1)
                    link(dve.tensor_scalar(gr[0:m, t, :], gr[0:m, t, :], 1.0, None, ALU.add))
                    link(dve.reciprocal(gr[0:m, t, :], gr[0:m, t, :]))
                dve.wait_ge(gs_turned, 1)
                dve.tensor_copy(gs[:, :, :], nbank[0:3 * CH, 0:NS].rearrange("p (b i) -> p i b", b=NB)).then_inc(gs_ready, 1)

                def gates(t):
                    dve.wait_ge(gate_exp, 1)
                    silu_tile(dve, k, gate_chain, mix, gate, mix, t).then_inc(gate_ready, 1)

                proj.dve(dve, beside={2: lambda n: gates(n), 3: lambda n: gates(n + 12)})


def block_final(nc, k):
    with k.scope():
        mixed = Mix(k, "4")
        xT = k.sb("xT4", [P, KT, T])
        xn = k.sb("xn4", [P, KT, T])
        gcol = k.sb("gcol4", [P, KT])
        yrow = k.sb("yrow", [P, 3, D])
        banks = [k.ps(f"zd{i}", [P, 512]) for i in range(4)]
        ybanks = [k.ps(f"yb{i}", [P, 512]) for i in range(3)]
        nbank = k.ps("nd", [P, 512])
        x_in, g_in = (k.sem(n) for n in ("xT4_in", "g4_in"))
        turned, y_ready, y_stored = (k.sem(n) for n in ("y_turned", "y_ready", "y_stored"))
        norm = Norm(k, "4", xT, xn, gcol, nbank)
        out = Proj(k, "4", k.w_out_odd, mixed.hi, mixed.lo, banks, [(4, 0, 0, None)], residual=xT)
        sizes = (P, P, NS)
        with nc.Block() as block:
            @block.sync
            def _(sp):
                mixed.sync(sp, k)
                sp.dma_start(gcol[:, :], k.final_norm).then_inc(g_in, 16)
                out.sync(sp)
                for t in range(3):
                    sp.wait_ge(y_ready, 4 * t + 4)
                    dst = k.out_y_p[t * P:(t + 1) * P, :] if t < 2 else k.out_y_s
                    sp.dma_start(dst, yrow[0:sizes[t], t, :]).then_inc(y_stored, 16)
                sp.wait_ge(y_stored, 48)

            @block.gpsimd
            def _(pool):
                pool.dma_start(xT[:, :, :], k.xt.rearrange("(k p) t -> p k t", p=P)).then_inc(x_in, 16)

            @block.scalar
            def _(act):
                mixed.act(act)
                out.act(act)
                norm.act(act)

            @block.tensor
            def _(pe):
                out.pe(pe, lambda e, q: e.wait_ge(mixed.ready, q + 1))
                norm.pe(pe)
                pe.wait_ge(norm.ready, KT)
                for n in range(12):
                    t, f = n // 4, n % 4
                    m = sizes[t]
                    if n >= 3:
                        pe.wait_ge(y_ready, n - 2)
                    for c in range(4):
                        ins = pe.transpose(ybanks[n % 3][0:m, c * P:(c + 1) * P], xn[:, 4 * f + c, t * P:t * P + m], k.ident[:, :])
                    ins.then_inc(turned, 1)

            @block.vector
            def _(dve):
                mixed.dve(dve)
                dve.wait_ge(x_in, 16)
                out.dve(dve)
                dve.wait_ge(out.z_ready, 20)
                dve.wait_ge(g_in, 16)
                norm.dve(dve, lambda e, t: None)
                for n in range(12):
                    t, f = n // 4, n % 4
                    m = sizes[t]
                    dve.wait_ge(turned, n + 1)
                    dve.tensor_copy(yrow[0:m, t, f * 512:(f + 1) * 512], ybanks[n % 3][0:m, :]).then_inc(y_ready, 1)


O_W, O_WN, O_S = 0, WIN, WIN + NQ
O_SN = O_S + PAST
O_C = O_SN + NQ
NSC = O_C + NCS


class Compress:

    def __init__(self, k, tag):
        self.k = k
        self.w1 = k.sb("cw1" + tag, [P, 2, CB, HD])
        self.w2 = k.sb("cw2" + tag, [P, 2, HD])
        self.pos = k.sb("cpos" + tag, [P, 2 * CB])
        self.b1 = k.sb("cb1" + tag, [P, 2])
        self.bias = k.sb("cbias" + tag, [P, 2])
        self.nbias = k.sb("cnbias" + tag, [P, 2])
        self.loaded, self.done, self.ready = (k.sem(n + tag) for n in ("cmp_in", "cmp_pos_done", "cmp_bias"))

    def sync(self, sp):
        for i in range(2):
            sp.dma_start(self.w1[:, i, :, :], self.k.cmp_w1[i].rearrange("l d e -> d l e")).then_inc(self.loaded, 16)
        sp.dma_start(self.w2[:, :, :], self.k.cmp_w2.rearrange("a e d -> e a d")).then_inc(self.loaded, 16)
        sp.dma_start(self.pos[:, :], self.k.cmp_pos).then_inc(self.loaded, 16)
        sp.dma_start(self.b1[:, :], self.k.cmp_b1).then_inc(self.loaded, 16)

    def pe(self, pe, bank):
        pe.wait_ge(self.loaded, 80)
        for i in range(2):
            for l in range(CB):
                ins = pe.matmul(bank[:, i:i + 1], self.w1[:, i, l, :], self.pos[:, i * CB + l:i * CB + l + 1], start=(l == 0), stop=(l == CB - 1))
        ins.then_inc(self.done, 1)

    def dve(self, dve, bank):
        dve.wait_ge(self.done, 1)
        link = Chain(dve, self.ready)
        link(dve.tensor_tensor(self.bias[:, :], bank[:, 0:2], self.b1[:, :], ALU.add))
        link(dve.tensor_scalar(self.nbias[:, :], self.bias[:, :], -1.0, None, ALU.mult))


def block_sample_c(nc, k):
    with k.scope():
        pk = k.sb("pk", [P, NPG, 3 * CKV])
        pv = k.sb("pv", [P, NPG, CKV])
        win = k.sb("win", [P, WIN // P, 2 * CKV])
        xt = k.sb("xtc", [P, 4, PAST])
        cmp = Compress(k, "s")
        qs = k.sb("qsc", [P, CH, NS])
        kn = k.sb("knc", [P, 2, CG, NS])
        vn = k.sb("vnc", [NQ, 2, CKV])
        qc = k.sb("qc", [P, CG, P])
        ktt = k.sb("kttc", [P, 2, 4, P])
        ptt = k.sb("pttc", [P, 2, 4, P])
        bias = k.sb("bias_sc", [P, O_C])
        s = k.sb("s_sc", [P, NSC])
        hh = k.sb("hh", [P, 2, CG * NCS])
        he = k.sb("he", [P, CG * NCS])
        kc = k.sb("kc", [P, CG * NCS])
        vc = k.sb("vc", [NCS, CKV])
        pct = k.sb("pct", [NCS, P])
        t1 = k.sb("t1", [P, NSEL])
        rank = k.sb("rank", [P, 3, NSEL])
        m8 = k.sb("m8", [P, 2, 8])
        st = k.sb("st_sc", [P, 3, 4])
        ov = k.sb("ov", [NCS, NSEL])
        hs = k.sb("hs", [P, P])
        gt = k.sb("gt", [P, 3, NB])
        oc = k.sb("oc", [P, HD])
        orow = k.sb("orowc", [P, HD])
        ot = k.sb("otc", [P, CH, NS])
        xb = [k.ps(f"xb{i}", [P, 512]) for i in range(2)]
        sb_ = [k.ps(f"scb{i}", [P, 512]) for i in range(2)]
        hb, mb, m2, ob = (k.ps(n, [P, 512]) for n in ("hb", "mb", "m2", "ob"))
        MC, MT1, MIMP = 16, 144, 184

        NPIECE = 4
        pt_in = k.sem("pt_in")
        pk_in = [k.sem(f"pk_in{i}") for i in range(NPIECE)]
        pv_in = [k.sem(f"pv_in{i}") for i in range(NPIECE)]
        win_in, vn_in, small_in, bias_in, gt_in = (k.sem(n) for n in ("win_in", "vnc_in", "smallc_in", "biasc_in", "gt_in"))
        zeroed, scaled, qc_ready, turned, evac_a, evac_d, score_q, s_evac = (
            k.sem(n) for n in ("zc_set", "qsc_scaled", "qc_ready", "c_turns", "c_evac_a", "c_evac_d", "c_scoreq", "c_sevac"))
        h_done, h_exp, hh_ready, w2_done, kc_ready, cs_done, new_done = (
            k.sem(n) for n in ("h_done", "h_exp", "hh_ready", "w2_done", "kc_ready", "cs_done", "new_done"))
        max_c, exp_c, pc_ready, pct_done, pct_ready, t1_done, t1_ready, imp_done = (
            k.sem(n) for n in ("max_c", "exp_c", "pc_ready", "pct_done", "pct_ready", "t1_done", "t1_ready", "imp_done"))
        max_w, exp_w, pw_ready, max_s, exp_s, ps_ready = (k.sem(n) for n in ("max_w", "exp_w", "pw_ready", "max_s", "exp_s", "ps_ready"))
        imp_seen = k.sem("imp_seen")
        chain, pv_q, o_evac, o_turned, o_ready, o_stored, rows_out, copied = (
            k.sem(n) for n in ("sc_chain", "pv_q", "oc_evac", "oc_turned", "oc_ready", "oc_stored", "rows_out", "copied6"))
        TX, TW, TS, TP = 0, NPG, NPG + 2, NPG + 10
        NT = TP + 6
        CHAIN = 21

        with nc.Block() as block:
            @block.sync
            def _(sp):
                cmp.sync(sp)
                for i in range(4):
                    sp.dma_start(qs[:, 4 * i:4 * i + 4, :], k.z2[i * 512:(i + 1) * 512, NP:T].rearrange("(h d) t -> d h t", d=HD)).then_inc(small_in, 16)
                for i, c in enumerate((C_KS, C_KW)):
                    sp.dma_start(kn[:, i, :, :], k.z2[c:c + CKV, NP:T].rearrange("(g d) t -> d g t", d=HD)).then_inc(small_in, 16)
                sp.dma_start(ov[:, :], k.c_overlap).then_inc(small_in, 16)
                sp.dma_start(hs[:, :], k.c_hsum).then_inc(small_in, 16)

                def load(b, first=False):
                    def pages(dst, sems, lo, hi, frees, free_at):
                        for pg in range(NPG):
                            n = pg * NPIECE // NPG
                            if not first and pg % (NPG // NPIECE) == 0:
                                sp.wait_ge(frees, free_at(n))
                                settle(sp, k)
                            page = sp.value_load(k.page_table[bass.ds(b, 1), pg:pg + 1], min_val=0, max_val=k.cache_c_kv.shape[0] - 1)
                            sp.dma_start(dst[:, pg, :], k.cache_c_kv[bass.ds(page, 1)].rearrange("a t c g d -> (a t) (c g d)")[:, lo:hi]
                                         ).then_inc(sems[n], 16)

                    pages(pk, pk_in, 0, 3 * CKV, turned, lambda n: b * NT - NT + (TS + 2 * n + 2))
                    sp.dma_start(win[:, :, :], k.cache_c_win[bass.ds(b, 1)].rearrange("a (r p) c g d -> p (a r) (c g d)", p=P)).then_inc(win_in, 16)
                    if not first:
                        sp.wait_ge(pv_q, b * 6)
                    sp.dma_start(vn[:, 0, :], k.kv2[bass.ds(b * NQ + NP, NQ), 3 * CKV:4 * CKV]).then_inc(vn_in, 16)
                    sp.dma_start(vn[:, 1, :], k.kv2[bass.ds(b * NQ + NP, NQ), 5 * CKV:6 * CKV]).then_inc(vn_in, 16)
                    pages(pv, pv_in, 3 * CKV, 4 * CKV, pv_q, lambda n: b * 6 - 6 + (2 + n))

                load(0, True)
                with sp.Fori(1, NB) as b:
                    sp.wait_ge(pv_q, b * 6 - 5)
                    load(b)
                sp.wait_ge(o_ready, NB)
                sp.dma_start(k.mt[:, NP:T].rearrange("(h d) t -> d h t", d=HD), ot[:, :, :]).then_inc(o_stored, 16)
                sp.wait_ge(o_stored, 16)

            @block.gpsimd
            def _(pool):
                link = Chain(pool, zeroed)
                link(pool.memset(qc[:, :, :], 0.0))
                link(pool.memset(rank[:, 0, :], 1.0e30))
                for g in range(CG):
                    for i in range(NQ):
                        r = (g * NQ + i) * CHG
                        pool.dma_start(bias[r:r + CHG, O_S:O_S + PAST + NQ], k.tab_hc[g * CHG:(g + 1) * CHG, NQ - 1 - i:NQ - 1 - i + PAST + NQ]).then_inc(bias_in, 16)
                        pool.dma_start(bias[r:r + CHG, O_W:O_W + WIN + NQ], k.tab_hw[g * CHG:(g + 1) * CHG, NQ - 1 - i:NQ - 1 - i + WIN + NQ]).then_inc(bias_in, 16)
                    for br in range(3):
                        pool.dma_start(gt[g * 64:(g + 1) * 64, br, :],
                                       dram_ap(k.gates_s, (br * CH + g * CHG) * NS, [(NB, NQ), (NS, CHG), (1, NB)])).then_inc(gt_in, 16)
                n = 0
                for dst, c0, c1 in ((k.out_rows_p, 0, 4 * CKV), (k.out_win_p, 4 * CKV, 6 * CKV)):
                    pool.dma_start(dst.rearrange("t c g d -> t (c g d)"), k.kv2[0:NP, c0:c1]).then_inc(rows_out, 16)
                    n += 1
                pool.dma_start(k.out_rows_s.rearrange("b t c g d -> (b t) (c g d)"), k.kv2[NP:T, 0:4 * CKV]).then_inc(rows_out, 16)
                n += 1
                for b in range(NB):
                    pool.dma_start(k.out_win_s[b, 0:WIN - NQ].rearrange("t c g d -> t (c g d)"), k.cache_c_win[b, NQ:WIN].rearrange("t c g d -> t (c g d)")).then_inc(rows_out, 16)
                    pool.dma_start(k.out_win_s[b, WIN - NQ:WIN].rearrange("t c g d -> t (c g d)"), k.kv2[NP + b * NQ:NP + (b + 1) * NQ, 4 * CKV:]).then_inc(rows_out, 16)
                    n += 2
                pool.wait_ge(scaled, 1)

                def fill_q(b):
                    wait(pool, score_q, b * 10)
                    wait(pool, cs_done, b * 1)
                    for g in range(CG):
                        pool.tensor_copy(qc[:, g, g * 64:(g + 1) * 64].rearrange("p (i h) -> p h i", h=CHG),
                                         qs[:, g * CHG:(g + 1) * CHG, bass.ds(b * NQ, NQ)]).then_inc(qc_ready, 1)

                def copy_kept(b):
                    row = 2 * NH * HD
                    for g, part, parts, m in ((1, 0, 1, 2 * (GROUPS[1][0] - NQ)), (2, 3, 4, 816)):
                        keep = (GROUPS[g][0] - NQ) // parts
                        dst, src = (a.rearrange("b t a h d -> b (t a h d)")[bass.ds(b, 1), (lo + part * keep) * row:(lo + (part + 1) * keep) * row]
                                    .rearrange("b (m n) -> (b m) n", m=m) for a, lo in ((k.out_a_s[g], 0), (k.cache_a[g], NQ)))
                        pool.dma_start(dst, src).then_inc(copied, 16)

                fill_q(0)
                copy_kept(0)
                with pool.Fori(1, NB) as b:
                    fill_q(b)
                    copy_kept(b)
                pool.wait_ge(copied, 2 * 16 * NB)
                pool.wait_ge(rows_out, 16 * n)

            def evac(eng, b, q, copy, sem):
                eng.wait_ge(turned, b * NT + (q + 1))
                bank = xb[q % 2]
                if q < TW:
                    copy(xt[:, :, q * P:(q + 1) * P], bank[:, :].rearrange("p (c n) -> p c n", c=4)).then_inc(sem, 1)
                elif q < TP:
                    if q >= TW + 2:
                        eng.wait_ge(score_q, b * 10 + (q - TW - 1))
                    copy(ktt[:, q % 2, :, :], bank[:, :].rearrange("p (c n) -> p c n", c=4)).then_inc(sem, 1)
                else:
                    if q >= TP + 2:
                        eng.wait_ge(pv_q, b * 6 + (q - TP - 1))
                    if q < TP + 5:
                        copy(ptt[:, q % 2, :, :], bank[:, :].rearrange("p (c n) -> p c n", c=4)).then_inc(sem, 1)
                    else:
                        copy(ptt[0:NQ, q % 2, 0:2, :], bank[0:NQ, 0:2 * P].rearrange("p (c n) -> p c n", c=2)).then_inc(sem, 1)

            @block.scalar
            def _(act):
                act.wait_ge(cmp.ready, 2)

                def one(b):
                    def ev(q):
                        evac(act, b, q, act.copy, evac_a)

                    for q in range(0, TW, 2):
                        ev(q)
                    for i in range(2):
                        act.wait_ge(h_done, b * 2 + (i + 1))
                        if i:
                            act.wait_ge(hh_ready, b * 2 + i)
                        else:
                            wait(act, hh_ready, b * 2)
                        act.activation(he[:, :], (hb, m2)[i][:, 0:CG * NCS], ACT.Exp, bias=cmp.nbias[:, i:i + 1], scale=-1.0).then_inc(h_exp, 1)
                    for q in (16, 18, 20, 22):
                        ev(q)
                    act.wait_ge(max_c, b + 1)
                    act.activation(s[:, O_C:], mb[:, MC:MC + NCS], ACT.Exp, bias=st[:, 0, 1:2], accum_out=st[:, 0, 2:3]).then_inc(exp_c, 1)
                    ev(24)
                    act.wait_ge(max_w, b + 1)
                    act.activation(s[:, O_W:O_S], s[:, O_W:O_S], ACT.Exp, bias=st[:, 1, 1:2], accum_out=st[:, 1, 2:3]).then_inc(exp_w, 1)
                    ev(26)
                    act.wait_ge(max_s, b + 1)
                    act.activation(s[:, O_S:O_C], s[:, O_S:O_C], ACT.Exp, bias=st[:, 2, 1:2], accum_out=st[:, 2, 2:3]).then_inc(exp_s, 1)
                    ev(28)
                    ev(30)

                one(0)
                with act.Fori(1, NB) as b:
                    one(b)

            @block.tensor
            def _(pe):
                cmp.pe(pe, hb)
                pe.wait_ge(cmp.ready, 2)
                pe.wait_ge(small_in, 128)

                def turn(b, q):
                    if q >= 2:
                        pe.wait_ge((evac_a, evac_d)[q % 2], b * (NT // 2) + q // 2)
                    else:
                        wait(pe, (evac_a, evac_d)[q % 2], b * (NT // 2))
                    if q < TW:
                        if q % (NPG // NPIECE) == 0:
                            pe.wait_ge(pk_in[q * NPIECE // NPG], b * 64 + 64)
                        src = [pk[:, q, j * P:(j + 1) * P] for j in range(4)]
                    elif q < TS:
                        if q == TW:
                            pe.wait_ge(win_in, b * 16 + 16)
                        src = [win[:, 2 * (q - TW) + j, g * P:(g + 1) * P] for j in range(2) for g in range(CG)]
                    elif q < TP:
                        src = [pk[:, 2 * (q - TS) + j, 2 * CKV + g * P:2 * CKV + (g + 1) * P] for j in range(2) for g in range(CG)]
                    elif q == TP:
                        pe.wait_ge(pw_ready, b + 1)
                        src = [s[:, O_W + j * P:O_W + (j + 1) * P] for j in range(4)]
                    elif q < TP + 5:
                        if q == TP + 1:
                            pe.wait_ge(ps_ready, b + 1)
                        o = O_S + (q - TP - 1) * 4 * P
                        src = [s[:, o + j * P:o + (j + 1) * P] for j in range(4)]
                    else:
                        settle(pe, k)
                        for j, o in enumerate((O_SN, O_WN)):
                            ins = pe.transpose(xb[q % 2][0:NQ, j * P:(j + 1) * P], s[:, o:o + NQ], k.ident[:, :])
                        ins.then_inc(turned, 1)
                        return
                    for j in range(4):
                        ins = pe.transpose(xb[q % 2][:, j * P:(j + 1) * P], src[j], k.ident[:, :])
                    ins.then_inc(turned, 1)

                def score(b, n):
                    q = TW + n
                    fill = n // 2
                    pe.wait_ge((evac_a, evac_d)[q % 2], b * (NT // 2) + (q // 2 + 1))
                    if n % 2 == 0:
                        if fill >= 2:
                            pe.wait_ge(s_evac, b * 5 + (fill - 1))
                        else:
                            wait(pe, s_evac, b * 5)
                    for j in range(2):
                        o = (n % 2) * 2 * P + j * P
                        for g in range(CG):
                            ins = pe.matmul(sb_[fill % 2][:, o:o + P], qc[:, g, :], ktt[:, q % 2, 2 * j + g, :], start=(g == 0), stop=(g == CG - 1))
                    ins.then_inc(score_q, 1)

                def values(b, n):
                    q = TP + n
                    pe.wait_ge((evac_a, evac_d)[q % 2], b * (NT // 2) + (q // 2 + 1))
                    if 1 <= n <= 4:
                        pe.wait_ge(pv_in[n - 1], b * 64 + 64)
                    if n == 5:
                        pe.wait_ge(vn_in, b * 32 + 32)
                    for j in range(4 if n < 5 else 2):
                        if n == 0:
                            w, v = ptt[:, q % 2, j, :], win[:, j, CKV:2 * CKV]
                        elif n < 5:
                            w, v = ptt[:, q % 2, j, :], pv[:, (n - 1) * 4 + j, :]
                        else:
                            w, v = ptt[0:NQ, q % 2, j, :], vn[:, j, :]
                        ins = pe.matmul(ob[:, CKV:2 * CKV], w, v, start=(n == 0 and j == 0), stop=(n == 5 and j == 1))
                    ins.then_inc(pv_q, 1)

                def one(b):
                    for q in range(TW):
                        turn(b, q)
                    for i in range(2):
                        if i == 0:
                            pe.wait_ge(evac_a, b * (NT // 2) + TW // 2)
                            pe.wait_ge(evac_d, b * (NT // 2) + TW // 2)
                            wait(pe, o_ready, b * 1)
                        for l in range(CB):
                            ins = pe.matmul((hb, m2)[i][:, 0:CG * NCS], cmp.w1[:, i, l, :],
                                            xt[:, 2 * i:2 * i + 2, l:l + CS * (NCS - 1) + 1:CS], start=(l == 0), stop=(l == CB - 1))
                        ins.then_inc(h_done, 1)
                    turn(b, TW)
                    turn(b, TW + 1)
                    pe.wait_ge(qc_ready, b * 2 + 2)
                    wait(pe, imp_seen, b * 1)
                    for i, o in ((1, 0), (0, NQ)):
                        for g in range(CG):
                            ins = pe.matmul(mb[:, o:o + NQ], qc[:, g, :], kn[:, i, g, bass.ds(b * NQ, NQ)], start=(g == 0), stop=(g == CG - 1))
                    ins.then_inc(new_done, 1)
                    for n in range(10):
                        score(b, n)
                        if n == 3:
                            pe.wait_ge(hh_ready, b * 2 + 2)
                            pe.matmul(hb[:, 0:CG * NCS], cmp.w2[:, 0, :], hh[:, 0, :], start=True, stop=True)
                            for g in range(CG):
                                ins = pe.matmul(hb[0:NCS, CG * NCS + g * HD:CG * NCS + (g + 1) * HD], hh[:, 1, g * NCS:(g + 1) * NCS], cmp.w2[:, 1, :], start=True, stop=True)
                            ins.then_inc(w2_done, 1)
                        if n == 5:
                            pe.wait_ge(kc_ready, b * 2 + 2)
                            for g in range(CG):
                                ins = pe.matmul(mb[:, MC:MC + NCS], qc[:, g, :], kc[:, g * NCS:(g + 1) * NCS], start=(g == 0), stop=(g == CG - 1))
                            ins.then_inc(cs_done, 1)
                        if n + 2 < 10:
                            turn(b, TW + n + 2)
                    pe.wait_ge(pc_ready, b + 1)
                    settle(pe, k)
                    pe.transpose(m2[0:NCS, 0:P], s[:, O_C:], k.ident[:, :]).then_inc(pct_done, 1)
                    turn(b, TP)
                    pe.wait_ge(pct_ready, b + 1)
                    pe.matmul(mb[:, MT1:MT1 + NSEL], pct[:, :], ov[:, :], start=True, stop=True).then_inc(t1_done, 1)
                    wait(pe, o_evac, b * 2)
                    pe.matmul(ob[:, 0:CKV], pct[:, :], vc[:, :], start=True, stop=True)
                    pe.wait_ge(t1_ready, b + 1)
                    pe.matmul(mb[:, MIMP:MIMP + NSEL], hs[:, :], t1[:, :], start=True, stop=True).then_inc(imp_done, 1)
                    values(b, 0)
                    turn(b, TP + 1)
                    for n in range(1, 6):
                        if n < 5:
                            turn(b, TP + n + 1)
                        values(b, n)
                    pe.wait_ge(o_evac, b * 2 + 2)
                    settle(pe, k)
                    pe.transpose(m2[:, 0:P], orow[:, :], k.ident[:, :]).then_inc(o_turned, 1)

                one(0)
                with pe.Fori(1, NB) as b:
                    one(b)

            @block.vector
            def _(dve):
                cmp.dve(dve, hb)
                dve.wait_ge(small_in, 128)
                dve.tensor_scalar(qs[:, :, :], qs[:, :, :], SCALE, None, ALU.mult).then_inc(scaled, 1)
                dve.wait_ge(zeroed, 2)
                dve.wait_ge(bias_in, 16 * 32)
                dve.wait_ge(gt_in, 16 * 6)

                def one(b):
                    link = Chain(dve, chain, b * CHAIN)

                    def ev(q):
                        evac(dve, b, q, dve.tensor_copy, evac_d)

                    def hidden(i):
                        dve.wait_ge(h_exp, b * 2 + (i + 1))
                        wait(dve, w2_done, b * 1)
                        link(dve.tensor_scalar(he[:, :], he[:, :], 1.0, None, ALU.add))
                        link(dve.reciprocal(he[:, :], he[:, :]))
                        dve.scalar_tensor_tensor(hh[:, i, :], (hb, m2)[i][:, 0:CG * NCS], cmp.bias[:, i:i + 1], he[:, :],
                                                 ALU.add, ALU.mult).then_inc(hh_ready, 1)

                    def fill(f):
                        dve.wait_ge(score_q, b * 10 + (2 * f + 2))
                        o = O_W if f == 0 else O_S + (f - 1) * 4 * P
                        dve.tensor_tensor(s[:, o:o + 4 * P], sb_[f % 2][:, :], bias[:, o:o + 4 * P], ALU.add).then_inc(s_evac, 1)

                    for q in range(1, TW, 2):
                        ev(q)
                    hidden(0)
                    ev(17)
                    hidden(1)
                    fill(0)
                    dve.wait_ge(new_done, b + 1)
                    link(dve.tensor_tensor(s[:, O_WN:O_WN + NQ], mb[:, 0:NQ], bias[:, O_WN:O_WN + NQ], ALU.add))
                    link(dve.tensor_tensor(s[:, O_SN:O_SN + NQ], mb[:, NQ:2 * NQ], bias[:, O_SN:O_SN + NQ], ALU.add))
                    ev(19)
                    fill(1)
                    dve.wait_ge(w2_done, b + 1)
                    dve.tensor_copy(kc[:, :], hb[:, 0:CG * NCS]).then_inc(kc_ready, 1)
                    dve.tensor_copy(vc[:, :], hb[0:NCS, CG * NCS:CG * NCS + CKV]).then_inc(kc_ready, 1)
                    ev(21)
                    dve.wait_ge(s_evac, b * 5 + 1)
                    link(dve.tensor_reduce(st[:, 1, 0:1], s[:, O_W:O_S], AX, ALU.max))
                    dve.tensor_scalar(st[:, 1, 1:2], st[:, 1, 0:1], -1.0, None, ALU.mult).then_inc(max_w, 1)
                    fill(2)
                    dve.wait_ge(cs_done, b + 1)
                    link(dve.tensor_reduce(st[:, 0, 0:1], mb[:, MC:MC + NCS], AX, ALU.max))
                    dve.tensor_scalar(st[:, 0, 1:2], st[:, 0, 0:1], -1.0, None, ALU.mult).then_inc(max_c, 1)
                    ev(23)
                    fill(3)
                    dve.wait_ge(exp_c, b + 1)
                    link(dve.reciprocal(st[:, 0, 3:4], st[:, 0, 2:3]))
                    dve.tensor_scalar(s[:, O_C:], s[:, O_C:], st[:, 0, 3:4], None, ALU.mult).then_inc(pc_ready, 1)
                    ev(25)
                    fill(4)
                    dve.wait_ge(exp_w, b + 1)
                    link(dve.reciprocal(st[:, 1, 3:4], st[:, 1, 2:3]))
                    dve.tensor_scalar(s[:, O_W:O_S], s[:, O_W:O_S], st[:, 1, 3:4], gt[:, 2, bass.ds(b, 1)],
                                      ALU.mult, ALU.mult).then_inc(pw_ready, 1)
                    dve.wait_ge(pct_done, b + 1)
                    dve.tensor_copy(pct[:, :], m2[0:NCS, 0:P]).then_inc(pct_ready, 1)
                    dve.wait_ge(t1_done, b + 1)
                    dve.tensor_copy(t1[:, :], mb[:, MT1:MT1 + NSEL]).then_inc(t1_ready, 1)
                    dve.wait_ge(imp_done, b + 1)
                    dve.tensor_copy(rank[:, 0, 1:NSEL - 2], mb[:, MIMP + 1:MIMP + NSEL - 2]).then_inc(imp_seen, 1)
                    dve.wait_ge(imp_seen, b + 1)
                    for i in range(2):
                        settle(dve, k)
                        link(dve.max(m8[:, i, :], rank[:, i, :]))
                        settle(dve, k)
                        link(dve.match_replace(rank[:, i + 1, :], m8[:, i, :], rank[:, i, :], -1.0))
                    link(dve.tensor_scalar(rank[:, 2, :], rank[:, 2, :], 0.0, MASK, ALU.is_ge, ALU.mult))
                    link(dve.tensor_reduce(st[:, 2, 0:1], s[:, O_SN:O_SN + NQ], AX, ALU.max))
                    dve.wait_ge(s_evac, b * 5 + 5)
                    settle(dve, k)
                    sv = s[:, O_S:O_S + PAST].rearrange("p (n c) -> p n c", c=SELB)
                    link(dve.tensor_tensor_reduce(sv, sv, rank[:, 2, 0:NSEL - 1].unsqueeze(2).broadcast_to([P, NSEL - 1, SELB]), 1.0,
                                                  st[:, 2, 0:1], ALU.add, ALU.max, st[:, 2, 1:2]))
                    link(dve.tensor_scalar(st[:, 2, 1:2], st[:, 2, 1:2], -1.0, None, ALU.mult))
                    dve.sem_inc(max_s, 1)
                    dve.wait_ge(exp_s, b + 1)
                    link(dve.reciprocal(st[:, 2, 3:4], st[:, 2, 2:3]))
                    dve.tensor_scalar(s[:, O_S:O_C], s[:, O_S:O_C], st[:, 2, 3:4], gt[:, 1, bass.ds(b, 1)],
                                      ALU.mult, ALU.mult).then_inc(ps_ready, 1)
                    for q in (27, 29, 31):
                        ev(q)
                    dve.wait_ge(pv_q, b * 6 + 6)
                    for g in range(CG):
                        rows = slice(g * 64, (g + 1) * 64)
                        link(dve.tensor_scalar(oc[rows, :], ob[rows, g * HD:(g + 1) * HD], gt[rows, 0, bass.ds(b, 1)], None, ALU.mult))
                        dve.tensor_tensor(orow[rows, :], ob[rows, CKV + g * HD:CKV + (g + 1) * HD], oc[rows, :], ALU.add).then_inc(o_evac, 1)
                    dve.wait_ge(o_turned, b + 1)
                    dve.tensor_copy(ot[:, :, bass.ds(b * NQ, NQ)].rearrange("p (g h) i -> p g h i", g=CG),
                                    m2[:, 0:P].rearrange("p (g i h) -> p g h i", g=CG, h=CHG)).then_inc(o_ready, 1)
                    assert link.n == CHAIN, link.n

                one(0)
                with dve.Fori(1, NB) as b:
                    one(b)


def block_prompt_c(nc, k):
    with k.scope():
        U = 2
        cmp = Compress(k, "p")
        xk = k.sb("xkp", [P, 4, NP])
        kk = k.sb("kkp", [P, 2, CG, NP])
        v = k.sb("vvp", [P, 2, 2, CKV])
        q = k.sb("qpc", [P, U, NP])
        tab = k.sb("tpc", [P, U, NP])
        cmask = k.sb("cmask", [P, 2, NCP])
        gr = k.sb("gpc", [P, 2, 3, CH])
        hh = k.sb("hhp", [P, 2, CG * NCP])
        he = k.sb("hep", [P, CG * NCP])
        kc = k.sb("kcp", [P, CG * NCP])
        vc = k.sb("vcp", [NCP, CKV])
        sc = k.sb("scp", [P, 2, 3, NP])
        pt = k.sb("ptpc", [P, 2, 5, P])
        st = k.sb("stpc", [P, 2, 4, 3])
        ot = k.sb("otpc", [P, U, NP])
        sps = [k.ps(f"spc{i}", [P, 1024]) for i in range(2)]
        tps = [k.ps(f"tpp{i}", [P, 512]) for i in range(2)]
        ops = [k.ps(f"opc{i}", [P, 512]) for i in range(2)]
        in_, kv_in, gates_in = k.sem("pc_in"), k.sem("pc_kv_in"), k.sem("pc_gates_in")
        h_done, h_exp, hh_ready, w2_done, kc_ready = (k.sem(n) for n in ("hp_done", "hp_exp", "hhp_ready", "w2p_done", "kcp_ready"))
        loaded = [k.sem(f"pc_loaded{u}") for u in range(U)]
        stored = [k.sem(f"pc_stored{u}") for u in range(U)]
        scaled, scored, max_done, exp_done, p_ready, chain, turned, pt_ready, pv_done, o_ready = (
            k.sem(n) for n in ("pc_scaled", "pc_scored", "pc_max", "pc_exp", "pc_p", "pc_chain", "pc_turned", "pc_pt", "pc_pv", "pc_o"))
        copied = k.sem("copied7")
        HG = CHG // U
        LINKS = 2 * U * 6

        def rounds():
            return [(g, g * HG) for g in range(CG)]

        with nc.Block() as block:
            @block.sync
            def _(sp):
                cmp.sync(sp)
                sp.dma_start(xk[:, :, :], k.z2[C_KC:C_KC + 2 * CKV, 0:NP].rearrange("(c p) t -> p c t", p=P)).then_inc(in_, 16)
                for i, c in enumerate((C_KS, C_KW)):
                    sp.dma_start(kk[:, i, :, :], k.z2[c:c + CKV, 0:NP].rearrange("(g d) t -> d g t", d=HD)).then_inc(kv_in, 16)
                for i, c in enumerate((3 * CKV, 5 * CKV)):
                    sp.dma_start(v[:, :, i, :], k.kv2[0:NP, c:c + CKV].rearrange("(t p) n -> p t n", p=P)).then_inc(kv_in, 16)
                sp.dma_start(cmask[:, :, :], k.c_cmask).then_inc(gates_in, 16)
                sp.dma_start(gr[:, :, :, :].rearrange("p t r h -> p t (r h)"), k.gates.rearrange("(t p) n -> p t n", p=P)).then_inc(gates_in, 16)
                for g, g0 in rounds():
                    with sp.Fori(g0, g0 + HG) as it:
                        for u in range(U):
                            sp.wait_ge(pv_done, it * (2 * U) + (2 * u + 2))
                            sp.dma_start(q[:, u, :], k.z2[bass.ds((it * U + u) * HD, HD), 0:NP]).then_inc(loaded[u], 16)
                            sp.dma_start(tab[:, u, :], k.toe_c[bass.ds(it * U + u, 1)].rearrange("a p n -> (a p) n")).then_inc(loaded[u], 16)

            @block.gpsimd
            def _(pool):
                for n, p in enumerate(k.cache_pieces[22:]):
                    pool.wait_ge(pv_done, 2 * U + 2 * n + 1)
                    pool.dma_start(*p).then_inc(copied, 16)
                pool.wait_ge(copied, 16 * len(k.cache_pieces[22:]))

            @block.scalar
            def _(act):
                for u in range(U):
                    act.sem_inc(stored[u], 16)
                act.wait_ge(cmp.ready, 2)
                for i in range(2):
                    act.wait_ge(h_done, i + 1)
                    wait(act, hh_ready, i)
                    act.activation(he[:, :], (tps[1], sps[0])[i][:, 0:CG * NCP], ACT.Exp, bias=cmp.nbias[:, i:i + 1], scale=-1.0).then_inc(h_exp, 1)
                for g, g0 in rounds():
                    with act.Fori(g0, g0 + HG) as it:
                        for u in range(U):
                            for qb in range(2):
                                n = 2 * u + qb
                                nk = P * (qb + 1)
                                act.wait_ge(max_done, it * (2 * U) + (n + 3))
                                for r, w in enumerate((NCP, nk, nk)):
                                    act.activation(sc[:, qb, r, 0:w], sc[:, qb, r, 0:w], ACT.Exp, bias=st[:, qb, 1, r:r + 1],
                                                   accum_out=st[:, qb, 2, r:r + 1]).then_inc(exp_done, 1)
                            act.wait_ge(o_ready, it * (2 * U) + (2 * u + 4))
                            act.dma_start(k.mt[bass.ds((it * U + u) * HD, HD), 0:NP], ot[:, u, :]).then_inc(stored[u], 16)
                for u in range(U):
                    act.wait_ge(stored[u], 16 * (CH // U) + 16)

            @block.tensor
            def _(pe):
                pe.sem_inc(pv_done, 2 * U)
                cmp.pe(pe, tps[0])
                pe.wait_ge(in_, 16)
                for i in range(2):
                    for l in range(CB):
                        ins = pe.matmul((tps[1], sps[0])[i][:, 0:CG * NCP], cmp.w1[:, i, l, :],
                                        xk[:, 2 * i:2 * i + 2, l:l + CS * (NCP - 1) + 1:CS], start=(l == 0), stop=(l == CB - 1))
                    ins.then_inc(h_done, 1)
                pe.wait_ge(hh_ready, 2)
                pe.matmul(ops[0][:, 0:CG * NCP], cmp.w2[:, 0, :], hh[:, 0, :], start=True, stop=True)
                for g in range(CG):
                    ins = pe.matmul(ops[1][0:NCP, g * HD:(g + 1) * HD], hh[:, 1, g * NCP:(g + 1) * NCP], cmp.w2[:, 1, :], start=True, stop=True)
                ins.then_inc(w2_done, 1)
                pe.wait_ge(kc_ready, 2)
                pe.wait_ge(kv_in, 64)
                for g, g0 in rounds():
                    with pe.Fori(g0, g0 + HG) as it:
                        for u in range(U):
                            pe.wait_ge(scaled, it * U + (u + 1))
                            for qb in range(2):
                                n = 2 * u + qb
                                nk = P * (qb + 1)
                                qq = q[:, u, qb * P:(qb + 1) * P]
                                pe.wait_ge(max_done, it * (2 * U) + (n + 1))
                                pe.matmul(sps[qb][:, 0:NCP], qq, kc[:, g * NCP:(g + 1) * NCP], start=True, stop=True)
                                pe.matmul(sps[qb][:, 16:16 + nk], qq, kk[:, 0, g, 0:nk], start=True, stop=True)
                                pe.matmul(sps[qb][:, 512:512 + nk], qq, kk[:, 1, g, 0:nk], start=True, stop=True).then_inc(scored, 1)
                            for qb in range(2):
                                n = 2 * u + qb
                                pe.wait_ge(p_ready, it * (2 * U) + (n + 1))
                                settle(pe, k)
                                pe.transpose(tps[0][0:NCP, 0:P], sc[:, qb, 0, 0:NCP], k.ident[:, :])
                                for h in range(qb + 1):
                                    ins = pe.transpose(tps[0][:, (1 + h) * P:(2 + h) * P], sc[:, qb, 1, h * P:(h + 1) * P], k.ident[:, :])
                                ins.then_inc(turned, 1)
                                for h in range(qb + 1):
                                    ins = pe.transpose(tps[1][:, h * P:(h + 1) * P], sc[:, qb, 2, h * P:(h + 1) * P], k.ident[:, :])
                                ins.then_inc(turned, 1)
                                pe.wait_ge(pt_ready, it * (6 * U) + (6 * u + 3 * qb + 3))
                                pe.wait_ge(o_ready, it * (2 * U) + (n + 1))
                                pe.matmul(ops[qb][:, 0:P], vc[:, g * HD:(g + 1) * HD], pt[0:NCP, qb, 0, :], start=True, stop=False)
                                for r in range(2):
                                    for h in range(qb + 1):
                                        ins = pe.matmul(ops[qb][:, 0:P], v[:, h, r, g * HD:(g + 1) * HD], pt[:, qb, 1 + 2 * r + h, :],
                                                        start=False, stop=(r == 1 and h == qb))
                                ins.then_inc(pv_done, 1)

            @block.vector
            def _(dve):
                dve.sem_inc(max_done, 2)
                dve.sem_inc(o_ready, 2)
                cmp.dve(dve, tps[0])
                link = Chain(dve, chain)
                for i in range(2):
                    dve.wait_ge(h_exp, i + 1)
                    link(dve.tensor_scalar(he[:, :], he[:, :], 1.0, None, ALU.add))
                    link(dve.reciprocal(he[:, :], he[:, :]))
                    dve.scalar_tensor_tensor(hh[:, i, :], (tps[1], sps[0])[i][:, 0:CG * NCP], cmp.bias[:, i:i + 1], he[:, :],
                                             ALU.add, ALU.mult).then_inc(hh_ready, 1)
                dve.wait_ge(w2_done, 1)
                dve.tensor_copy(kc[:, :], ops[0][:, 0:CG * NCP]).then_inc(kc_ready, 1)
                dve.tensor_copy(vc[:, :], ops[1][0:NCP, 0:CKV]).then_inc(kc_ready, 1)
                dve.wait_ge(gates_in, 32)
                for g, g0 in rounds():
                    with dve.Fori(g0, g0 + HG) as it:
                        link = Chain(dve, chain, it * LINKS + 4)
                        for u in range(U):
                            dve.wait_ge(loaded[u], it * 32 + 32)
                            dve.tensor_scalar(q[:, u, :], q[:, u, :], SCALE, None, ALU.mult).then_inc(scaled, 1)
                            for qb in range(2):
                                n = 2 * u + qb
                                nk = P * (qb + 1)
                                dve.wait_ge(scored, it * (2 * U) + (n + 1))
                                settle(dve, k)
                                link(dve.tensor_tensor_reduce(sc[:, qb, 0, 0:NCP], sps[qb][:, 0:NCP], cmask[:, qb, :], 1.0, MASK / 10,
                                                              ALU.add, ALU.max, st[:, qb, 0, 0:1]))
                                for r, o in ((1, 16), (2, 512)):
                                    settle(dve, k)
                                    link(dve.tensor_tensor_reduce(sc[:, qb, r, 0:nk], sps[qb][:, o:o + nk], tab[:, u, NP - nk:NP], 1.0, -3.0e38,
                                                                  ALU.add, ALU.max, st[:, qb, 0, r:r + 1]))
                                dve.tensor_scalar(st[:, qb, 1, :], st[:, qb, 0, :], -1.0, None, ALU.mult).then_inc(max_done, 1)
                            for qb in range(2):
                                n = 2 * u + qb
                                nk = P * (qb + 1)
                                dve.wait_ge(exp_done, it * (6 * U) + (3 * n + 3))
                                link(dve.tensor_scalar(st[:, qb, 2, :], st[:, qb, 2, :], 1.0e-30, None, ALU.max))
                                link(dve.reciprocal(st[:, qb, 3, :], st[:, qb, 2, :]))
                                link(dve.tensor_tensor(st[:, qb, 3, :], st[:, qb, 3, :],
                                                       gr[:, qb, :, bass.ds(it * U + u, 1)].rearrange("p r a -> p (r a)"), ALU.mult))
                                for r, w in enumerate((NCP, nk, nk)):
                                    ins = dve.tensor_scalar(sc[:, qb, r, 0:w], sc[:, qb, r, 0:w], st[:, qb, 3, r:r + 1], None, ALU.mult)
                                ins.then_inc(p_ready, 1)
                            for qb in range(2):
                                dve.wait_ge(turned, it * (4 * U) + (4 * u + 2 * qb + 1))
                                dve.tensor_copy(pt[0:NCP, qb, 0, :], tps[0][0:NCP, 0:P]).then_inc(pt_ready, 1)
                                dve.tensor_copy(pt[:, qb, 1:2 + qb, :], tps[0][:, P:(2 + qb) * P].rearrange("p (c n) -> p c n", n=P)).then_inc(pt_ready, 1)
                                dve.wait_ge(turned, it * (4 * U) + (4 * u + 2 * qb + 2))
                                dve.tensor_copy(pt[:, qb, 3:4 + qb, :], tps[1][:, 0:(1 + qb) * P].rearrange("p (c n) -> p c n", n=P)).then_inc(pt_ready, 1)
                            for qb in range(2):
                                n = 2 * u + qb
                                dve.wait_ge(pv_done, it * (2 * U) + (2 * U + n + 1))
                                dve.wait_ge(stored[u], it * 16 + 16)
                                dve.tensor_copy(ot[:, u, qb * P:(qb + 1) * P], ops[qb][:, 0:P]).then_inc(o_ready, 1)
                        assert link.n == LINKS


PHASES = (block_even_in, block_sample_a, block_prompt_a, block_even_out_odd_in, block_sample_c, block_prompt_c, block_final,)


class Kit:

    def __init__(self, nc):
        self.nc = nc
        self.stacks = [ExitStack()]
        self.sems = []
        self.phase = 0

    def sem(self, name):
        self.sems.append(self.nc.alloc_semaphore(name))
        return self.sems[-1]

    def sb(self, name, shape, dt=F32):
        return self.stacks[-1].enter_context(self.nc.sbuf_tensor(name, shape, dt))

    def sb_and_lo(self, name, shape):
        with self.nc.sbuf_tensor(name, shape, F32) as full:
            pass
        lo = self.sb(name + "_lo", shape, F32R)
        return full, lo

    def ps(self, name, shape):
        return self.stacks[-1].enter_context(self.nc.psum_tensor(name, shape, F32))

    def scope(self):
        return Scope(self)


class Scope:

    def __init__(self, kit):
        self.kit = kit

    def __enter__(self):
        self.kit.stacks.append(ExitStack())
        self.kit.phase += 1
        self.kit.settled = self.kit.sem(f"settled{self.kit.phase}")

    def __exit__(self, *exc):
        self.kit.stacks.pop().close()
        self.kit.nc.clear_and_free_semaphores(self.kit.sems)
        self.kit.sems = []
        self.kit.nc.all_engine_barrier()


def build(nc, ins, outs):
    def scratch(name, *shape):
        return nc.dram_tensor(name, list(shape), F32, kind="Internal").ap()

    k = Kit(nc)
    k.x_prompt = ins["x_prompt"][0]
    k.norm_even = ins["norm_even"][0]
    k.w_in_even = ins["w_in_even"][0]
    k.conv_w = ins["conv_w"][0]
    k.conv_b = ins["conv_b"][0]
    k.conv_ln_g = ins["conv_ln_g"][0]
    k.conv_ln_b = ins["conv_ln_b"][0]
    k.conv_pw_w = ins["conv_pw_w"][0]
    k.conv_pw_b = ins["conv_pw_b"][0]
    k.w_out_even = ins["w_out_even"][0]
    k.norm_odd = ins["norm_odd"][0]
    k.w_in_odd = ins["w_in_odd"][0]
    k.cmp_w1 = ins["cmp_w1"][0]
    k.cmp_w2 = ins["cmp_w2"][0]
    k.w_out_odd = ins["w_out_odd"][0]
    k.state_b_conv = ins["state_b_conv"][0]
    k.cache_c_kv = ins["cache_c_kv"][0]
    k.cache_c_win = ins["cache_c_win"][0]
    k.cmp_pos = ins["cmp_pos"]
    k.cmp_b1 = ins["cmp_b1"]
    k.final_norm = ins["final_norm"]
    k.rel_bias = ins["rel_bias"]
    k.page_table = ins["page_table"]
    k.c_ident = ins["c_ident"]
    k.c_onehot = ins["c_onehot"]
    k.c_overlap = ins["c_overlap"]
    k.c_hsum = ins["c_hsum"]
    k.c_cmask = ins["c_cmask"]
    k.x_sample = ins["x_sample"].rearrange("b t d -> (b t) d")
    k.cache_a = [ins[f"cache_a_kv{g}"][0] for g in range(NG)]
    k.out_y_p, k.out_y_s = outs[0][0], outs[1].rearrange("b t d -> (b t) d")
    k.out_a_p = [outs[2 + g][0, 0] for g in range(NG)]
    k.out_conv_p, k.out_rows_p, k.out_win_p = outs[5][0, 0], outs[6][0, 0], outs[7][0, 0]
    k.out_a_s = [outs[8 + g][0] for g in range(NG)]
    k.out_conv_s, k.out_rows_s, k.out_win_s = outs[11][0], outs[12][0], outs[13][0]
    k.zt = scratch("zt", EVEN_IN, T)
    k.kv = scratch("kv", T, 2 * QKV)
    k.xt = scratch("xt", D, T)
    k.mt = scratch("mt", D, T)
    k.z2 = scratch("z2", Z2_GP + CW, T)
    k.kv2 = scratch("kv2", T, 6 * CKV)
    k.gates = scratch("gates", NP, 3 * CH)
    k.gates_s = scratch("gates_s", 3 * CH, NQ, NB)
    k.tab_a = scratch("tab_a", NG, NH, FW)
    k.tab_c = scratch("tab_c", CH, FW)
    k.tab_sa = scratch("tab_sa", NQ, NH, SA)
    k.tab_hc = scratch("tab_hc", CH, HC)
    k.tab_hw = scratch("tab_hw", CH, HWC)
    k.toe_a = scratch("toe_a", NG, NH, P, NP)
    k.toe_c = scratch("toe_c", CH, P, NP)
    k.gate = scratch("gate", D, T)
    k.cache_pieces = cache_pieces(k)
    with k.stacks[0]:
        k.ident = k.sb("ident", [P, P])
        k.ones = k.sb("ones", [P, P])
        k.eps = k.sb("eps", [P, 1])
        for phase in PHASES:
            phase(nc, k)


_NAMES = ['x_prompt', 'x_sample', 'cache_a_kv0', 'cache_a_kv1', 'cache_a_kv2', 'state_b_conv', 'cache_c_kv', 'cache_c_win',
          'page_table', 'rel_bias', 'norm_even', 'w_in_even', 'conv_w', 'conv_b', 'conv_ln_g', 'conv_ln_b', 'conv_pw_w',
          'conv_pw_b', 'w_out_even', 'norm_odd', 'w_in_odd', 'cmp_pos', 'cmp_w1', 'cmp_b1', 'cmp_w2', 'w_out_odd', 'final_norm']
_OUTS = [(1, NP, D), (NB, NQ, D),
         (1, 1, 128, 2, 8, 128), (1, 1, NP, 2, 8, 128), (1, 1, NP, 2, 8, 128),
         (1, 1, 30, 1024), (1, 1, NP, 4, 2, 128), (1, 1, NP, 2, 2, 128),
         (1, NB, 128, 2, 8, 128), (1, NB, 512, 2, 8, 128), (1, NB, 2048, 2, 8, 128),
         (1, NB, 30, 1024), (1, NB, NQ, 4, 2, 128), (1, NB, 512, 2, 2, 128)]


def kernel(**inputs):
    import concourse.bacc as _bacc
    from concourse.bass_utils import run_bass_kernel_spmd as _run

    nc = _bacc.Bacc("TRN2", target_bir_lowering=False, num_devices=1)
    arrays, ins = {}, {}
    given = {name: np.ascontiguousarray(inputs[name]) for name in _NAMES}
    given.update(host_constants())
    for name in ("norm_even", "conv_b", "conv_ln_g", "conv_ln_b", "conv_pw_b", "norm_odd", "final_norm"):
        a = given[name]
        given[name] = np.ascontiguousarray(a.reshape(*a.shape[:-1], -1, P).swapaxes(-1, -2))
    given["conv_w"] = np.ascontiguousarray(given["conv_w"].reshape(1, TAPS, -1, P).transpose(0, 3, 2, 1))
    for name in ("cmp_pos", "cmp_b1"):
        a = given[name]
        given[name] = np.ascontiguousarray(np.moveaxis(a.reshape(2, -1, HD), 2, 0))
    for name, a in given.items():
        arrays[f"in_{name}"] = a
        ins[name] = nc.dram_tensor(f"in_{name}", a.shape, mybir.dt.from_np(a.dtype), kind="ExternalInput").ap()
    outs = [nc.dram_tensor(f"out_{i}", shape, F32, kind="ExternalOutput").ap() for i, shape in enumerate(_OUTS)]
    build(nc, ins, outs)
    r = _run(nc, [arrays], core_ids=[0])
    return tuple(r.results[0][f"out_{i}"] for i in range(len(_OUTS)))
```

```python
import math
from contextlib import ExitStack

import numpy as np

import concourse.bass as bass
from concourse import mybir

F32 = mybir.dt.float32
F32R = mybir.dt.float32r
I32 = mybir.dt.int32
ALU = mybir.AluOpType
ACT = mybir.ActivationFunctionType
AX = mybir.AxisListType.X

P = 128
D = 2048
NP = 256
NB, NQ = 8, 8
NS = NB * NQ
T = NP + NS
PAST = 2048
PAGE = 128
NPG = PAST // PAGE
HD = 128
SCALE = HD ** -0.5
EPS = 1e-6
MASK = -1.0e30
GROUPS = ((128, 1), (512, 4), (2048, 16))
NG, NH = 3, 8
QKV = NG * NH * HD
WB = 1024
TAPS = 31
EVEN_IN = 3 * QKV + NH * HD + 3 * WB
CH, CG = 16, 2
CHG = CH // CG
CW = CH * HD
CKV = CG * HD
CB, CS = 32, 16
NCS = PAST // CS - 1
NCP = NP // CS - 1
SELB = 64
NSEL = -(-(PAST + NQ) // SELB)
WIN = 512
NBUCK, MAXD = 32, 2048
KT = D // P
GW = 512
Z_GA, Z_A, Z_GT, Z_GB = 3 * QKV, 3 * QKV + 1024, 3 * QKV + 2048, 3 * QKV + 3072
C_KC, C_VC, C_KS, C_VS, C_KW, C_VW = (CW + i * CKV for i in range(6))
C_GL = CW + 6 * CKV
C_GP = C_GL + 3 * CH
ODD_IN = C_GP + CW
Z2_GP = C_GL
FW = 384
SA = NG * P + NG * NQ
HC = PAST + NQ + NQ - 1
HWC = WIN + NQ + NQ - 1


def host_constants():
    def onehot(dist, ok):
        d = np.maximum(dist, 0)
        ratio = np.log(np.maximum(d, 1).astype(np.float32) / np.float32(NBUCK // 2)) / np.float32(math.log(MAXD / (NBUCK // 2)))
        large = np.minimum(NBUCK // 2 + (ratio * np.float32(NBUCK // 2)).astype(np.int32), NBUCK - 1)
        b = np.where(d < NBUCK // 2, d, large)
        out = np.zeros((NBUCK + 1, dist.size), np.float32)
        n = np.arange(dist.size)
        out[b[ok], n[ok]] = 1.0
        out[NBUCK, ~ok] = MASK
        return out

    c = np.arange(FW)
    dist = 255 - c
    parts = [onehot(dist, (dist >= 0) & (dist <= w) & (dist % dil == 0)) for w, dil in GROUPS]
    parts.append(onehot(dist, dist >= 0))
    for i in range(NQ):
        j = np.arange(P)
        m = np.arange(NQ)
        for w, dil in GROUPS:
            dd = w + i - (dil * j + i % dil)
            parts.append(onehot(dd, (dd >= 0) & (dd <= w)))
        for w, dil in GROUPS:
            dd = i - m
            parts.append(onehot(dd, (dd >= 0) & (dd % dil == 0)))
    c = np.arange(HC)
    parts.append(onehot(PAST + NQ - 1 - c, PAST + NQ - 1 - c >= 0))
    c = np.arange(HWC)
    dd = WIN + NQ - 1 - c
    parts.append(onehot(dd, (dd >= 0) & (dd <= WIN)))
    ci, si = np.arange(NCS)[:, None], np.arange(NSEL)[None, :]
    overlap = ((ci * CS < (si + 1) * SELB) & (ci * CS + CB > si * SELB)).astype(np.float32)
    r = np.arange(P)
    hsum = (r[:, None] // CHG == r[None, :] // CHG).astype(np.float32)
    q = np.arange(NP).reshape(2, P)
    n = np.arange(NCP)
    cmask = np.where(n[None, None] * CS + CB - 1 <= q.T[:, :, None], 0.0, MASK).astype(np.float32)
    return {
        "c_ident": np.eye(P, dtype=np.float32),
        "c_onehot": np.concatenate(parts, axis=1),
        "c_overlap": overlap,
        "c_hsum": hsum,
        "c_cmask": np.ascontiguousarray(cmask),
    }


def ap_of(view, offset, dims):
    return bass.AP(tensor=view.tensor, offset=view.offset + offset, ap=[list(view.ap[0])] + [list(d) for d in dims])


def dram_ap(view, offset, dims):
    return bass.AP(tensor=view.tensor, offset=view.offset + offset, ap=[list(d) for d in dims])


class Chain:

    def __init__(self, eng, sem, base=0):
        self.eng, self.sem, self.base, self.n = eng, sem, base, 0

    def __call__(self, ins):
        self.n += 1
        ins.then_inc(self.sem, 1)
        self.eng.wait_ge(self.sem, self.base + self.n)


def wait(eng, sem, value):
    if not isinstance(value, int) or value > 0:
        eng.wait_ge(sem, value)


def settle(eng, k):
    eng.sem_inc(k.settled, 1)


def cache_pieces(k):
    pieces = []
    row = 2 * NH * HD
    for g, parts in ((2, 4), (0, 1)):
        keep = (GROUPS[g][0] - NQ) // parts
        m = 816 if g == 2 else keep * 2
        for b in range(NB):
            src = k.cache_a[g][b].rearrange("t a h d -> (t a h d)")
            dst = k.out_a_s[g][b].rearrange("t a h d -> (t a h d)")
            for i in range(max(parts - 1, 1)):
                lo = i * keep * row
                pieces.append((dst[lo:lo + keep * row].rearrange("(m n) -> m n", m=m),
                               src[lo + NQ * row:lo + (NQ + keep) * row].rearrange("(m n) -> m n", m=m)))
    return pieces




class Norm:

    def __init__(self, k, tag, xT, xn, gcol, ps, hi=None, lo=None):
        self.k, self.xT, self.xn, self.gcol, self.ps, self.hi, self.lo = k, xT, xn, gcol, ps, hi, lo
        self.sq = k.sb("sq" + tag, [P, 4, T])
        self.rs = k.sb("rs" + tag, [P, T])
        self.sq_ready, self.sq_used, self.root_done, self.chain, self.full, self.hi_made, self.ready = (
            k.sem(n + tag) for n in ("sq_ready", "sq_used", "root_done", "norm_chain", "xn_full", "xn_hi", "xn_ready"))

    def dve(self, dve, x_wait, free=None):
        k = self.k
        for t in range(KT):
            x_wait(dve, t)
            if t >= 4:
                dve.wait_ge(self.sq_used, t - 3)
            dve.tensor_tensor(self.sq[:, t % 4, :], self.xT[:, t, :], self.xT[:, t, :], ALU.mult).then_inc(self.sq_ready, 1)
        dve.wait_ge(self.root_done, 1)
        link = Chain(dve, self.chain)
        link(dve.reciprocal(self.rs[:, :], self.rs[:, :]))
        if free:
            free(dve)

        def lo(t):
            dve.wait_ge(self.hi_made, t + 1)
            dve.tensor_tensor(self.lo[:, t, :], self.xn[:, t, :], self.hi[:, t, :], ALU.subtract).then_inc(self.ready, 1)

        for t in range(KT):
            dve.scalar_tensor_tensor(self.xn[:, t, :], self.xT[:, t, :], self.gcol[:, t:t + 1], self.rs[:, :],
                                     ALU.mult, ALU.mult).then_inc(self.full if self.hi is not None else self.ready, 1)
            if self.hi is not None and t >= 2:
                lo(t - 2)
        if self.hi is not None:
            lo(KT - 2)
            lo(KT - 1)

    def pe(self, pe):
        for t in range(KT):
            pe.wait_ge(self.sq_ready, t + 1)
            pe.matmul(self.ps[:, 0:T], self.k.ones[:, :], self.sq[:, t % 4, :], start=(t == 0), stop=(t == KT - 1)
                      ).then_inc(self.sq_used, 1)

    def act(self, act):
        act.wait_ge(self.sq_used, KT)
        act.activation(self.rs[:, :], self.ps[:, 0:T], ACT.Sqrt, bias=self.k.eps[:, :], scale=1.0 / D).then_inc(self.root_done, 1)
        if self.hi is not None:
            for t in range(KT):
                act.wait_ge(self.full, t + 1)
                act.copy(self.hi[:, t, :], self.xn[:, t, :]).then_inc(self.hi_made, 1)


class Proj:

    def __init__(self, k, tag, w, rhs_hi, rhs_lo, banks, segs, zt=None, rows=None, row_banks=None, residual=None, after=None):
        self.k, self.banks, self.segs, self.zt, self.after = k, banks, segs, zt, after
        self.xh, self.xl = rhs_hi, rhs_lo
        self.w = w.rearrange("(k p) n -> p k n", p=P)
        self.nq, self.kq = 4, KT // 4
        self.rows, self.row_banks, self.residual = rows, row_banks, residual
        if after is None:
            self.wt, self.lo = k.sb_and_lo("w" + tag, [P, self.nq, self.kq, GW])
            self.hi = k.sb("w_hi" + tag, [P, 2, self.kq, GW], F32R)
        else:
            self.wt, self.hi, self.lo = after.wt, after.hi, after.lo
        self.n_groups = sum(s[0] for s in segs)
        self.loaded = [k.sem(f"w_loaded{q}" + tag) for q in range(self.nq)]
        self.freed = [k.sem(f"w_freed{q}" + tag) for q in range(self.nq - 1)]
        self.tile_done, self.z_ready, self.z_stored, self.hi_ready, self.hi_used, self.lo_ready = (
            k.sem(n + tag) for n in ("tile_done", "z_ready", "z_stored", "w_hi_ready", "w_hi_used", "w_lo_ready"))
        if residual is None:
            self.z = k.sb("z" + tag, [P, 4, T])
        if rows is not None:
            self.rsb = k.sb("rows" + tag, [P, 3, GW])
            self.rows_done, self.rows_evac, self.rows_stored = (k.sem(n + tag) for n in ("rows_done", "rows_evac", "rows_stored"))

    def segments(self):
        g = r = 0
        for i, (n, src, dst, rc) in enumerate(self.segs):
            yield i, n, src, dst, rc, g, r
            g += n
            r += n * (rc is not None)

    def loop(self, eng, seg, body, ahead=None, end=None):
        start = 0
        if ahead and seg[0] == 0:
            body(0, ahead)
            start = 1
        end = seg[1] if end is None else end
        if end > start:
            with eng.Fori(start, end) as it:
                body(it, lambda q: None)

    def sync(self, sp, ahead=None):
        if self.after is not None:
            sp.wait_ge(self.after.tile_done, 4 * self.after.n_groups + 4)
        for seg in self.segments():
            _, n, src, dst, rc, g0, r0 = seg

            def body(it, first):
                for q in range(self.nq):
                    first(q)
                    if q < self.nq - 1:
                        sp.wait_ge(self.freed[q], it + (g0 + 1))
                    else:
                        sp.wait_ge(self.tile_done, it * 4 + (4 * g0 + 4))
                    sp.dma_start(self.wt[:, q, :, :], self.w[:, q * self.kq:(q + 1) * self.kq, bass.ds(it * GW + src, GW)]
                                 ).then_inc(self.loaded[q], 16)

            self.loop(sp, seg, body, ahead)

    def pe(self, pe, quarter_wait=None, before=None):
        for q in range(self.nq - 1):
            pe.sem_inc(self.freed[q], 1)
        pe.sem_inc(self.tile_done, 4)
        pe.sem_inc(self.hi_used, 2)
        for i, n, src, dst, rc, g0, r0 in self.segments():
            if before and i in before:
                before[i](pe)
            with pe.Fori(0, n) as it:
                for q in range(self.nq):
                    if quarter_wait:
                        quarter_wait(pe, q)
                    pe.wait_ge(self.hi_ready, it * 4 + (4 * g0 + q + 1))
                    for c in range(4):
                        if q == 0:
                            pe.wait_ge(self.z_ready, it * 4 + (4 * g0 + c + 1))
                        for j in range(self.kq):
                            for m, x in enumerate((self.xh, self.xl)):
                                ins = pe.matmul(self.banks[c][:, 0:T], self.hi[:, q % 2, j, c * P:(c + 1) * P],
                                                x[:, q * self.kq + j, :], start=(q == 0 and j == 0 and m == 0), stop=False)
                    ins.then_inc(self.hi_used, 1)
                    pe.wait_ge(self.lo_ready, it * 4 + (4 * g0 + q + 3))
                    for c in range(4):
                        for j in range(self.kq):
                            ins = pe.matmul(self.banks[c][:, 0:T], self.lo[:, q, j, c * P:(c + 1) * P],
                                            self.xh[:, q * self.kq + j, :], start=False, stop=(q == self.nq - 1 and j == self.kq - 1))
                        if q == self.nq - 1:
                            ins.then_inc(self.tile_done, 1)
                        elif c == 3:
                            ins.then_inc(self.freed[q], 1)
                if rc is not None:
                    pe.wait_ge(self.z_ready, it * 4 + (4 * g0 + 8))
                    pe.wait_ge(self.rows_evac, it * 3 + (3 * r0 + 3))
                    for t, m in enumerate((P, P, NS)):
                        for c in range(4):
                            ins = pe.transpose(self.row_banks[t][0:m, c * P:(c + 1) * P], self.z[:, c, t * P:t * P + m],
                                               self.k.ident[:, :])
                        ins.then_inc(self.rows_done, 1)

    def make_hi(self, act, it, g0, q):
        act.wait_ge(self.loaded[q % 4], it * 16 + (16 * (g0 + q // 4) + 16))
        if q == 0:
            act.copy(self.hi[:, 0, :, :], self.wt[:, 0, :, :]).then_inc(self.hi_ready, 1)
            return
        act.wait_ge(self.hi_used, it * 4 + (4 * g0 + q + 1))
        act.wait_ge(self.lo_ready, it * 4 + (4 * g0 + q + 1))
        act.copy(self.hi[:, q % 2, :, :], self.wt[:, q % 4, :, :]).then_inc(self.hi_ready, 1)

    def act(self, act, before=None, ahead=None):
        if self.residual is None:
            act.sem_inc(self.z_ready, 4)
            act.sem_inc(self.z_stored, 16)
        if self.rows is not None:
            act.sem_inc(self.rows_evac, 3)
            act.sem_inc(self.rows_stored, 32)

        def group(it, seg, more, first):
            _, n, src, dst, rc, g0, r0 = seg
            for q in range(1, 5 if more else 4):
                first(q - 1)
                self.make_hi(act, it, g0, q)
            if self.residual is not None:
                return
            act.wait_ge(self.z_stored, it * 16 + (16 * g0 + 16))
            for c in range(4):
                act.wait_ge(self.tile_done, it * 4 + (4 * g0 + 4 + c + 1))
                act.copy(self.z[:, c, :], self.banks[c][:, 0:T]).then_inc(self.z_ready, 1)
            act.wait_ge(self.z_ready, it * 4 + (4 * g0 + 8))
            act.dma_start(self.zt[bass.ds(it * GW + dst, GW), :].rearrange("(c p) t -> p c t", p=P), self.z[:, :, :]
                          ).then_inc(self.z_stored, 16)
            if rc is not None:
                act.wait_ge(self.rows_stored, it * 32 + (32 * r0 + 32))
                for t, m in enumerate((P, P, NS)):
                    act.wait_ge(self.rows_done, it * 3 + (3 * r0 + t + 1))
                    act.copy(self.rsb[0:m, t, :], self.row_banks[t][0:m, :]).then_inc(self.rows_evac, 1)
                act.wait_ge(self.rows_evac, it * 3 + (3 * r0 + 6))
                act.dma_start(self.rows[0:NP, bass.ds(it * GW + rc, GW)].rearrange("(t p) n -> p t n", p=P), self.rsb[:, 0:2, :]
                              ).then_inc(self.rows_stored, 16)
                act.dma_start(self.rows[NP:T, bass.ds(it * GW + rc, GW)], self.rsb[0:NS, 2, :]).then_inc(self.rows_stored, 16)

        for seg in self.segments():
            i, n, last = seg[0], seg[1], seg[5] + seg[1] == self.n_groups
            if before and i in before:
                before[i](act)
            self.loop(act, seg, lambda it, first: group(it, seg, True, first), ahead, n - last)
            if last:
                group(n - 1, seg, False, lambda q: None)

    def dve(self, dve, before=None, beside=None, ahead=None):
        if self.residual is not None:
            dve.sem_inc(self.z_ready, 4)
        dve.sem_inc(self.lo_ready, 2)
        for seg in self.segments():
            i, n, src, dst, rc, g0, r0 = seg
            if before and i in before:
                before[i](dve)

            def body(it, first):
                for q in range(self.nq):
                    first(q)
                    dve.wait_ge(self.hi_ready, it * 4 + (4 * g0 + q + 1))
                    dve.tensor_tensor(self.lo[:, q, :, :], self.wt[:, q, :, :], self.hi[:, q % 2, :, :], ALU.subtract).then_inc(self.lo_ready, 1)
                    if beside and i in beside:
                        beside[i](it * 4 + q)
                if self.residual is not None:
                    for c in range(4):
                        dve.wait_ge(self.tile_done, it * 4 + (4 * g0 + 4 + c + 1))
                        x = self.residual[:, bass.ds(it * 4 + (4 * g0 + c), 1), :]
                        dve.tensor_tensor(x, x, self.banks[c][:, 0:T].unsqueeze(1), ALU.add).then_inc(self.z_ready, 1)

            self.loop(dve, seg, body, ahead)


def table_jobs(k):
    jobs, c = [], 0
    for g in range(NG):
        jobs.append(([(slice(g * NH, (g + 1) * NH), c, 0, FW)], NH, FW, k.tab_a[g]))
        c += FW
    jobs.append(([(slice(0, CH), c, 0, FW)], CH, FW, k.tab_c))
    c += FW
    for i in range(NQ):
        parts = []
        for g in range(NG):
            parts.append((slice(g * NH, (g + 1) * NH), c, g * P, P))
            c += P
        for g in range(NG):
            parts.append((slice(g * NH, (g + 1) * NH), c, NG * P + g * NQ, NQ))
            c += NQ
        jobs.append((parts, NH, SA, k.tab_sa[i]))
    for dst, width in ((k.tab_hc, HC), (k.tab_hw, HWC)):
        for o in range(0, width, 512):
            n = min(512, width - o)
            jobs.append(([(slice(0, CH), c + o, 0, n)], CH, n, dst[:, o:o + n]))
        c += width
    return jobs, c


def silu_tile(dve, k, sem, x, e, out, t):
    at = lambda v: v[:, bass.ds(t, 1), :]
    link = Chain(dve, sem, t * 2)
    link(dve.tensor_scalar(at(e), at(e), 1.0, None, ALU.add))
    settle(dve, k)
    link(dve.reciprocal(at(e), at(e)))
    return dve.tensor_tensor(at(out), at(x), at(e), ALU.mult)


def block_even_in(nc, k):
    KB = WB // P
    H = TAPS - 1
    with k.scope():
        xrow = k.sb("xrow", [P, 3, D])
        flat = xrow[:, :, :].rearrange("p a n -> p (a n)")
        u = flat[:, 0:KB * T].rearrange("p (c t) -> p c t", t=T)
        e = flat[:, KB * T:2 * KB * T].rearrange("p (c t) -> p c t", t=T)
        xT, xl = k.sb_and_lo("xT1", [P, KT, T])
        xh = k.sb("xh1", [P, KT, T], F32R)
        gcol = k.sb("gcol1", [P, KT])
        jobs, ncols = table_jobs(k)
        wide = k.sb("wide", [P, KB * WB])
        onehot = wide[0:NBUCK + 1, 0:ncols]
        pw = wide[:, :].rearrange("p (c n) -> p c n", n=WB)
        relb = k.sb("relb", [NBUCK + 1, NG * NH])
        up = k.sb("up", [P, KB, H + NP])
        us = k.sb("us", [P, KB, NB, H + NQ])
        y = k.sb("y", [P, KB, T])
        tab = y[0:CH, :, :].rearrange("p c t -> p (c t)")[:, 0:1024].rearrange("p (s n) -> p s n", s=2)
        hrow = k.sb("hrow", [4 * H, 2, WB])
        crow = hrow[0:NS, :, :]
        taps = k.sb("taps", [P, KB, TAPS])
        vec = k.sb("cvec", [P, 4, KB])
        mu = k.sb("mu", [P, T])
        rs = k.sb("rsb", [P, T])
        banks = [k.ps(f"zb{i}", [P, 512]) for i in range(4)]
        rbanks = [k.ps(f"rb{i}", [P, 512]) for i in range(3)]
        nbank = k.ps("nb", [P, 512])
        x_loaded, g_loaded, tab_loaded, xt_stored = (k.sem(n) for n in ("x_loaded", "g1_loaded", "tab_loaded", "xt_stored"))
        consts_loaded, consts_set = k.sem("consts_loaded"), k.sem("consts_set")
        turned, xT_ready = k.sem("x_turned"), k.sem("xT_ready")
        tab_done, tab_evac = k.sem("tab_done"), k.sem("tab_evac")
        tab_stored = [k.sem(f"tab_stored{i}") for i in range(2)]
        copied = k.sem("copied")
        u_in, h_in, v_in, pw_in = (k.sem(n) for n in ("glu_in", "hist_in", "cvec_in", "pw_in"))
        s_copied, padded, e_done, u_ready, chain = (k.sem(n) for n in ("conv_copied", "conv_padded", "glu_exp", "u_ready", "conv_chain"))
        h_turned, h_evac, c_turned, c_evac, c_stored = (k.sem(n) for n in ("h_turned", "h_evac", "c_turned", "c_evac", "c_stored"))
        taps_done, y_sum, yc_ready, var_sum, root, e2_done, act_ready, pw_done, o_ready, o_stored = (
            k.sem(n) for n in ("taps_done", "y_sum", "yc_ready", "var_sum", "ln_root", "silu_exp", "silu_ready", "pw_done", "ob_ready", "ob_stored"))
        ln_in, gate_in, gate_exp, gate_ready, gate_stored = (k.sem(n) for n in ("ln_in", "gate_in", "gate_exp", "gate_ready", "gate_stored"))
        glu_chain, silu_chain, gate_chain0, gate_chain1 = (k.sem(n) for n in ("glu_chain", "silu_chain", "gate_chain0", "gate_chain1"))
        norm = Norm(k, "1", xT, xT, gcol, nbank, hi=xh, lo=xl)
        GLU, GB, GB2, GA, GA2, Q, K0, K1, K2, K3, K4, K5, K6, K7, K8, K9 = range(16)
        proj = Proj(k, "1", k.w_in_even, xh, xl, banks,
                    [(4, Z_A, Z_A, None), (1, Z_GB, Z_GB, None), (1, Z_GB + GW, Z_GB + GW, None), (1, Z_GA, Z_GA, None),
                     (1, Z_GA + GW, Z_GA + GW, None), (6, 0, 0, None)]
                    + [(1, QKV + n * GW, QKV + n * GW, n * GW) for n in range(7)]
                    + [(n, QKV + g * GW, QKV + g * GW, g * GW) for g, n in ((7, 2), (9, 2), (11, 1))],
                    zt=k.zt, rows=k.kv, row_banks=rbanks)
        with nc.Block() as block:
            @block.sync
            def _(sp):
                sp.dma_start(k.ident[:, :], k.c_ident).then_inc(consts_loaded, 16)
                sp.dma_start(xrow[:, 0:2, :], k.x_prompt.rearrange("(t p) n -> p t n", p=P)).then_inc(x_loaded, 16)
                sp.dma_start(xrow[0:NS, 2, :], k.x_sample).then_inc(x_loaded, 16)
                sp.dma_start(gcol[:, :], k.norm_even).then_inc(g_loaded, 16)
                sp.dma_start(onehot, k.c_onehot).then_inc(tab_loaded, 16)
                sp.dma_start(relb[0:NBUCK, :], k.rel_bias).then_inc(tab_loaded, 16)
                proj.sync(sp)
                sp.wait_ge(proj.z_stored, 16 * 27)
                sp.wait_ge(proj.rows_stored, 32 * 13)

            @block.gpsimd
            def _(pool):
                link = Chain(pool, consts_set)
                link(pool.memset(k.ones[:, :], 1.0))
                link(pool.memset(k.eps[:, :], EPS))
                link(pool.memset(relb[NBUCK:NBUCK + 1, :], 1.0))
                pool.memset(up[:, :, 0:H], 0.0).then_inc(padded, 1)
                for i in range(2):
                    pool.dma_start(hrow[:, i, :], k.state_b_conv[4 * i:4 * i + 4].rearrange("b t n -> (b t) n")).then_inc(h_in, 16)
                pool.dma_start(taps[:, :, :], k.conv_w).then_inc(v_in, 16)
                for i, v in enumerate((k.conv_b, k.conv_ln_g, k.conv_ln_b, k.conv_pw_b)):
                    pool.dma_start(vec[:, i, :], v).then_inc(v_in, 16)
                pool.wait_ge(xT_ready, KT)
                pool.dma_start(k.xt.rearrange("(k p) t -> p k t", p=P), xT[:, :, :]).then_inc(xt_stored, 16)
                pool.wait_ge(tab_done, len(jobs))
                pool.dma_start(pw[:, :, :], k.conv_pw_w.rearrange("(c p) n -> p c n", p=P)).then_inc(pw_in, 16)
                for b in range(NB):
                    pool.dma_start(k.out_conv_s[b, 0:H - NQ, :], k.state_b_conv[b, NQ:H, :]).then_inc(s_copied, 16)
                pieces = k.cache_pieces[0:15]
                sent = 0

                def send(groups):
                    n = 0
                    for g in groups:
                        pool.wait_ge(proj.tile_done, 4 * g + 4)
                        pool.dma_start(*pieces[sent + n]).then_inc(copied, 16)
                        n += 1
                    return n

                pool.wait_ge(proj.z_stored, 16 * 5)
                pool.dma_start(u, k.zt[Z_A:Z_A + WB, :].rearrange("(c p) t -> p c t", p=P)).then_inc(u_in, 16)
                pool.dma_start(e, k.zt[Z_GT:Z_GT + WB, :].rearrange("(c p) t -> p c t", p=P)).then_inc(u_in, 16)
                sent += send((6,))
                pool.wait_ge(c_evac, 4)
                pool.dma_start(k.out_conv_p, crow[0:H, 0, :]).then_inc(c_stored, 16)
                for b in range(NB):
                    pool.dma_start(k.out_conv_s[b, H - NQ:H, :], crow[b * NQ:(b + 1) * NQ, 1, :]).then_inc(c_stored, 16)
                sent += send((8, 9, 10, 11, 12, 13, 14, 15, 17))
                pool.wait_ge(o_ready, KB)
                pool.dma_start(k.mt[NH * HD:, :].rearrange("(c p) t -> p c t", p=P), y[:, :, :]).then_inc(o_stored, 16)
                pool.wait_ge(o_stored, 16)
                for buf, z in ((u, Z_GA), (y[:, :, :], Z_GB)):
                    pool.dma_start(buf, k.zt[z:z + WB, :].rearrange("(c p) t -> p c t", p=P)).then_inc(gate_in, 16)
                sent += send((21, 22, 23))
                for i, buf in enumerate((u, y[:, :, :])):
                    pool.wait_ge(gate_ready, KB * (i + 1))
                    pool.dma_start(k.gate[i * WB:(i + 1) * WB, :].rearrange("(c p) t -> p c t", p=P), buf).then_inc(gate_stored, 16)
                sent += send((24, 25))
                pool.wait_ge(copied, 16 * sent)
                pool.wait_ge(s_copied, 16 * NB)
                pool.wait_ge(c_stored, 16 * (NB + 1))
                pool.wait_ge(gate_stored, 32)

            @block.scalar
            def _(act):
                for n, (parts, m, width, dst) in enumerate(jobs):
                    act.wait_ge(tab_done, n + 1)
                    if n >= 2:
                        act.wait_ge(tab_stored[n % 2], 16 * (n // 2))
                    act.copy(tab[0:m, n % 2, 0:width], rbanks[n % 2][0:m, 0:width]).then_inc(tab_evac, 1)
                    act.wait_ge(tab_evac, n + 1)
                    act.dma_start(dst, tab[0:m, n % 2, 0:width]).then_inc(tab_stored[n % 2], 16)
                norm.act(act)
                proj.make_hi(act, 0, 0, 0)

                def glu_exp(act):
                    act.wait_ge(u_in, 32)
                    act.activation(e, e, ACT.Exp, scale=-1.0).then_inc(e_done, 1)

                def deviation(act):
                    act.wait_ge(var_sum, 1)
                    act.activation(rs[:, :], nbank[:, 0:T], ACT.Sqrt, bias=k.eps[:, :], scale=1.0 / WB).then_inc(root, 1)

                def silu_exps(act):
                    for c in range(KB):
                        act.wait_ge(ln_in, c + 1)
                        act.activation(e[:, c, :], y[:, c, :], ACT.Exp, scale=-1.0).then_inc(e2_done, 1)

                def gate_exps(act, i):
                    act.wait_ge(gate_in, 32)
                    if i:
                        act.wait_ge(gate_ready, KB)
                    act.activation(e, (u, y[:, :, :])[i], ACT.Exp, scale=-1.0).then_inc(gate_exp, 1)

                proj.act(act, {GB2: glu_exp, K3: deviation, K4: silu_exps, K7: lambda e: gate_exps(e, 0), K8: lambda e: gate_exps(e, 1)})
                for i in range(2):
                    act.wait_ge(tab_stored[i], 16 * len(jobs[i::2]))

            @block.tensor
            def _(pe):
                pe.wait_ge(consts_loaded, 16)
                pe.wait_ge(x_loaded, 32)
                for t in range(KT):
                    if t >= 4:
                        pe.wait_ge(xT_ready, t - 3)
                    for j, m in enumerate((P, P, NS)):
                        ins = pe.transpose(banks[t % 4][:, j * P:j * P + m], xrow[0:m, j, t * P:(t + 1) * P], k.ident[0:m, 0:m])
                    ins.then_inc(turned, 1)
                pe.wait_ge(consts_set, 3)
                norm.pe(pe)
                pe.wait_ge(tab_loaded, 32)

                def tables(pe):
                    for n, (parts, m, width, dst) in enumerate(jobs):
                        if n >= 2:
                            pe.wait_ge(tab_evac, n - 1)
                        for heads, c, o, w in parts:
                            ins = pe.matmul(rbanks[n % 2][0:m, o:o + w], relb[:, heads], onehot[:, c:c + w], start=True, stop=True)
                        ins.then_inc(tab_done, 1)

                def history(pe):
                    pe.wait_ge(h_in, 32)
                    pe.wait_ge(tab_evac, len(jobs))
                    for c in range(KB):
                        if c >= 2:
                            pe.wait_ge(h_evac, c - 1)
                        for i in range(2):
                            ins = pe.transpose(rbanks[c % 2][:, i * 4 * H:(i + 1) * 4 * H], hrow[:, i, c * P:(c + 1) * P], k.ident[0:4 * H, 0:4 * H])
                        ins.then_inc(h_turned, 1)

                def new_rows(pe):
                    pe.wait_ge(u_ready, KB)
                    pe.wait_ge(h_evac, KB)
                    for j, (lo, m) in enumerate(((NP - H, H), (NP, NS))):
                        for half in range(2):
                            if j:
                                pe.wait_ge(c_evac, half + 1)
                            for c in range(4):
                                ins = pe.transpose(rbanks[half][0:m, c * P:(c + 1) * P], u[:, half * 4 + c, lo:lo + m], k.ident[:, :])
                            ins.then_inc(c_turned, 1)

                def sum_y(pe):
                    pe.wait_ge(taps_done, 2 * KB * TAPS)
                    for c in range(KB):
                        ins = pe.matmul(nbank[:, 0:T], k.ones[:, :], y[:, c, :], start=(c == 0), stop=(c == KB - 1))
                    ins.then_inc(y_sum, 1)

                def sum_var(pe):
                    pe.wait_ge(yc_ready, 1)
                    for c in range(KB):
                        ins = pe.matmul(nbank[:, 0:T], k.ones[:, :], e[:, c, :], start=(c == 0), stop=(c == KB - 1))
                    ins.then_inc(var_sum, 1)

                def pointwise(pe):
                    pe.wait_ge(act_ready, KB)
                    pe.wait_ge(pw_in, 16)
                    pe.wait_ge(proj.rows_evac, 3 * 6 + 3)
                    for n in range(KB):
                        if n >= 2:
                            pe.wait_ge(o_ready, n - 1)
                        for c in range(KB):
                            ins = pe.matmul(rbanks[n % 2][:, 0:T], pw[:, c, n * P:(n + 1) * P], u[:, c, :], start=(c == 0), stop=(c == KB - 1))
                        ins.then_inc(pw_done, 1)
                    pe.wait_ge(o_ready, KB)

                tables(pe)
                proj.pe(pe, lambda e, q: e.wait_ge(norm.ready, 4 * q + 4), {GB: history, Q: new_rows, K2: sum_y, K3: sum_var, K6: pointwise})

            @block.vector
            def _(dve):
                for t in range(KT):
                    dve.wait_ge(turned, t + 1)
                    dve.tensor_copy(xT[:, t, :], banks[t % 4][:, 0:T]).then_inc(xT_ready, 1)
                dve.wait_ge(g_loaded, 16)
                norm.dve(dve, lambda e, t: e.wait_ge(xT_ready, t + 1), lambda e: e.wait_ge(xt_stored, 16))
                link = Chain(dve, chain)

                def history(dve):
                    for c in range(KB):
                        dve.wait_ge(h_turned, c + 1)
                        dve.tensor_copy(us[:, c, :, 0:H], rbanks[c % 2][:, 0:NB * H].rearrange("p (b t) -> p b t", t=H)).then_inc(h_evac, 1)

                def glu(t):
                    dve.wait_ge(e_done, 1)
                    silu_tile(dve, k, glu_chain, u, e, u, t).then_inc(u_ready, 1)

                def spread_u(dve):
                    dve.wait_ge(u_ready, KB)
                    link(dve.tensor_copy(up[:, :, H:], u[:, :, 0:NP]))
                    link(dve.tensor_copy(us[:, :, :, H:], u[:, :, NP:T].rearrange("p c (b q) -> p c b q", q=NQ)))

                def views(c, j, t):
                    if j == 0:
                        return y[:, c, 0:NP], up[:, c, bass.ds(t, NP)]
                    return y[:, c, NP:T].rearrange("p (b q) -> p b q", q=NQ), us[:, c, :, bass.ds(t, NQ)]

                def first_tap(dve):
                    for j, m in enumerate((H, NS)):
                        for half in range(2):
                            dve.wait_ge(c_turned, 2 * j + half + 1)
                            dve.tensor_copy(crow[0:m, j, half * 512:(half + 1) * 512], rbanks[half][0:m, :]).then_inc(c_evac, 1)
                    dve.wait_ge(v_in, 80)
                    dve.wait_ge(padded, 1)
                    for i in range(2):
                        dve.wait_ge(tab_stored[i], 16 * len(jobs[i::2]))
                    for j in range(2):
                        for c in range(KB):
                            out, x = views(c, j, 0)
                            dve.tensor_scalar(out, x, taps[:, c, 0:1], vec[:, 0, c:c + 1], ALU.mult, ALU.add).then_inc(taps_done, 1)

                def tap(t):
                    for j in range(2):
                        for c in range(KB):
                            n = j * KB + c
                            dve.wait_ge(taps_done, t * (2 * KB) + (n + 1 - 2 * KB))
                            out, x = views(c, j, t)
                            dve.scalar_tensor_tensor(out, x, taps[:, c, bass.ds(t, 1)], out, ALU.mult, ALU.add).then_inc(taps_done, 1)

                def last_taps(dve):
                    tap(TAPS - 2)
                    tap(TAPS - 1)

                all_c = [P, KB, T]

                def centre(dve):
                    dve.wait_ge(y_sum, 1)
                    link(dve.tensor_scalar(mu[:, :], nbank[:, 0:T], 1.0 / WB, None, ALU.mult))
                    link(dve.tensor_tensor(y[:, :, :], y[:, :, :], mu[:, :].unsqueeze(1).broadcast_to(all_c), ALU.subtract))
                    dve.tensor_tensor(e, y[:, :, :], y[:, :, :], ALU.mult).then_inc(yc_ready, 1)

                def scale(dve):
                    dve.wait_ge(root, 1)
                    link(dve.reciprocal(rs[:, :], rs[:, :]))
                    link(dve.tensor_tensor(y[:, :, :], y[:, :, :], rs[:, :].unsqueeze(1).broadcast_to(all_c), ALU.mult))
                    for c in range(KB):
                        dve.tensor_scalar(y[:, c, :], y[:, c, :], vec[:, 1, c:c + 1], vec[:, 2, c:c + 1], ALU.mult, ALU.add).then_inc(ln_in, 1)

                def silu(t):
                    dve.wait_ge(e2_done, t + 1)
                    silu_tile(dve, k, silu_chain, y, e, u, t).then_inc(act_ready, 1)

                def pointwise(dve):
                    for n in range(KB):
                        dve.wait_ge(pw_done, n + 1)
                        dve.tensor_scalar(y[:, n, :], rbanks[n % 2][:, 0:T], vec[:, 3, n:n + 1], None, ALU.add).then_inc(o_ready, 1)

                def gate(i, t):
                    buf = (u, y)[i]
                    dve.wait_ge(gate_exp, i + 1)
                    silu_tile(dve, k, (gate_chain0, gate_chain1)[i], buf, e, buf, t).then_inc(gate_ready, 1)

                proj.dve(dve, {GB: history, GA2: spread_u, Q: first_tap, K1: last_taps, K2: centre, K3: scale, K6: pointwise},
                         {GB2: lambda n: glu(n), GA: lambda n: glu(n + 4), Q: lambda n: tap(n + 1), K0: lambda n: tap(n + 25),
                          K4: lambda n: silu(n), K5: lambda n: silu(n + 4), K7: lambda n: gate(0, n), K8: lambda n: gate(1, n)})


NR = NQ * NH
ZN = [0, NH * NR, 2 * NH * NR]
Z1 = 3 * NH * NR
Z2 = Z1 + 4 * NH * NR
ZQ = Z2 + NQ * NH * NR
TILES = [(0, 0)] + [(1, r) for r in range(4)] + [(2, i) for i in range(NQ)]


def z_block(g, r, h):
    o = (ZN[0], Z1, Z2)[g] + (r * NH + h) * NR
    return slice(o, o + NR)


def block_sample_a(nc, k):
    with k.scope():
        kt = [k.sb("ka0", [P, 1, NH * HD]), k.sb("ka1", [P, 4, NH * HD]), k.sb("ka2", [P, NQ, NH * HD])]
        vt = [k.sb("va0", [P, 1, NH * HD]), k.sb("va1", [P, 4, NH * HD]), k.sb("va2", [P, NQ, NH * HD])]
        vnew = k.sb("vnew", [NG * NQ, NH * HD])
        qs = k.sb("qsa", [P, NG * NH, NS])
        kn = k.sb("kna", [P, NG * NH, NS])
        qz = k.sb("qz", [P, ZQ])
        pz = k.sb("pz", [P, ZQ - 2 * NH * NR])
        pzn = k.sb("pzn", [NG * NQ, NH, NR])
        bias = k.sb("bias_sa", [NR, SA])
        s = k.sb("s_sa", [NR, SA])
        stat = k.sb("stat_sa", [NR, 4])
        ktt = k.sb("ktt", [P, 2, 4 * P])
        orow = k.sb("orow", [NR, HD])
        ot = k.sb("ot_sa", [P, NH, NS])
        kps = [k.ps(f"kps{i}", [P, 512]) for i in range(2)]
        sps, pps, ops, tps = (k.ps(n, [P, 512]) for n in ("sps", "pps", "ops", "tps"))
        pieces = [(0, 0, 1), (1, 0, 4), (2, 0, 4), (2, 4, 8)]
        k_in = [k.sem(f"ka_in{i}") for i in range(4)]
        v_in = [k.sem(f"va_in{i}") for i in range(4)]
        vn_in, q_in, b_in, zeroed = k.sem("vn_in"), k.sem("qa_in"), k.sem("ba_in"), k.sem("za_set")
        qz_ready, turned, evac_a, evac_d = k.sem("qz_ready"), k.sem("ka_turned"), k.sem("ka_evac_a"), k.sem("ka_evac_d")
        scored, score_tiles = k.sem("sa_done"), k.sem("sa_tiles")
        chain, max_done, exp_done, p_ready = k.sem("sa_chain"), k.sem("sa_max"), k.sem("sa_exp"), k.sem("sa_p")
        p_turned, pz_ready, pv_done, o_evac, o_turned, o_ready, o_stored = (
            k.sem(n) for n in ("pa_turned", "pza_ready", "pva_done", "oa_evac", "oa_turned", "oa_ready", "oa_stored"))
        pv_tiles = k.sem("pva_tiles")
        scaled, toe_stored, rows_out = k.sem("qa_scaled"), k.sem("toe_stored"), k.sem("rows_a_out")
        p_zeroed = k.sem("za_p_set")
        NQUAD = 2 * len(TILES)

        def tile_src(g, lo, hi, b, kv):
            w, dil = GROUPS[g]
            v = k.cache_a[g].rearrange("b (j r) a h d -> b j r a (h d)", r=dil)
            return v[bass.ds(b, 1), :, lo:hi, kv, :].rearrange("b j r n -> (b j) r n")

        with nc.Block() as block:
            @block.sync
            def _(sp):
                for i in range(NG):
                    for dst, row in ((qs, i), (kn, NG + i)):
                        sp.dma_start(dst[:, i * NH:(i + 1) * NH, :], k.zt[row * NH * HD:(row + 1) * NH * HD, NP:T].rearrange("(h d) t -> d h t", d=HD)).then_inc(q_in, 16)
                sp.dma_start(bias[:, :], k.tab_sa.rearrange("i h n -> (i h) n")).then_inc(b_in, 16)

                def load_k(b, first=False):
                    for n, (g, lo, hi) in enumerate(pieces):
                        if not first:
                            sp.wait_ge(turned, b * NQUAD - NQUAD + 2 * sum(t[2] - t[1] for t in pieces[:n + 1]))
                        sp.dma_start(kt[g][:, lo:hi, :], tile_src(g, lo, hi, b, 0)).then_inc(k_in[n], 16)

                def load_v(b, first=False):
                    for n, (g, lo, hi) in enumerate(pieces):
                        if not first:
                            sp.wait_ge(pv_tiles, b * 4 - 4 + (n + 1))
                        sp.dma_start(vt[g][:, lo:hi, :], tile_src(g, lo, hi, b, 1)).then_inc(v_in[n], 16)
                    if not first:
                        sp.wait_ge(pv_done, b * 1)
                    for g in range(NG):
                        c = QKV + g * NH * HD
                        sp.dma_start(vnew[g * NQ:(g + 1) * NQ, :], k.kv[bass.ds(b * NQ + NP, NQ), c:c + NH * HD]).then_inc(vn_in, 16)

                load_k(0, True)
                load_v(0, True)
                load_k(1)
                with sp.Fori(1, NB - 1) as b:
                    load_k(b + 1)
                    load_v(b)
                load_v(NB - 1)
                sp.wait_ge(o_ready, NB)
                sp.dma_start(k.mt[0:NH * HD, NP:T].rearrange("(h d) t -> d h t", d=HD), ot[:, :, :]).then_inc(o_stored, 16)
                sp.wait_ge(o_stored, 16)

            @block.gpsimd
            def _(pool):
                link = Chain(pool, zeroed)
                link(pool.memset(qz[:, :], 0.0))
                pool.wait_ge(scaled, 1)

                def fill_q(b):
                    wait(pool, scored, b * 1)
                    for g in range(NG):
                        pool.tensor_copy(ap_of(qz[:, :], ZN[g], [(NR + 1, NH), (NH, NQ)]),
                                         qs[:, g * NH:(g + 1) * NH, bass.ds(b * NQ, NQ)]).then_inc(qz_ready, 1)
                    for h in range(2):
                        pool.tensor_copy(ap_of(qz[:, :], Z1 + h * 4 * NH, [(NH * NR + NH, 4), (NR + 1, NH)]),
                                         qs[:, NH:2 * NH, bass.ds(b * NQ + 4 * h, 4)].rearrange("p h i -> p i h")).then_inc(qz_ready, 1)
                    pool.tensor_copy(ap_of(qz[:, :], Z2, [(NH * NR + NH, NQ), (NR + 1, NH)]),
                                     qs[:, 2 * NH:3 * NH, bass.ds(b * NQ, NQ)].rearrange("p h i -> p i h")).then_inc(qz_ready, 1)

                fill_q(0)
                pool.dma_start(k.toe_a.rearrange("g h p n -> (g h) p n"), dram_ap(k.tab_a, P - 1, [(FW, NG * NH), (-1, P), (1, NP)])).then_inc(toe_stored, 16)
                pool.dma_start(k.toe_c, dram_ap(k.tab_c, P - 1, [(FW, CH), (-1, P), (1, NP)])).then_inc(toe_stored, 16)
                n_rows = 0
                for g, (w, _) in enumerate(GROUPS):
                    keep = min(w, NP)
                    for kv in range(2):
                        c = kv * QKV + g * NH * HD
                        pool.dma_start(k.out_a_p[g][:, kv, :, :].rearrange("t h d -> t (h d)"), k.kv[NP - keep:NP, c:c + NH * HD]).then_inc(rows_out, 16)
                        for b in range(NB):
                            pool.dma_start(k.out_a_s[g][b, w - NQ:w, kv, :, :].rearrange("t h d -> t (h d)"),
                                           k.kv[NP + b * NQ:NP + (b + 1) * NQ, c:c + NH * HD]).then_inc(rows_out, 16)
                        n_rows += 1 + NB

                with pool.Fori(1, NB) as b:
                    fill_q(b)
                pool.wait_ge(toe_stored, 32)
                pool.wait_ge(rows_out, 16 * n_rows)

            def evac_k(eng, b, odd, sem):
                copy = eng.tensor_copy if odd else eng.copy
                for q in range(odd, NQUAD, 2):
                    eng.wait_ge(turned, b * NQUAD + (q + 1))
                    wait(eng, score_tiles, b * NQUAD + (q - 1))
                    copy(ktt[:, q % 2, :], kps[q % 2][:, :]).then_inc(sem, 1)

            @block.scalar
            def _(act):
                def one(b):
                    evac_k(act, b, 0, evac_a)
                    act.wait_ge(max_done, b + 1)
                    act.activation(s[:, :], s[:, :], ACT.Exp, bias=stat[:, 1:2], accum_out=stat[:, 2:3]).then_inc(exp_done, 1)

                one(0)
                with act.Fori(1, NB) as b:
                    one(b)

            @block.tensor
            def _(pe):
                def quad_turn(b, q):
                    g, r = TILES[q // 2]
                    if q % 2 == 0 and (g, r) in [(p_[0], p_[1]) for p_ in pieces]:
                        pe.wait_ge(k_in[[(p_[0], p_[1]) for p_ in pieces].index((g, r))], b * 16 + 16)
                    if q >= 2:
                        pe.wait_ge((evac_a, evac_d)[q % 2], b * (NQUAD // 2) + q // 2)
                    for j in range(4):
                        h = 4 * (q % 2) + j
                        ins = pe.transpose(kps[q % 2][:, j * P:(j + 1) * P], kt[g][:, r, h * HD:(h + 1) * HD], k.ident[:, :])
                    ins.then_inc(turned, 1)

                def quad_score(b, q):
                    g, r = TILES[q // 2]
                    pe.wait_ge((evac_a, evac_d)[q % 2], b * (NQUAD // 2) + (q // 2 + 1))
                    for j in range(4):
                        h = 4 * (q % 2) + j
                        first = r == 0 and h == 0
                        last = r == (0, 3, NQ - 1)[g] and h == NH - 1
                        ins = pe.matmul(sps[0:NR, g * P:(g + 1) * P], qz[:, z_block(g, r, h)], ktt[:, q % 2, j * P:(j + 1) * P],
                                        start=first, stop=last)
                    ins.then_inc(score_tiles, 1)

                def scores(b):
                    quad_turn(b, 0)
                    pe.wait_ge(qz_ready, b * 6 + 6)
                    wait(pe, max_done, b * 1)
                    for q in range(NQUAD):
                        if q + 1 < NQUAD:
                            quad_turn(b, q + 1)
                        quad_score(b, q)
                    for g in range(NG):
                        for h in range(NH):
                            o = ZN[g] + h * NR
                            ins = pe.matmul(sps[0:NR, NG * P + g * NQ:NG * P + (g + 1) * NQ], qz[:, o:o + NR],
                                            kn[:, g * NH + h, bass.ds(b * NQ, NQ)], start=(h == 0), stop=(h == NH - 1))
                    ins.then_inc(scored, 1)

                def turn_p(b):
                    pe.wait_ge(p_ready, b + 1)
                    wait(pe, pz_ready, b * 5)
                    settle(pe, k)
                    for g in range(NG):
                        pe.transpose(pps[:, g * NR:(g + 1) * NR], s[:, g * P:(g + 1) * P], k.ident[0:NR, 0:NR])
                    pe.transpose(pps[0:NG * NQ, NG * NR:(NG + 1) * NR], s[:, NG * P:SA], k.ident[0:NR, 0:NR]).then_inc(p_turned, 1)

                def values(b):
                    pe.wait_ge(pz_ready, b * 5 + 5)
                    wait(pe, o_evac, b * 1)
                    n = 0
                    for g, r in TILES:
                        for m, (pg, lo, hi) in enumerate(pieces):
                            if (pg, lo) == (g, r):
                                pe.wait_ge(v_in[m], b * 16 + 16)
                        for h in range(NH):
                            c = z_block(g, r, h).start - (2 * NH * NR if g else 0)
                            ins = pe.matmul(ops[0:NR, 0:HD], pz[:, c:c + NR], vt[g][:, r, h * HD:(h + 1) * HD],
                                            start=(n == 0), stop=False)
                            n += 1
                        if (g, r + 1) in [(p_[0], p_[2]) for p_ in pieces]:
                            ins.then_inc(pv_tiles, 1)
                    pe.wait_ge(vn_in, b * 48 + 48)
                    for h in range(NH):
                        ins = pe.matmul(ops[0:NR, 0:HD], pzn[:, h, :], vnew[:, h * HD:(h + 1) * HD], start=False, stop=(h == NH - 1))
                    ins.then_inc(pv_done, 1)

                def turn_o(b):
                    pe.wait_ge(o_evac, b + 1)
                    wait(pe, o_ready, b * 1)
                    settle(pe, k)
                    pe.transpose(tps[:, 0:NR], orow[:, :], k.ident[0:NR, 0:NR]).then_inc(o_turned, 1)

                scores(0)
                turn_p(0)
                with pe.Fori(1, NB) as b:
                    scores(b)
                    values(b - 1)
                    turn_p(b)
                    turn_o(b - 1)
                values(NB - 1)
                turn_o(NB - 1)

            @block.vector
            def _(dve):
                dve.wait_ge(q_in, 96)
                dve.tensor_scalar(qs[:, :, :], qs[:, :, :], SCALE, None, ALU.mult).then_inc(scaled, 1)
                dve.wait_ge(b_in, 16)

                def softmax(b):
                    link = Chain(dve, chain, b * 2)
                    dve.wait_ge(scored, b + 1)
                    wait(dve, p_turned, b * 1)
                    settle(dve, k)
                    link(dve.tensor_tensor_reduce(s[:, :], sps[0:NR, 0:SA], bias[:, :], 1.0, -3.0e38, ALU.add, ALU.max, stat[:, 0:1]))
                    dve.tensor_scalar(stat[:, 1:2], stat[:, 0:1], -1.0, None, ALU.mult).then_inc(max_done, 1)
                    dve.wait_ge(exp_done, b + 1)
                    link(dve.reciprocal(stat[:, 3:4], stat[:, 2:3]))
                    dve.tensor_scalar(s[:, :], s[:, :], stat[:, 3:4], None, ALU.mult).then_inc(p_ready, 1)

                def fill_p(b):
                    dve.wait_ge(p_turned, b + 1)
                    wait(dve, pv_done, b * 1)
                    dve.tensor_copy(ap_of(pz[:, :], 0, [(NR + 1, NH), (NH, NQ)]),
                                    ap_of(pps[:, :], 0, [(1, NH), (NH, NQ)])).then_inc(pz_ready, 1)
                    o1, o2 = Z1 - 2 * NH * NR, Z2 - 2 * NH * NR
                    for h in range(2):
                        dve.tensor_copy(ap_of(pz[:, :], o1 + h * 4 * NH, [(NH * NR + NH, 4), (NR + 1, NH)]),
                                        ap_of(pps[:, :], NR + h * 4 * NH, [(NH, 4), (1, NH)])).then_inc(pz_ready, 1)
                    dve.tensor_copy(ap_of(pz[:, :], o2, [(NH * NR + NH, NQ), (NR + 1, NH)]),
                                    ap_of(pps[:, :], 2 * NR, [(NH, NQ), (1, NH)])).then_inc(pz_ready, 1)
                    dve.tensor_copy(ap_of(pzn[:, :, :], 0, [(NR + 1, NH), (NH, NQ)]),
                                    ap_of(pps[0:NG * NQ, :], 3 * NR, [(1, NH), (NH, NQ)])).then_inc(pz_ready, 1)

                def out_rows(b):
                    dve.wait_ge(pv_done, b + 1)
                    wait(dve, o_turned, b * 1)
                    dve.tensor_copy(orow[:, :], ops[0:NR, 0:HD]).then_inc(o_evac, 1)

                def out_cols(b):
                    dve.wait_ge(o_turned, b + 1)
                    dve.tensor_copy(ot[:, :, bass.ds(b * NQ, NQ)], tps[:, 0:NR].rearrange("p (i h) -> p h i", h=NH)).then_inc(o_ready, 1)

                evac_k(dve, 0, 1, evac_d)
                link = Chain(dve, p_zeroed)
                link(dve.memset(pz[:, :], 0.0))
                link(dve.memset(pzn[:, :, :], 0.0))
                softmax(0)
                fill_p(0)
                with dve.Fori(1, NB) as b:
                    evac_k(dve, b, 1, evac_d)
                    softmax(b)
                    out_rows(b - 1)
                    fill_p(b)
                    out_cols(b - 1)
                out_rows(NB - 1)
                out_cols(NB - 1)


def block_prompt_a(nc, k):
    with k.scope():
        U = 2
        q = k.sb("qpa", [P, U, NG, NP])
        kk = k.sb("kpa", [P, U, NG, NP])
        v = k.sb("vpa", [P, U, 2, NG, HD])
        tab = k.sb("tpa", [P, U, NG, NP])
        s = k.sb("spa", [P, 2, NG, NP])
        pt = k.sb("ptpa", [P, 2, 2 * NG, P])
        stat = k.sb("stpa", [P, 2, 4])
        ot = k.sb("otpa", [P, U, NP])
        sps = [k.ps(f"spa{i}", [P, 1024]) for i in range(2)]
        pps = [k.ps(f"ppa{i}", [P, 512]) for i in range(2)]
        ops = [k.ps(f"opa{i}", [P, 512]) for i in range(2)]
        loaded = [k.sem(f"pp_in{u}") for u in range(U)]
        q_scaled, scored, max_done, exp_done, p_ready, chain = (
            k.sem(n) for n in ("pp_scaled", "pp_scored", "pp_max", "pp_exp", "pp_p", "pp_chain"))
        turned, pt_ready, pv_done, o_ready = (k.sem(n) for n in ("pp_turned", "pp_pt", "pp_pv", "pp_o"))
        stored = [k.sem(f"pp_stored{u}") for u in range(U)]

        with nc.Block() as block:
            @block.sync
            def _(sp):
                with sp.Fori(0, NH // U) as it:
                    for u in range(U):
                        h = it * U + u
                        sp.wait_ge(pv_done, it * (2 * U) + (2 * u + 2))
                        for src, dst in ((0, q), (QKV, kk)):
                            sp.dma_start(dst[:, u, :, :], k.zt[src:src + QKV, 0:NP].rearrange("(g h d) t -> h d g t", g=NG, h=NH)
                                         [bass.ds(h, 1)].rearrange("a d g t -> (a d) g t")).then_inc(loaded[u], 16)
                        sp.dma_start(v[:, u, 0, :, :], k.kv[0:P, QKV:2 * QKV].rearrange("p (g h d) -> h p g d", g=NG, h=NH)
                                     [bass.ds(h, 1)].rearrange("a p g d -> (a p) g d")).then_inc(loaded[u], 16)
                        sp.dma_start(v[:, u, 1, :, :], k.kv[P:NP, QKV:2 * QKV].rearrange("p (g h d) -> h p g d", g=NG, h=NH)
                                     [bass.ds(h, 1)].rearrange("a p g d -> (a p) g d")).then_inc(loaded[u], 16)
                        for g in range(NG):
                            sp.dma_start(tab[:, u, g, :], k.toe_a[g][bass.ds(h, 1)].rearrange("a p n -> (a p) n")).then_inc(loaded[u], 16)

            @block.scalar
            def _(act):
                for u in range(U):
                    act.sem_inc(stored[u], 16)
                with act.Fori(0, NH // U) as it:
                    for u in range(U):
                        for qb in range(2):
                            n = 2 * u + qb
                            nk = P * (qb + 1)
                            act.wait_ge(max_done, it * (2 * U) + (n + 3))
                            act.activation(s[:, qb, :, 0:nk], s[:, qb, :, 0:nk], ACT.Exp, bias=stat[:, qb, 1:2],
                                           accum_out=stat[:, qb, 2:3]).then_inc(exp_done, 1)
                        act.wait_ge(o_ready, it * (2 * U) + (2 * u + 4))
                        act.dma_start(k.mt[bass.ds((it * U + u) * HD, HD), 0:NP], ot[:, u, :]).then_inc(stored[u], 16)
                for u in range(U):
                    act.wait_ge(stored[u], 16 * (NH // U) + 16)

            @block.tensor
            def _(pe):
                pe.sem_inc(pv_done, 2 * U)
                with pe.Fori(0, NH // U) as it:
                    for u in range(U):
                        pe.wait_ge(loaded[u], it * 112 + 112)
                        pe.wait_ge(q_scaled, it * U + (u + 1))
                        for qb in range(2):
                            n = 2 * u + qb
                            nk = P * (qb + 1)
                            pe.wait_ge(max_done, it * (2 * U) + (n + 1))
                            for g in range(NG):
                                ins = pe.matmul(sps[qb][:, g * NP:g * NP + nk], q[:, u, g, qb * P:(qb + 1) * P], kk[:, u, g, 0:nk],
                                                start=True, stop=True)
                            ins.then_inc(scored, 1)
                        for qb in range(2):
                            n = 2 * u + qb
                            pe.wait_ge(p_ready, it * (2 * U) + (n + 1))
                            for half in range(qb + 1):
                                for g in range(NG):
                                    ins = pe.transpose(pps[half][:, g * P:(g + 1) * P], s[:, qb, g, half * P:(half + 1) * P], k.ident[:, :])
                                ins.then_inc(turned, 1)
                            pe.wait_ge(pt_ready, it * (3 * U) + (3 * u + (1, 3)[qb]))
                            pe.wait_ge(o_ready, it * (2 * U) + (n + 1))
                            for half in range(qb + 1):
                                for g in range(NG):
                                    ins = pe.matmul(ops[qb][:, 0:P], v[:, u, half, g, :], pt[:, qb, half * NG + g, :],
                                                    start=(half == 0 and g == 0), stop=(half == qb and g == NG - 1))
                            ins.then_inc(pv_done, 1)

            @block.vector
            def _(dve):
                dve.sem_inc(max_done, 2)
                dve.sem_inc(o_ready, 2)
                with dve.Fori(0, NH // U) as it:
                    link = Chain(dve, chain, it * (4 * U))
                    for u in range(U):
                        dve.wait_ge(loaded[u], it * 112 + 112)
                        dve.tensor_scalar(q[:, u, :, :], q[:, u, :, :], SCALE, None, ALU.mult).then_inc(q_scaled, 1)
                        for qb in range(2):
                            n = 2 * u + qb
                            nk = P * (qb + 1)
                            lo = NP - nk
                            dve.wait_ge(scored, it * (2 * U) + (n + 1))
                            settle(dve, k)
                            link(dve.tensor_tensor_reduce(s[:, qb, :, 0:nk], sps[qb][:, 0:NG * NP].rearrange("p (g n) -> p g n", g=NG)[:, :, 0:nk],
                                                          tab[:, u, :, lo:NP], 1.0, -3.0e38, ALU.add, ALU.max, stat[:, qb, 0:1]))
                            dve.tensor_scalar(stat[:, qb, 1:2], stat[:, qb, 0:1], -1.0, None, ALU.mult).then_inc(max_done, 1)
                        for qb in range(2):
                            n = 2 * u + qb
                            nk = P * (qb + 1)
                            dve.wait_ge(exp_done, it * (2 * U) + (n + 1))
                            link(dve.reciprocal(stat[:, qb, 3:4], stat[:, qb, 2:3]))
                            dve.tensor_scalar(s[:, qb, :, 0:nk], s[:, qb, :, 0:nk], stat[:, qb, 3:4], None, ALU.mult).then_inc(p_ready, 1)
                        for qb in range(2):
                            n = 2 * u + qb
                            for half in range(qb + 1):
                                dve.wait_ge(turned, it * (3 * U) + (3 * u + qb + half + 1))
                                dve.tensor_copy(pt[:, qb, half * NG:(half + 1) * NG, :], pps[half][:, 0:NG * P].rearrange("p (g n) -> p g n", g=NG)).then_inc(pt_ready, 1)
                        for qb in range(2):
                            n = 2 * u + qb
                            dve.wait_ge(pv_done, it * (2 * U) + (2 * U + n + 1))
                            dve.wait_ge(stored[u], it * 16 + 16)
                            dve.tensor_copy(ot[:, u, qb * P:(qb + 1) * P], ops[qb][:, 0:P]).then_inc(o_ready, 1)


class Mix:

    def __init__(self, k, tag):
        self.mix, self.lo = k.sb_and_lo("mix" + tag, [P, KT, T])
        self.gate, self.hi = k.sb_and_lo("gate" + tag, [P, KT, T])
        self.loaded = [k.sem(f"mix_in{c}" + tag) for c in range(4)]
        self.full, self.hi_made, self.ready = (k.sem(n + tag) for n in ("mix_full", "mix_hi", "mix_ready"))

    def load(self, sp, k, c):
        for dst, src in ((self.mix, k.mt), (self.gate, k.gate)):
            sp.dma_start(dst[:, c * 4:(c + 1) * 4, :], src[c * 512:(c + 1) * 512, :].rearrange("(k p) t -> p k t", p=P)).then_inc(self.loaded[c], 16)

    def make(self, dve, c):
        s = slice(c * 4, (c + 1) * 4)
        dve.wait_ge(self.loaded[c], 32)
        dve.tensor_tensor(self.mix[:, s, :], self.mix[:, s, :], self.gate[:, s, :], ALU.mult).then_inc(self.full, 1)
        dve.wait_ge(self.hi_made, c + 1)
        dve.tensor_tensor(self.lo[:, s, :], self.mix[:, s, :], self.hi[:, s, :], ALU.subtract).then_inc(self.ready, 1)

    def make_hi(self, act, c):
        s = slice(c * 4, (c + 1) * 4)
        act.wait_ge(self.full, c + 1)
        act.copy(self.hi[:, s, :], self.mix[:, s, :]).then_inc(self.hi_made, 1)


def block_even_out_odd_in(nc, k):
    with k.scope():
        mixed = Mix(k, "2")
        mix, gate = mixed.mix, mixed.gate
        xT = k.sb("xT2", [P, KT, T])
        xn, xl = k.sb_and_lo("xn2", [P, KT, T])
        xh = k.sb("xh2", [P, KT, T], F32R)
        gcol = k.sb("gcol2", [P, KT])
        wg = k.sb("wg", [P, KT, 3 * CH])
        gr = k.sb("gr", [P, 3, 3 * CH])
        banks = [k.ps(f"zc{i}", [P, 512]) for i in range(4)]
        rbanks = [k.ps(f"rc{i}", [P, 512]) for i in range(3)]
        nbank = k.ps("nc2", [P, 512])
        x_in, g_in, wg_in = (k.sem(n) for n in ("xT2_in", "g2_in", "wg_in"))
        gate_in, gate_exp, gate_chain, gate_ready, gate_stored, copied = (
            k.sem(n) for n in ("gate3_in", "gate3_exp", "gate3_chain", "gate3_ready", "gate3_stored", "copied3"))
        gs = k.sb("gs", [3 * CH, NQ, NB])
        gs_turned, gs_ready = k.sem("gs_turned"), k.sem("gs_ready")
        gl_done, gl_exp, gl_chain, gl_stored, xt_stored = (k.sem(n) for n in ("gl_done", "gl_exp", "gl_chain", "gl_stored", "xt2_stored"))
        norm = Norm(k, "2", xT, xn, gcol, nbank, hi=xh, lo=xl)
        out = Proj(k, "2", k.w_out_even, mixed.hi, mixed.lo, banks, [(4, 0, 0, None)], residual=xT)
        proj = Proj(k, "3", k.w_in_odd, xh, xl, banks, [(4, C_GP, Z2_GP, None), (1, 0, 0, None), (3, GW, GW, None), (1, CW, CW, 0), (2, CW + GW, CW + GW, GW)],
                    zt=k.z2, rows=k.kv2, row_banks=rbanks, after=out)
        with nc.Block() as block:
            @block.sync
            def _(sp):
                view = lambda a: a.rearrange("(k p) t -> p k t", p=P)
                sp.dma_start(gcol[:, :], k.norm_odd).then_inc(g_in, 16)
                out.sync(sp, lambda q: mixed.load(sp, k, q))
                sp.dma_start(wg[:, :, :], k.w_in_odd[:, C_GL:C_GL + 3 * CH].rearrange("(k p) n -> p k n", p=P)).then_inc(wg_in, 16)
                proj.sync(sp)
                sp.dma_start(view(k.xt), xT[:, :, :]).then_inc(xt_stored, 16)
                sp.dma_start(k.gates.rearrange("(t p) n -> p t n", p=P), gr[:, 0:2, :]).then_inc(gl_stored, 16)
                sp.wait_ge(gs_ready, 1)
                sp.dma_start(k.gates_s, gs[:, :, :]).then_inc(gl_stored, 16)
                sp.wait_ge(gl_stored, 32)
                sp.wait_ge(xt_stored, 16)
                sp.wait_ge(proj.z_stored, 16 * 12)
                sp.wait_ge(proj.rows_stored, 32 * 4)

            @block.scalar
            def _(act):
                out.make_hi(act, 0, 0, 0)
                out.act(act, ahead=lambda q: mixed.make_hi(act, q))
                norm.act(act)
                for t, m in enumerate((P, P, NS)):
                    act.wait_ge(gl_done, t + 1)
                    act.activation(gr[0:m, t, :], rbanks[t][0:m, 0:3 * CH], ACT.Exp, scale=-1.0).then_inc(gl_exp, 1)

                def gate_exps(act):
                    act.wait_ge(gate_in, 16)
                    act.activation(gate[:, :, :], mix[:, :, :], ACT.Exp, scale=-1.0).then_inc(gate_exp, 1)

                proj.make_hi(act, 0, 0, 0)
                proj.act(act, {2: gate_exps})

            @block.gpsimd
            def _(pool):
                pool.wait_ge(mixed.loaded[3], 32)
                pool.dma_start(xT[:, :, :], k.xt.rearrange("(k p) t -> p k t", p=P)).then_inc(x_in, 16)
                pieces = k.cache_pieces[15:23]
                for n, p in enumerate(pieces):
                    pool.wait_ge(out.tile_done if n < 3 else proj.tile_done, 4 * n + 8 if n < 3 else 4 * (n - 3) + 8)
                    pool.dma_start(*p).then_inc(copied, 16)
                    if n == 5:
                        pool.wait_ge(proj.z_stored, 16 * 5)
                        pool.dma_start(mix[:, :, :], k.z2[Z2_GP:, :].rearrange("(k p) t -> p k t", p=P)).then_inc(gate_in, 16)
                pool.wait_ge(gate_ready, KT)
                pool.dma_start(k.gate.rearrange("(k p) t -> p k t", p=P), mix[:, :, :]).then_inc(gate_stored, 16)
                pool.wait_ge(gate_stored, 16)
                pool.wait_ge(copied, 16 * len(pieces))

            @block.tensor
            def _(pe):
                out.pe(pe, lambda e, q: e.wait_ge(mixed.ready, q + 1))
                norm.pe(pe)
                pe.wait_ge(wg_in, 16)
                pe.wait_ge(norm.ready, KT)
                for t, m in enumerate((P, P, NS)):
                    for j in range(KT):
                        for i, x in enumerate((xh[:, j, :].bitcast(F32), xl[:, j, :].bitcast(F32))):
                            ins = pe.matmul(rbanks[t][0:m, 0:3 * CH], x[:, t * P:t * P + m], wg[:, j, :],
                                            start=(j == 0 and i == 0), stop=(j == KT - 1 and i == 1))
                    ins.then_inc(gl_done, 1)
                pe.wait_ge(gl_chain, 6)
                pe.transpose(nbank[0:3 * CH, 0:NS], gr[0:NS, 2, :], k.ident[0:NS, 0:NS]).then_inc(gs_turned, 1)
                proj.pe(pe)

            @block.vector
            def _(dve):
                def first(q):
                    mixed.make(dve, q)
                    if q == 3:
                        dve.wait_ge(x_in, 16)

                out.dve(dve, ahead=first)
                dve.wait_ge(out.z_ready, 20)
                dve.wait_ge(g_in, 16)
                norm.dve(dve, lambda e, t: None)
                link = Chain(dve, gl_chain)
                for t, m in enumerate((P, P, NS)):
                    dve.wait_ge(gl_exp, t + 1)
                    link(dve.tensor_scalar(gr[0:m, t, :], gr[0:m, t, :], 1.0, None, ALU.add))
                    link(dve.reciprocal(gr[0:m, t, :], gr[0:m, t, :]))
                dve.wait_ge(gs_turned, 1)
                dve.tensor_copy(gs[:, :, :], nbank[0:3 * CH, 0:NS].rearrange("p (b i) -> p i b", b=NB)).then_inc(gs_ready, 1)

                def gates(t):
                    dve.wait_ge(gate_exp, 1)
                    silu_tile(dve, k, gate_chain, mix, gate, mix, t).then_inc(gate_ready, 1)

                proj.dve(dve, beside={2: lambda n: gates(n), 3: lambda n: gates(n + 12)})


def block_final(nc, k):
    with k.scope():
        mixed = Mix(k, "4")
        xT = k.sb("xT4", [P, KT, T])
        xn = k.sb("xn4", [P, KT, T])
        gcol = k.sb("gcol4", [P, KT])
        yrow = k.sb("yrow", [P, 3, D])
        banks = [k.ps(f"zd{i}", [P, 512]) for i in range(4)]
        ybanks = [k.ps(f"yb{i}", [P, 512]) for i in range(3)]
        nbank = k.ps("nd", [P, 512])
        x_in, g_in = (k.sem(n) for n in ("xT4_in", "g4_in"))
        turned, y_ready, y_stored = (k.sem(n) for n in ("y_turned", "y_ready", "y_stored"))
        norm = Norm(k, "4", xT, xn, gcol, nbank)
        out = Proj(k, "4", k.w_out_odd, mixed.hi, mixed.lo, banks, [(4, 0, 0, None)], residual=xT)
        sizes = (P, P, NS)
        with nc.Block() as block:
            @block.sync
            def _(sp):
                sp.dma_start(gcol[:, :], k.final_norm).then_inc(g_in, 16)
                out.sync(sp, lambda q: mixed.load(sp, k, q))
                for t in range(3):
                    sp.wait_ge(y_ready, 4 * t + 4)
                    dst = k.out_y_p[t * P:(t + 1) * P, :] if t < 2 else k.out_y_s
                    sp.dma_start(dst, yrow[0:sizes[t], t, :]).then_inc(y_stored, 16)
                sp.wait_ge(y_stored, 48)

            @block.gpsimd
            def _(pool):
                pool.wait_ge(mixed.loaded[3], 32)
                pool.dma_start(xT[:, :, :], k.xt.rearrange("(k p) t -> p k t", p=P)).then_inc(x_in, 16)

            @block.scalar
            def _(act):
                out.make_hi(act, 0, 0, 0)
                out.act(act, ahead=lambda q: mixed.make_hi(act, q))
                norm.act(act)

            @block.tensor
            def _(pe):
                out.pe(pe, lambda e, q: e.wait_ge(mixed.ready, q + 1))
                norm.pe(pe)
                pe.wait_ge(norm.ready, KT)
                for n in range(12):
                    t, f = n // 4, n % 4
                    m = sizes[t]
                    if n >= 3:
                        pe.wait_ge(y_ready, n - 2)
                    for c in range(4):
                        ins = pe.transpose(ybanks[n % 3][0:m, c * P:(c + 1) * P], xn[:, 4 * f + c, t * P:t * P + m], k.ident[:, :])
                    ins.then_inc(turned, 1)

            @block.vector
            def _(dve):
                def first(q):
                    mixed.make(dve, q)
                    if q == 3:
                        dve.wait_ge(x_in, 16)

                out.dve(dve, ahead=first)
                dve.wait_ge(out.z_ready, 20)
                dve.wait_ge(g_in, 16)
                norm.dve(dve, lambda e, t: None)
                for n in range(12):
                    t, f = n // 4, n % 4
                    m = sizes[t]
                    dve.wait_ge(turned, n + 1)
                    dve.tensor_copy(yrow[0:m, t, f * 512:(f + 1) * 512], ybanks[n % 3][0:m, :]).then_inc(y_ready, 1)


O_W, O_WN, O_S = 0, WIN, WIN + NQ
O_SN = O_S + PAST
O_C = O_SN + NQ
NSC = O_C + NCS


class Compress:

    def __init__(self, k):
        self.k = k
        self.w1, self.w2, self.pos, self.b1, self.bias, self.nbias = (
            k.sb(name, shape, lasting=True) for name, shape in (
                ("cmp_w1", [P, 2, CB, HD]), ("cmp_w2", [P, 2, HD]), ("cmp_pos", [P, 2 * CB]), ("cmp_b1", [P, 2]),
                ("cmp_bias", [P, 2]), ("cmp_nbias", [P, 2])))
        self.loaded, self.done, self.ready = (k.sem(n) for n in ("cmp_in", "cmp_pos_done", "cmp_bias_ready"))

    def sync(self, sp):
        for i in range(2):
            sp.dma_start(self.w1[:, i, :, :], self.k.cmp_w1[i].rearrange("l d e -> d l e")).then_inc(self.loaded, 16)
        sp.dma_start(self.w2[:, :, :], self.k.cmp_w2.rearrange("a e d -> e a d")).then_inc(self.loaded, 16)
        sp.dma_start(self.pos[:, :], self.k.cmp_pos).then_inc(self.loaded, 16)
        sp.dma_start(self.b1[:, :], self.k.cmp_b1).then_inc(self.loaded, 16)

    def pe(self, pe, bank):
        pe.wait_ge(self.loaded, 80)
        for i in range(2):
            for l in range(CB):
                ins = pe.matmul(bank[:, i:i + 1], self.w1[:, i, l, :], self.pos[:, i * CB + l:i * CB + l + 1], start=(l == 0), stop=(l == CB - 1))
        ins.then_inc(self.done, 1)

    def dve(self, dve, bank):
        dve.wait_ge(self.done, 1)
        link = Chain(dve, self.ready)
        link(dve.tensor_tensor(self.bias[:, :], bank[:, 0:2], self.b1[:, :], ALU.add))
        link(dve.tensor_scalar(self.nbias[:, :], self.bias[:, :], -1.0, None, ALU.mult))


def block_sample_c(nc, k):
    with k.scope():
        k.compress = cmp = Compress(k)
        raw = k.sb("raw", [P, NPG, 2 * CKV])
        sel = k.sb("sel", [P, NPG, 2 * CKV])
        win = k.sb("win", [P, WIN // P, 2 * CKV])
        xt = k.sb("xtc", [P, 4, PAST])
        qs = k.sb("qsc", [P, CH, NS])
        kn = k.sb("knc", [P, 2, CG, NS])
        vn = k.sb("vnc", [NQ, 2, CKV])
        qc = k.sb("qc", [P, CG, P])
        ktt = k.sb("kttc", [P, 2, 4, P])
        ptt = k.sb("pttc", [P, 2, 4, P])
        bias = k.sb("bias_sc", [P, O_C])
        s = k.sb("s_sc", [P, NSC])
        hh = k.sb("hh", [P, 2, CG * NCS])
        he = k.sb("he", [P, CG * NCS])
        kc = k.sb("kc", [P, CG * NCS])
        vc = k.sb("vc", [NCS, CKV])
        pct = k.sb("pct", [NCS, P])
        t1 = k.sb("t1", [P, NSEL])
        rank = k.sb("rank", [P, 3, NSEL])
        m8 = k.sb("m8", [P, 2, 8])
        st = k.sb("st_sc", [P, 3, 4])
        sums = k.sb("sums_sc", [P, 4])
        ov = k.sb("ov", [NCS, NSEL])
        hs = k.sb("hs", [P, P])
        gt = k.sb("gt", [P, 3, NB])
        oc = k.sb("oc", [P, HD])
        orow = k.sb("orowc", [P, HD])
        ot = k.sb("otc", [P, CH, NS])
        xb = [k.ps(f"xb{i}", [P, 512]) for i in range(2)]
        sb_ = [k.ps(f"scb{i}", [P, 512]) for i in range(2)]
        hb, mb, m2, ob = (k.ps(n, [P, 512]) for n in ("hb", "mb", "m2", "ob"))
        MC, MT1, MIMP = 16, 144, 184

        NPIECE = 4
        pt_in = k.sem("pt_in")
        raw_in = [k.sem(f"raw_in{i}") for i in range(NPIECE)]
        sel_in = [k.sem(f"sel_in{i}") for i in range(NPIECE)]
        win_in, vn_in, small_in, bias_in, gt_in = (k.sem(n) for n in ("win_in", "vnc_in", "smallc_in", "biasc_in", "gt_in"))
        zeroed, scaled, qc_ready, turned, evac_a, evac_d, score_q, s_evac = (
            k.sem(n) for n in ("zc_set", "qsc_scaled", "qc_ready", "c_turns", "c_evac_a", "c_evac_d", "c_scoreq", "c_sevac"))
        h_done, h_exp, hh_ready, w2_done, kc_ready, cs_done, new_done = (
            k.sem(n) for n in ("h_done", "h_exp", "hh_ready", "w2_done", "kc_ready", "cs_done", "new_done"))
        max_c, exp_c, pc_ready, pct_done, pct_ready, t1_done, t1_ready, imp_done = (
            k.sem(n) for n in ("max_c", "exp_c", "pc_ready", "pct_done", "pct_ready", "t1_done", "t1_ready", "imp_done"))
        max_w, exp_w, pw_ready, max_s, exp_s = (k.sem(n) for n in ("max_w", "exp_w", "pw_ready", "max_s", "exp_s"))
        imp_seen = k.sem("imp_seen")
        chain, pv_q, o_evac, o_turned, o_ready, o_stored, rows_out, copied = (
            k.sem(n) for n in ("sc_chain", "pv_q", "oc_evac", "oc_turned", "oc_ready", "oc_stored", "rows_out", "copied6"))
        TX, TW, TS, TP = 0, NPG, NPG + 2, NPG + 10
        NT = TP + 6
        CHAIN = 25

        with nc.Block() as block:
            @block.sync
            def _(sp):
                cmp.sync(sp)
                for i in range(4):
                    sp.dma_start(qs[:, 4 * i:4 * i + 4, :], k.z2[i * 512:(i + 1) * 512, NP:T].rearrange("(h d) t -> d h t", d=HD)).then_inc(small_in, 16)
                for i, c in enumerate((C_KS, C_KW)):
                    sp.dma_start(kn[:, i, :, :], k.z2[c:c + CKV, NP:T].rearrange("(g d) t -> d g t", d=HD)).then_inc(small_in, 16)
                sp.dma_start(ov[:, :], k.c_overlap).then_inc(small_in, 16)
                sp.dma_start(hs[:, :], k.c_hsum).then_inc(small_in, 16)

                def load(b, first=False):
                    def pages(dst, sems, lo, hi, frees, free_at):
                        for pg in range(NPG):
                            n = pg * NPIECE // NPG
                            if not first and pg % (NPG // NPIECE) == 0:
                                sp.wait_ge(frees, free_at(n))
                                settle(sp, k)
                            page = sp.value_load(k.page_table[bass.ds(b, 1), pg:pg + 1], min_val=0, max_val=k.cache_c_kv.shape[0] - 1)
                            sp.dma_start(dst[:, pg, :], k.cache_c_kv[bass.ds(page, 1)].rearrange("a t c g d -> (a t) (c g d)")[:, lo:hi]
                                         ).then_inc(sems[n], 16)

                    pages(raw, raw_in, 0, 2 * CKV, turned, lambda n: b * NT - NT + NPG // NPIECE * (n + 1))
                    if not first:
                        sp.wait_ge(pv_q, b * 6 - 5)
                    sp.dma_start(win[:, :, :], k.cache_c_win[bass.ds(b, 1)].rearrange("a (r p) c g d -> p (a r) (c g d)", p=P)).then_inc(win_in, 16)
                    pages(sel, sel_in, 2 * CKV, 4 * CKV, pv_q, lambda n: b * 6 - 6 + (2 + n))
                    if not first:
                        sp.wait_ge(pv_q, b * 6)
                    sp.dma_start(vn[:, 0, :], k.kv2[bass.ds(b * NQ + NP, NQ), 3 * CKV:4 * CKV]).then_inc(vn_in, 16)
                    sp.dma_start(vn[:, 1, :], k.kv2[bass.ds(b * NQ + NP, NQ), 5 * CKV:6 * CKV]).then_inc(vn_in, 16)

                load(0, True)
                with sp.Fori(1, NB) as b:
                    load(b)
                sp.wait_ge(o_ready, NB)
                sp.dma_start(k.mt[:, NP:T].rearrange("(h d) t -> d h t", d=HD), ot[:, :, :]).then_inc(o_stored, 16)
                sp.wait_ge(o_stored, 16)

            @block.gpsimd
            def _(pool):
                link = Chain(pool, zeroed)
                link(pool.memset(qc[:, :, :], 0.0))
                link(pool.memset(rank[:, 0, :], 1.0e30))
                for g in range(CG):
                    for i in range(NQ):
                        r = (g * NQ + i) * CHG
                        pool.dma_start(bias[r:r + CHG, O_S:O_S + PAST + NQ], k.tab_hc[g * CHG:(g + 1) * CHG, NQ - 1 - i:NQ - 1 - i + PAST + NQ]).then_inc(bias_in, 16)
                        pool.dma_start(bias[r:r + CHG, O_W:O_W + WIN + NQ], k.tab_hw[g * CHG:(g + 1) * CHG, NQ - 1 - i:NQ - 1 - i + WIN + NQ]).then_inc(bias_in, 16)
                    for br in range(3):
                        pool.dma_start(gt[g * 64:(g + 1) * 64, br, :],
                                       dram_ap(k.gates_s, (br * CH + g * CHG) * NS, [(NB, NQ), (NS, CHG), (1, NB)])).then_inc(gt_in, 16)
                n = 0
                for dst, c0, c1 in ((k.out_rows_p, 0, 4 * CKV), (k.out_win_p, 4 * CKV, 6 * CKV)):
                    pool.dma_start(dst.rearrange("t c g d -> t (c g d)"), k.kv2[0:NP, c0:c1]).then_inc(rows_out, 16)
                    n += 1
                pool.dma_start(k.out_rows_s.rearrange("b t c g d -> (b t) (c g d)"), k.kv2[NP:T, 0:4 * CKV]).then_inc(rows_out, 16)
                n += 1
                for b in range(NB):
                    pool.dma_start(k.out_win_s[b, 0:WIN - NQ].rearrange("t c g d -> t (c g d)"), k.cache_c_win[b, NQ:WIN].rearrange("t c g d -> t (c g d)")).then_inc(rows_out, 16)
                    pool.dma_start(k.out_win_s[b, WIN - NQ:WIN].rearrange("t c g d -> t (c g d)"), k.kv2[NP + b * NQ:NP + (b + 1) * NQ, 4 * CKV:]).then_inc(rows_out, 16)
                    n += 2
                pool.wait_ge(scaled, 1)

                def fill_q(b):
                    wait(pool, score_q, b * 10)
                    wait(pool, cs_done, b * 1)
                    for g in range(CG):
                        pool.tensor_copy(qc[:, g, g * 64:(g + 1) * 64].rearrange("p (i h) -> p h i", h=CHG),
                                         qs[:, g * CHG:(g + 1) * CHG, bass.ds(b * NQ, NQ)]).then_inc(qc_ready, 1)

                def copy_kept(b):
                    row = 2 * NH * HD
                    for g, part, parts, m in ((1, 0, 1, 2 * (GROUPS[1][0] - NQ)), (2, 3, 4, 816)):
                        keep = (GROUPS[g][0] - NQ) // parts
                        dst, src = (a.rearrange("b t a h d -> b (t a h d)")[bass.ds(b, 1), (lo + part * keep) * row:(lo + (part + 1) * keep) * row]
                                    .rearrange("b (m n) -> (b m) n", m=m) for a, lo in ((k.out_a_s[g], 0), (k.cache_a[g], NQ)))
                        pool.dma_start(dst, src).then_inc(copied, 16)

                fill_q(0)
                copy_kept(0)
                with pool.Fori(1, NB) as b:
                    fill_q(b)
                    copy_kept(b)
                pool.wait_ge(copied, 2 * 16 * NB)
                pool.wait_ge(rows_out, 16 * n)

            def evac(eng, b, q, copy, sem):
                eng.wait_ge(turned, b * NT + (q + 1))
                bank = xb[q % 2]
                if q < TW:
                    copy(xt[:, :, q * P:(q + 1) * P], bank[:, :].rearrange("p (c n) -> p c n", c=4)).then_inc(sem, 1)
                elif q < TP:
                    if q >= TW + 2:
                        eng.wait_ge(score_q, b * 10 + (q - TW - 1))
                    copy(ktt[:, q % 2, :, :], bank[:, :].rearrange("p (c n) -> p c n", c=4)).then_inc(sem, 1)
                else:
                    if q >= TP + 2:
                        eng.wait_ge(pv_q, b * 6 + (q - TP - 1))
                    if q < TP + 5:
                        copy(ptt[:, q % 2, :, :], bank[:, :].rearrange("p (c n) -> p c n", c=4)).then_inc(sem, 1)
                    else:
                        copy(ptt[0:NQ, q % 2, 0:2, :], bank[0:NQ, 0:2 * P].rearrange("p (c n) -> p c n", c=2)).then_inc(sem, 1)

            @block.scalar
            def _(act):
                act.wait_ge(cmp.ready, 2)

                def one(b):
                    def ev(q):
                        evac(act, b, q, act.copy, evac_a)

                    for q in range(0, TW, 2):
                        ev(q)
                    for i in range(2):
                        act.wait_ge(h_done, b * 2 + (i + 1))
                        if i:
                            act.wait_ge(hh_ready, b * 2 + i)
                        else:
                            wait(act, hh_ready, b * 2)
                        act.activation(he[:, :], (hb, m2)[i][:, 0:CG * NCS], ACT.Exp, bias=cmp.nbias[:, i:i + 1], scale=-1.0).then_inc(h_exp, 1)
                    for q in (16, 18, 20, 22):
                        ev(q)
                    act.wait_ge(max_c, b + 1)
                    act.activation(s[:, O_C:], mb[:, MC:MC + NCS], ACT.Exp, bias=st[:, 0, 1:2], accum_out=st[:, 0, 2:3]).then_inc(exp_c, 1)
                    ev(24)
                    act.wait_ge(max_w, b + 1)
                    act.activation(s[:, O_W:O_S], s[:, O_W:O_S], ACT.Exp, bias=st[:, 1, 1:2], accum_out=st[:, 1, 2:3]).then_inc(exp_w, 1)
                    ev(26)
                    act.wait_ge(max_s, b + 1)
                    for i in range(4):
                        lo, hi = O_S + i * 4 * P, O_S + (i + 1) * 4 * P + NQ * (i == 3)
                        act.activation(s[:, lo:hi], s[:, lo:hi], ACT.Exp, bias=st[:, 2, 1:2], accum_out=sums[:, i:i + 1]).then_inc(exp_s, 1)
                    ev(28)
                    ev(30)

                one(0)
                with act.Fori(1, NB) as b:
                    one(b)

            @block.tensor
            def _(pe):
                cmp.pe(pe, hb)
                pe.wait_ge(cmp.ready, 2)
                pe.wait_ge(small_in, 128)

                def turn(b, q):
                    if q >= 2:
                        pe.wait_ge((evac_a, evac_d)[q % 2], b * (NT // 2) + q // 2)
                    else:
                        wait(pe, (evac_a, evac_d)[q % 2], b * (NT // 2))
                    if q < TW:
                        if q % (NPG // NPIECE) == 0:
                            pe.wait_ge(raw_in[q * NPIECE // NPG], b * 64 + 64)
                        src = [raw[:, q, j * P:(j + 1) * P] for j in range(4)]
                    elif q < TS:
                        if q == TW:
                            pe.wait_ge(win_in, b * 16 + 16)
                        src = [win[:, 2 * (q - TW) + j, g * P:(g + 1) * P] for j in range(2) for g in range(CG)]
                    elif q < TP:
                        if (q - TS) % 2 == 0:
                            pe.wait_ge(sel_in[(q - TS) // 2], b * 64 + 64)
                        src = [sel[:, 2 * (q - TS) + j, g * P:(g + 1) * P] for j in range(2) for g in range(CG)]
                    elif q == TP:
                        pe.wait_ge(pw_ready, b + 1)
                        src = [s[:, O_W + j * P:O_W + (j + 1) * P] for j in range(4)]
                    elif q < TP + 5:
                        pe.wait_ge(exp_s, b * 4 + (q - TP))
                        o = O_S + (q - TP - 1) * 4 * P
                        src = [s[:, o + j * P:o + (j + 1) * P] for j in range(4)]
                    else:
                        settle(pe, k)
                        for j, o in enumerate((O_SN, O_WN)):
                            ins = pe.transpose(xb[q % 2][0:NQ, j * P:(j + 1) * P], s[:, o:o + NQ], k.ident[:, :])
                        ins.then_inc(turned, 1)
                        return
                    for j in range(4):
                        ins = pe.transpose(xb[q % 2][:, j * P:(j + 1) * P], src[j], k.ident[:, :])
                    ins.then_inc(turned, 1)

                def score(b, n):
                    q = TW + n
                    fill = n // 2
                    pe.wait_ge((evac_a, evac_d)[q % 2], b * (NT // 2) + (q // 2 + 1))
                    if n % 2 == 0:
                        if fill >= 2:
                            pe.wait_ge(s_evac, b * 5 + (fill - 1))
                        else:
                            wait(pe, s_evac, b * 5)
                    for j in range(2):
                        o = (n % 2) * 2 * P + j * P
                        for g in range(CG):
                            ins = pe.matmul(sb_[fill % 2][:, o:o + P], qc[:, g, :], ktt[:, q % 2, 2 * j + g, :], start=(g == 0), stop=(g == CG - 1))
                    ins.then_inc(score_q, 1)

                def values(b, n):
                    q = TP + n
                    pe.wait_ge((evac_a, evac_d)[q % 2], b * (NT // 2) + (q // 2 + 1))
                    if n == 5:
                        pe.wait_ge(vn_in, b * 32 + 32)
                    for j in range(4 if n < 5 else 2):
                        if n == 0:
                            w, v = ptt[:, q % 2, j, :], win[:, j, CKV:2 * CKV]
                        elif n < 5:
                            w, v = ptt[:, q % 2, j, :], sel[:, (n - 1) * 4 + j, CKV:2 * CKV]
                        else:
                            w, v = ptt[0:NQ, q % 2, j, :], vn[:, j, :]
                        if n == 0 or (n, j) == (5, 1):
                            ins = pe.matmul(ob[:, CKV:2 * CKV], w, v, start=(n == 0 and j == 0), stop=(n == 5))
                        else:
                            ins = pe.matmul(hb[:, 0:CKV], w, v, start=(n == 1 and j == 0), stop=(n == 5))
                    ins.then_inc(pv_q, 1)

                def one(b):
                    for q in range(TW):
                        turn(b, q)
                    for i in range(2):
                        if i == 0:
                            pe.wait_ge(evac_a, b * (NT // 2) + TW // 2)
                            pe.wait_ge(evac_d, b * (NT // 2) + TW // 2)
                            wait(pe, o_ready, b * 1)
                        for l in range(CB):
                            ins = pe.matmul((hb, m2)[i][:, 0:CG * NCS], cmp.w1[:, i, l, :],
                                            xt[:, 2 * i:2 * i + 2, l:l + CS * (NCS - 1) + 1:CS], start=(l == 0), stop=(l == CB - 1))
                        ins.then_inc(h_done, 1)
                    turn(b, TW)
                    turn(b, TW + 1)
                    pe.wait_ge(qc_ready, b * 2 + 2)
                    wait(pe, imp_seen, b * 1)
                    for i, o in ((1, 0), (0, NQ)):
                        for g in range(CG):
                            ins = pe.matmul(mb[:, o:o + NQ], qc[:, g, :], kn[:, i, g, bass.ds(b * NQ, NQ)], start=(g == 0), stop=(g == CG - 1))
                    ins.then_inc(new_done, 1)
                    for n in range(10):
                        score(b, n)
                        if n == 3:
                            pe.wait_ge(hh_ready, b * 2 + 2)
                            pe.matmul(hb[:, 0:CG * NCS], cmp.w2[:, 0, :], hh[:, 0, :], start=True, stop=True)
                            for g in range(CG):
                                ins = pe.matmul(hb[0:NCS, CG * NCS + g * HD:CG * NCS + (g + 1) * HD], hh[:, 1, g * NCS:(g + 1) * NCS], cmp.w2[:, 1, :], start=True, stop=True)
                            ins.then_inc(w2_done, 1)
                        if n == 4:
                            pe.wait_ge(kc_ready, b * 2 + 2)
                            for g in range(CG):
                                ins = pe.matmul(mb[:, MC:MC + NCS], qc[:, g, :], kc[:, g * NCS:(g + 1) * NCS], start=(g == 0), stop=(g == CG - 1))
                            ins.then_inc(cs_done, 1)
                        if n == 6:
                            pe.wait_ge(pc_ready, b + 1)
                            settle(pe, k)
                            pe.transpose(m2[0:NCS, 0:P], s[:, O_C:], k.ident[:, :]).then_inc(pct_done, 1)
                        if n == 7:
                            pe.wait_ge(pct_ready, b + 1)
                            pe.matmul(mb[:, MT1:MT1 + NSEL], pct[:, :], ov[:, :], start=True, stop=True).then_inc(t1_done, 1)
                        if n == 8:
                            pe.wait_ge(t1_ready, b + 1)
                            pe.matmul(mb[:, MIMP:MIMP + NSEL], hs[:, :], t1[:, :], start=True, stop=True).then_inc(imp_done, 1)
                        if n + 2 < 10:
                            turn(b, TW + n + 2)
                    turn(b, TP)
                    wait(pe, o_evac, b * 2)
                    pe.matmul(ob[:, 0:CKV], pct[:, :], vc[:, :], start=True, stop=True)
                    values(b, 0)
                    turn(b, TP + 1)
                    for n in range(1, 6):
                        if n < 5:
                            turn(b, TP + n + 1)
                        values(b, n)
                    pe.wait_ge(o_evac, b * 2 + 2)
                    settle(pe, k)
                    pe.transpose(m2[:, 0:P], orow[:, :], k.ident[:, :]).then_inc(o_turned, 1)

                one(0)
                with pe.Fori(1, NB) as b:
                    one(b)

            @block.vector
            def _(dve):
                cmp.dve(dve, hb)
                dve.wait_ge(small_in, 128)
                dve.tensor_scalar(qs[:, :, :], qs[:, :, :], SCALE, None, ALU.mult).then_inc(scaled, 1)
                dve.wait_ge(zeroed, 2)
                dve.wait_ge(bias_in, 16 * 32)
                dve.wait_ge(gt_in, 16 * 6)

                def one(b):
                    link = Chain(dve, chain, b * CHAIN)

                    def ev(q):
                        evac(dve, b, q, dve.tensor_copy, evac_d)

                    def hidden(i):
                        dve.wait_ge(h_exp, b * 2 + (i + 1))
                        wait(dve, w2_done, b * 1)
                        link(dve.tensor_scalar(he[:, :], he[:, :], 1.0, None, ALU.add))
                        link(dve.reciprocal(he[:, :], he[:, :]))
                        dve.scalar_tensor_tensor(hh[:, i, :], (hb, m2)[i][:, 0:CG * NCS], cmp.bias[:, i:i + 1], he[:, :],
                                                 ALU.add, ALU.mult).then_inc(hh_ready, 1)

                    def fill(f):
                        dve.wait_ge(score_q, b * 10 + (2 * f + 2))
                        o = O_W if f == 0 else O_S + (f - 1) * 4 * P
                        dve.tensor_tensor(s[:, o:o + 4 * P], sb_[f % 2][:, :], bias[:, o:o + 4 * P], ALU.add).then_inc(s_evac, 1)

                    for q in range(1, TW, 2):
                        ev(q)
                    hidden(0)
                    ev(17)
                    hidden(1)
                    fill(0)
                    dve.wait_ge(new_done, b + 1)
                    link(dve.tensor_tensor(s[:, O_WN:O_WN + NQ], mb[:, 0:NQ], bias[:, O_WN:O_WN + NQ], ALU.add))
                    link(dve.tensor_tensor(s[:, O_SN:O_SN + NQ], mb[:, NQ:2 * NQ], bias[:, O_SN:O_SN + NQ], ALU.add))
                    ev(19)
                    fill(1)
                    dve.wait_ge(w2_done, b + 1)
                    dve.tensor_copy(kc[:, :], hb[:, 0:CG * NCS]).then_inc(kc_ready, 1)
                    dve.tensor_copy(vc[:, :], hb[0:NCS, CG * NCS:CG * NCS + CKV]).then_inc(kc_ready, 1)
                    ev(21)
                    dve.wait_ge(cs_done, b + 1)
                    link(dve.tensor_reduce(st[:, 0, 0:1], mb[:, MC:MC + NCS], AX, ALU.max))
                    dve.tensor_scalar(st[:, 0, 1:2], st[:, 0, 0:1], -1.0, None, ALU.mult).then_inc(max_c, 1)
                    fill(2)
                    ev(23)
                    dve.wait_ge(exp_c, b + 1)
                    link(dve.reciprocal(st[:, 0, 3:4], st[:, 0, 2:3]))
                    dve.tensor_scalar(s[:, O_C:], s[:, O_C:], st[:, 0, 3:4], None, ALU.mult).then_inc(pc_ready, 1)
                    dve.wait_ge(s_evac, b * 5 + 1)
                    link(dve.tensor_reduce(st[:, 1, 0:1], s[:, O_W:O_S], AX, ALU.max))
                    dve.tensor_scalar(st[:, 1, 1:2], st[:, 1, 0:1], -1.0, None, ALU.mult).then_inc(max_w, 1)
                    dve.wait_ge(pct_done, b + 1)
                    dve.tensor_copy(pct[:, :], m2[0:NCS, 0:P]).then_inc(pct_ready, 1)
                    fill(3)
                    dve.wait_ge(t1_done, b + 1)
                    dve.tensor_copy(t1[:, :], mb[:, MT1:MT1 + NSEL]).then_inc(t1_ready, 1)
                    ev(25)
                    dve.wait_ge(exp_w, b + 1)
                    link(dve.reciprocal(st[:, 1, 3:4], st[:, 1, 2:3]))
                    dve.tensor_scalar(s[:, O_W:O_S], s[:, O_W:O_S], st[:, 1, 3:4], gt[:, 2, bass.ds(b, 1)],
                                      ALU.mult, ALU.mult).then_inc(pw_ready, 1)
                    dve.wait_ge(imp_done, b + 1)
                    dve.tensor_copy(rank[:, 0, 1:NSEL - 2], mb[:, MIMP + 1:MIMP + NSEL - 2]).then_inc(imp_seen, 1)
                    dve.wait_ge(imp_seen, b + 1)
                    for i in range(2):
                        settle(dve, k)
                        link(dve.max(m8[:, i, :], rank[:, i, :]))
                        settle(dve, k)
                        link(dve.match_replace(rank[:, i + 1, :], m8[:, i, :], rank[:, i, :], -1.0))
                    link(dve.tensor_scalar(rank[:, 2, :], rank[:, 2, :], 0.0, MASK, ALU.is_ge, ALU.mult))
                    link(dve.tensor_reduce(st[:, 2, 0:1], s[:, O_SN:O_SN + NQ], AX, ALU.max))
                    fill(4)
                    dve.wait_ge(s_evac, b * 5 + 5)
                    settle(dve, k)
                    sv = s[:, O_S:O_S + PAST].rearrange("p (n c) -> p n c", c=SELB)
                    link(dve.tensor_tensor_reduce(sv, sv, rank[:, 2, 0:NSEL - 1].unsqueeze(2).broadcast_to([P, NSEL - 1, SELB]), 1.0,
                                                  st[:, 2, 0:1], ALU.add, ALU.max, st[:, 2, 1:2]))
                    link(dve.tensor_scalar(st[:, 2, 1:2], st[:, 2, 1:2], -1.0, None, ALU.mult))
                    dve.sem_inc(max_s, 1)
                    for q in (27, 29, 31):
                        ev(q)
                    dve.wait_ge(exp_s, b * 4 + 4)
                    link(dve.tensor_reduce(st[:, 2, 2:3], sums[:, :], AX, ALU.add))
                    link(dve.reciprocal(st[:, 2, 3:4], st[:, 2, 2:3]))
                    link(dve.tensor_tensor(st[:, 2, 3:4], st[:, 2, 3:4], gt[:, 1, bass.ds(b, 1)], ALU.mult))
                    dve.wait_ge(pv_q, b * 6 + 6)
                    for g in range(CG):
                        rows = slice(g * 64, (g + 1) * 64)
                        link(dve.tensor_scalar(oc[rows, :], ob[rows, g * HD:(g + 1) * HD], gt[rows, 0, bass.ds(b, 1)], None, ALU.mult))
                        link(dve.scalar_tensor_tensor(oc[rows, :], hb[rows, g * HD:(g + 1) * HD], st[rows, 2, 3:4], oc[rows, :], ALU.mult, ALU.add))
                        dve.tensor_tensor(orow[rows, :], ob[rows, CKV + g * HD:CKV + (g + 1) * HD], oc[rows, :], ALU.add).then_inc(o_evac, 1)
                    dve.wait_ge(o_turned, b + 1)
                    dve.tensor_copy(ot[:, :, bass.ds(b * NQ, NQ)].rearrange("p (g h) i -> p g h i", g=CG),
                                    m2[:, 0:P].rearrange("p (g i h) -> p g h i", g=CG, h=CHG)).then_inc(o_ready, 1)
                    assert link.n == CHAIN, link.n

                one(0)
                with dve.Fori(1, NB) as b:
                    one(b)


def block_prompt_c(nc, k):
    with k.scope():
        cmp = k.compress
        xk = k.sb("xkp", [P, 4, NP])
        kk = k.sb("kkp", [P, 2, CG, NP])
        v = k.sb("vvp", [P, 2, 2, CKV])
        q_all = k.sb("qpa_c", [P, CG, CHG, NP])
        q = k.sb("qpc", [P, CG, NP])
        tab = k.sb("tpc", [P, CG, NP])
        cmask = k.sb("cmask", [P, 2, NCP])
        gr = k.sb("gpc", [P, 2, 3, CH])
        hh = k.sb("hhp", [P, 2, CG * NCP])
        he = k.sb("hep", [P, CG * NCP])
        kc = k.sb("kcp", [P, CG * NCP])
        vc = k.sb("vcp", [NCP, CKV])
        sc = k.sb("scp", [P, CG, 2, 3, NP])
        pt = k.sb("ptpc", [P, CG, 6, P])
        pc = k.sb("pcpc", [NCP, CG, 2, P])
        st = k.sb("stpc", [P, CG, 2, 4, 3])
        ot = k.sb("otpc", [P, CG, CHG, NP])
        sps = [k.ps(f"spc{i}", [P, 1024]) for i in range(2)]
        tps = [k.ps(f"tpp{i}", [P, 512]) for i in range(3)]
        ops = k.ps("opc", [P, 512])
        hidden = (tps[1], sps[0])
        in_, kv_in, gates_in = k.sem("pc_in"), k.sem("pc_kv_in"), k.sem("pc_gates_in")
        h_done, h_exp, hh_ready, w2_done, kc_ready = (k.sem(n) for n in ("hp_done", "hp_exp", "hhp_ready", "w2p_done", "kcp_ready"))
        loaded = [k.sem(f"pc_loaded{u}") for u in range(CG)]
        q_in, scaled, scored, max_done, exp_done, p_ready, chain, score_chain, weight_chain = (
            k.sem(n) for n in ("pc_q_in", "pc_scaled", "pc_scored", "pc_max", "pc_exp", "pc_p", "pc_chain", "pc_chain_s", "pc_chain_w"))
        turned, pt_act, pt_dve, pv_done, o_ready, stored, copied = (
            k.sem(n) for n in ("pc_turned", "pc_pt_act", "pc_pt_dve", "pc_pv", "pc_o", "pc_stored", "copied7"))

        def steps(eng, step):
            for n in (-1, 0, 1):
                step(0, n)
            with eng.Fori(1, CHG - 1) as it:
                step(it, 0)
                step(it, 1)
            for n in range(CH - 2, CH + 2):
                step(0, n)

        def on(it, m):
            return not isinstance(it, int) or 0 <= 2 * it + m < CH

        def head(it, m):
            return bass.ds(it + m // 2, 1), m % 2

        with nc.Block() as block:
            @block.sync
            def _(sp):
                sp.dma_start(xk[:, :, :], k.z2[C_KC:C_KC + 2 * CKV, 0:NP].rearrange("(c p) t -> p c t", p=P)).then_inc(in_, 16)
                for i, c in enumerate((C_KS, C_KW)):
                    sp.dma_start(kk[:, i, :, :], k.z2[c:c + CKV, 0:NP].rearrange("(g d) t -> d g t", d=HD)).then_inc(kv_in, 16)
                for i, c in enumerate((3 * CKV, 5 * CKV)):
                    sp.dma_start(v[:, :, i, :], k.kv2[0:NP, c:c + CKV].rearrange("(t p) n -> p t n", p=P)).then_inc(kv_in, 16)
                sp.dma_start(cmask[:, :, :], k.c_cmask).then_inc(gates_in, 16)
                sp.dma_start(gr[:, :, :, :].rearrange("p t r h -> p t (r h)"), k.gates.rearrange("(t p) n -> p t n", p=P)).then_inc(gates_in, 16)

                def load_table(j, g):
                    sp.dma_start(tab[:, g, :], k.toe_c[bass.ds(j + g * CHG, 1)].rearrange("a p n -> (a p) n")).then_inc(loaded[g], 16)

                for g in range(CG):
                    load_table(0, g)
                with sp.Fori(1, CHG) as j:
                    for g in range(CG):
                        sp.wait_ge(max_done, j * 4 + (2 * g - 2))
                        load_table(j, g)
                sp.wait_ge(o_ready, CH)
                for g in range(CG):
                    sp.dma_start(k.mt[g * CHG * HD:(g + 1) * CHG * HD, 0:NP].rearrange("(j d) t -> d j t", d=HD), ot[:, g, :, :]).then_inc(stored, 16)
                sp.wait_ge(stored, 32)

            @block.gpsimd
            def _(pool):
                for g in range(CG):
                    pool.dma_start(q_all[:, g, :, :], k.z2[g * CHG * HD:(g + 1) * CHG * HD, 0:NP].rearrange("(j d) t -> d j t", d=HD)).then_inc(q_in, 16)
                for n, p in enumerate(k.cache_pieces[23:]):
                    pool.wait_ge(pv_done, n + 3)
                    pool.dma_start(*p).then_inc(copied, 16)
                pool.wait_ge(copied, 16 * len(k.cache_pieces[23:]))

            @block.scalar
            def _(act):
                for i in range(2):
                    act.wait_ge(h_done, i + 1)
                    wait(act, hh_ready, i)
                    act.activation(he[:, :], hidden[i][:, 0:CG * NCP], ACT.Exp, bias=cmp.nbias[:, i:i + 1], scale=-1.0).then_inc(h_exp, 1)

                def step(it, m):
                    if on(it, m - 1):
                        u = (m - 1) % 2
                        act.wait_ge(pv_done, it * 2 + m)
                        act.wait_ge(turned, it * 6 + (3 * m - 2))
                        act.copy(pt[:, u, 0:2, :], tps[0][:, 0:2 * P].rearrange("p (c n) -> p c n", n=P)).then_inc(pt_act, 1)
                        act.wait_ge(turned, it * 6 + 3 * m)
                        act.copy(pc[:, u, :, :], tps[2][0:NCP, 0:2 * P].rearrange("p (c n) -> p c n", n=P)).then_inc(pt_act, 1)
                    if on(it, m + 1):
                        u = (m + 1) % 2
                        for qb in range(2):
                            act.wait_ge(max_done, it * 4 + (2 * m + 3 + qb))
                            nk = P * (qb + 1)
                            for r, w in enumerate((NCP, nk, nk)):
                                act.activation(sc[:, u, qb, r, 0:w], sc[:, u, qb, r, 0:w], ACT.Exp, bias=st[:, u, qb, 1, r:r + 1],
                                               accum_out=st[:, u, qb, 2, r:r + 1]).then_inc(exp_done, 1)

                steps(act, step)

            @block.tensor
            def _(pe):
                pe.sem_inc(pv_done, 2)
                pe.wait_ge(in_, 16)
                for i in range(2):
                    for l in range(CB):
                        ins = pe.matmul(hidden[i][:, 0:CG * NCP], cmp.w1[:, i, l, :],
                                        xk[:, 2 * i:2 * i + 2, l:l + CS * (NCP - 1) + 1:CS], start=(l == 0), stop=(l == CB - 1))
                    ins.then_inc(h_done, 1)
                pe.wait_ge(hh_ready, 2)
                pe.matmul(ops[:, 0:CG * NCP], cmp.w2[:, 0, :], hh[:, 0, :], start=True, stop=True)
                for g in range(CG):
                    ins = pe.matmul(tps[2][0:NCP, g * HD:(g + 1) * HD], hh[:, 1, g * NCP:(g + 1) * NCP], cmp.w2[:, 1, :], start=True, stop=True)
                ins.then_inc(w2_done, 1)
                pe.wait_ge(kc_ready, 2)
                pe.wait_ge(kv_in, 64)

                def step(it, m):
                    if on(it, m + 1):
                        g = (m + 1) % 2
                        pe.wait_ge(scaled, it * 2 + (m + 2))
                        for qb in range(2):
                            nk = P * (qb + 1)
                            qq = q[:, g, qb * P:(qb + 1) * P]
                            wait(pe, max_done, it * 4 + (2 * m + 1 + qb) if on(it, m) else 0)
                            pe.matmul(sps[qb][:, 0:NCP], qq, kc[:, g * NCP:(g + 1) * NCP], start=True, stop=True)
                            pe.matmul(sps[qb][:, 16:16 + nk], qq, kk[:, 0, g, 0:nk], start=True, stop=True)
                            pe.matmul(sps[qb][:, 512:512 + nk], qq, kk[:, 1, g, 0:nk], start=True, stop=True).then_inc(scored, 1)
                    if on(it, m - 1):
                        g = (m - 1) % 2
                        pe.wait_ge(pt_act, it * 4 + 2 * m)
                        pe.wait_ge(pt_dve, it * 2 + m)
                        wait(pe, o_ready, it * 2 + (m - 1))
                        for qb in range(2):
                            pe.matmul(ops[:, qb * P:(qb + 1) * P], vc[:, g * HD:(g + 1) * HD], pc[:, g, qb, :], start=True, stop=False)
                            for r in range(2):
                                for h in range(qb + 1):
                                    ins = pe.matmul(ops[:, qb * P:(qb + 1) * P], v[:, h, r, g * HD:(g + 1) * HD],
                                                    pt[:, g, r if qb == 0 else 2 + 2 * r + h, :], start=False, stop=(r == 1 and h == qb))
                        ins.then_inc(pv_done, 1)
                    if on(it, m):
                        u = m % 2
                        pe.wait_ge(p_ready, it * 4 + (2 * m + 1))
                        wait(pe, pt_act, it * 4 + 2 * m)
                        wait(pe, pt_dve, it * 2 + m)
                        settle(pe, k)
                        for r in range(2):
                            ins = pe.transpose(tps[0][:, r * P:(r + 1) * P], sc[:, u, 0, 1 + r, 0:P], k.ident[:, :])
                        ins.then_inc(turned, 1)
                        pe.wait_ge(p_ready, it * 4 + (2 * m + 2))
                        for r in range(2):
                            for h in range(2):
                                ins = pe.transpose(tps[1][:, (2 * r + h) * P:(2 * r + h + 1) * P], sc[:, u, 1, 1 + r, h * P:(h + 1) * P], k.ident[:, :])
                        ins.then_inc(turned, 1)
                        for qb in range(2):
                            ins = pe.transpose(tps[2][0:NCP, qb * P:(qb + 1) * P], sc[:, u, qb, 0, 0:NCP], k.ident[:, :])
                        ins.then_inc(turned, 1)

                steps(pe, step)

            @block.vector
            def _(dve):
                link = Chain(dve, chain)
                for i in range(2):
                    dve.wait_ge(h_exp, i + 1)
                    link(dve.tensor_scalar(he[:, :], he[:, :], 1.0, None, ALU.add))
                    link(dve.reciprocal(he[:, :], he[:, :]))
                    dve.scalar_tensor_tensor(hh[:, i, :], hidden[i][:, 0:CG * NCP], cmp.bias[:, i:i + 1], he[:, :],
                                             ALU.add, ALU.mult).then_inc(hh_ready, 1)
                dve.wait_ge(w2_done, 1)
                dve.tensor_copy(kc[:, :], ops[:, 0:CG * NCP]).then_inc(kc_ready, 1)
                dve.tensor_copy(vc[:, :], tps[2][0:NCP, 0:CKV]).then_inc(kc_ready, 1)
                dve.wait_ge(gates_in, 32)
                dve.wait_ge(q_in, 32)

                def step(it, m):
                    if on(it, m + 1):
                        j, g = head(it, m + 1)
                        dve.tensor_scalar(q[:, g, :].unsqueeze(1), q_all[:, g, j, :], SCALE, None, ALU.mult).then_inc(scaled, 1)
                    if on(it, m - 2):
                        j, g = head(it, m - 2)
                        dve.wait_ge(pv_done, it * 2 + (m + 1))
                        dve.tensor_copy(ot[:, g, j, :], ops[:, 0:NP].unsqueeze(1)).then_inc(o_ready, 1)
                    if on(it, m - 1):
                        u = (m - 1) % 2
                        dve.wait_ge(pv_done, it * 2 + m)
                        dve.wait_ge(turned, it * 6 + (3 * m - 1))
                        dve.tensor_copy(pt[:, u, 2:6, :], tps[1][:, :].rearrange("p (c n) -> p c n", n=P)).then_inc(pt_dve, 1)
                    if on(it, m):
                        u = m % 2
                        link = Chain(dve, weight_chain, it * 12 + 6 * m)
                        for qb in range(2):
                            nk = P * (qb + 1)
                            s = st[:, u, qb]
                            dve.wait_ge(exp_done, it * 12 + (6 * m + 3 * qb + 3))
                            link(dve.tensor_scalar(s[:, 2, :], s[:, 2, :], 1.0e-30, None, ALU.max))
                            link(dve.reciprocal(s[:, 3, :], s[:, 2, :]))
                            link(dve.tensor_tensor(s[:, 3, :], s[:, 3, :],
                                                   gr[:, qb, :, bass.ds(it + (m // 2 + u * CHG), 1)].rearrange("p r a -> p (r a)"), ALU.mult))
                            for r, w in enumerate((NCP, nk, nk)):
                                ins = dve.tensor_scalar(sc[:, u, qb, r, 0:w], sc[:, u, qb, r, 0:w], s[:, 3, r:r + 1], None, ALU.mult)
                            ins.then_inc(p_ready, 1)
                    if on(it, m + 1):
                        u = (m + 1) % 2
                        link = Chain(dve, score_chain, it * 12 + 6 * (m + 1))
                        dve.wait_ge(loaded[u], it * 16 + (16 * ((m + 1) // 2) + 16))
                        wait(dve, turned, it * 6 + 3 * m)
                        for qb in range(2):
                            nk = P * (qb + 1)
                            s = st[:, u, qb]
                            dve.wait_ge(scored, it * 4 + (2 * m + 3 + qb))
                            settle(dve, k)
                            link(dve.tensor_tensor_reduce(sc[:, u, qb, 0, 0:NCP], sps[qb][:, 0:NCP], cmask[:, qb, :], 1.0, MASK / 10,
                                                          ALU.add, ALU.max, s[:, 0, 0:1]))
                            for r, o in ((1, 16), (2, 512)):
                                settle(dve, k)
                                link(dve.tensor_tensor_reduce(sc[:, u, qb, r, 0:nk], sps[qb][:, o:o + nk], tab[:, u, NP - nk:NP], 1.0, -3.0e38,
                                                              ALU.add, ALU.max, s[:, 0, r:r + 1]))
                            dve.tensor_scalar(s[:, 1, :], s[:, 0, :], -1.0, None, ALU.mult).then_inc(max_done, 1)

                steps(dve, step)


PHASES = (block_even_in, block_sample_a, block_prompt_a, block_even_out_odd_in, block_sample_c, block_prompt_c, block_final,)


class Kit:

    def __init__(self, nc):
        self.nc = nc
        self.stacks = [ExitStack()]
        self.sems = []
        self.phase = 0

    def sem(self, name):
        self.sems.append(self.nc.alloc_semaphore(name))
        return self.sems[-1]

    def sb(self, name, shape, dt=F32, lasting=False):
        return self.stacks[0 if lasting else -1].enter_context(self.nc.sbuf_tensor(name, shape, dt))

    def sb_and_lo(self, name, shape):
        with self.nc.sbuf_tensor(name, shape, F32) as full:
            pass
        lo = self.sb(name + "_lo", shape, F32R)
        return full, lo

    def ps(self, name, shape):
        return self.stacks[-1].enter_context(self.nc.psum_tensor(name, shape, F32))

    def scope(self):
        return Scope(self)


class Scope:

    def __init__(self, kit):
        self.kit = kit

    def __enter__(self):
        self.kit.stacks.append(ExitStack())
        self.kit.phase += 1
        self.kit.settled = self.kit.sem(f"settled{self.kit.phase}")

    def __exit__(self, *exc):
        self.kit.stacks.pop().close()
        self.kit.nc.clear_and_free_semaphores(self.kit.sems)
        self.kit.sems = []
        self.kit.nc.all_engine_barrier()


def build(nc, ins, outs):
    def scratch(name, *shape):
        return nc.dram_tensor(name, list(shape), F32, kind="Internal").ap()

    k = Kit(nc)
    k.x_prompt = ins["x_prompt"][0]
    k.norm_even = ins["norm_even"][0]
    k.w_in_even = ins["w_in_even"][0]
    k.conv_w = ins["conv_w"][0]
    k.conv_b = ins["conv_b"][0]
    k.conv_ln_g = ins["conv_ln_g"][0]
    k.conv_ln_b = ins["conv_ln_b"][0]
    k.conv_pw_w = ins["conv_pw_w"][0]
    k.conv_pw_b = ins["conv_pw_b"][0]
    k.w_out_even = ins["w_out_even"][0]
    k.norm_odd = ins["norm_odd"][0]
    k.w_in_odd = ins["w_in_odd"][0]
    k.cmp_w1 = ins["cmp_w1"][0]
    k.cmp_w2 = ins["cmp_w2"][0]
    k.w_out_odd = ins["w_out_odd"][0]
    k.state_b_conv = ins["state_b_conv"][0]
    k.cache_c_kv = ins["cache_c_kv"][0]
    k.cache_c_win = ins["cache_c_win"][0]
    k.cmp_pos = ins["cmp_pos"]
    k.cmp_b1 = ins["cmp_b1"]
    k.final_norm = ins["final_norm"]
    k.rel_bias = ins["rel_bias"]
    k.page_table = ins["page_table"]
    k.c_ident = ins["c_ident"]
    k.c_onehot = ins["c_onehot"]
    k.c_overlap = ins["c_overlap"]
    k.c_hsum = ins["c_hsum"]
    k.c_cmask = ins["c_cmask"]
    k.x_sample = ins["x_sample"].rearrange("b t d -> (b t) d")
    k.cache_a = [ins[f"cache_a_kv{g}"][0] for g in range(NG)]
    k.out_y_p, k.out_y_s = outs[0][0], outs[1].rearrange("b t d -> (b t) d")
    k.out_a_p = [outs[2 + g][0, 0] for g in range(NG)]
    k.out_conv_p, k.out_rows_p, k.out_win_p = outs[5][0, 0], outs[6][0, 0], outs[7][0, 0]
    k.out_a_s = [outs[8 + g][0] for g in range(NG)]
    k.out_conv_s, k.out_rows_s, k.out_win_s = outs[11][0], outs[12][0], outs[13][0]
    k.zt = scratch("zt", EVEN_IN, T)
    k.kv = scratch("kv", T, 2 * QKV)
    k.xt = scratch("xt", D, T)
    k.mt = scratch("mt", D, T)
    k.z2 = scratch("z2", Z2_GP + CW, T)
    k.kv2 = scratch("kv2", T, 6 * CKV)
    k.gates = scratch("gates", NP, 3 * CH)
    k.gates_s = scratch("gates_s", 3 * CH, NQ, NB)
    k.tab_a = scratch("tab_a", NG, NH, FW)
    k.tab_c = scratch("tab_c", CH, FW)
    k.tab_sa = scratch("tab_sa", NQ, NH, SA)
    k.tab_hc = scratch("tab_hc", CH, HC)
    k.tab_hw = scratch("tab_hw", CH, HWC)
    k.toe_a = scratch("toe_a", NG, NH, P, NP)
    k.toe_c = scratch("toe_c", CH, P, NP)
    k.gate = scratch("gate", D, T)
    k.cache_pieces = cache_pieces(k)
    with k.stacks[0]:
        k.ident = k.sb("ident", [P, P])
        k.ones = k.sb("ones", [P, P])
        k.eps = k.sb("eps", [P, 1])
        for phase in PHASES:
            phase(nc, k)


_NAMES = ['x_prompt', 'x_sample', 'cache_a_kv0', 'cache_a_kv1', 'cache_a_kv2', 'state_b_conv', 'cache_c_kv', 'cache_c_win',
          'page_table', 'rel_bias', 'norm_even', 'w_in_even', 'conv_w', 'conv_b', 'conv_ln_g', 'conv_ln_b', 'conv_pw_w',
          'conv_pw_b', 'w_out_even', 'norm_odd', 'w_in_odd', 'cmp_pos', 'cmp_w1', 'cmp_b1', 'cmp_w2', 'w_out_odd', 'final_norm']
_OUTS = [(1, NP, D), (NB, NQ, D),
         (1, 1, 128, 2, 8, 128), (1, 1, NP, 2, 8, 128), (1, 1, NP, 2, 8, 128),
         (1, 1, 30, 1024), (1, 1, NP, 4, 2, 128), (1, 1, NP, 2, 2, 128),
         (1, NB, 128, 2, 8, 128), (1, NB, 512, 2, 8, 128), (1, NB, 2048, 2, 8, 128),
         (1, NB, 30, 1024), (1, NB, NQ, 4, 2, 128), (1, NB, 512, 2, 2, 128)]


def kernel(**inputs):
    import concourse.bacc as _bacc
    from concourse.bass_utils import run_bass_kernel_spmd as _run

    nc = _bacc.Bacc("TRN2", target_bir_lowering=False, num_devices=1)
    arrays, ins = {}, {}
    given = {name: np.ascontiguousarray(inputs[name]) for name in _NAMES}
    given.update(host_constants())
    for name in ("norm_even", "conv_b", "conv_ln_g", "conv_ln_b", "conv_pw_b", "norm_odd", "final_norm"):
        a = given[name]
        given[name] = np.ascontiguousarray(a.reshape(*a.shape[:-1], -1, P).swapaxes(-1, -2))
    given["conv_w"] = np.ascontiguousarray(given["conv_w"].reshape(1, TAPS, -1, P).transpose(0, 3, 2, 1))
    for name in ("cmp_pos", "cmp_b1"):
        a = given[name]
        given[name] = np.ascontiguousarray(np.moveaxis(a.reshape(2, -1, HD), 2, 0))
    for name, a in given.items():
        arrays[f"in_{name}"] = a
        ins[name] = nc.dram_tensor(f"in_{name}", a.shape, mybir.dt.from_np(a.dtype), kind="ExternalInput").ap()
    outs = [nc.dram_tensor(f"out_{i}", shape, F32, kind="ExternalOutput").ap() for i, shape in enumerate(_OUTS)]
    build(nc, ins, outs)
    r = _run(nc, [arrays], core_ids=[0])
    return tuple(r.results[0][f"out_{i}"] for i in range(len(_OUTS)))
```
